# Optimizing a Trainium2 kernel written in Bass

```python
import math
import jax, jax.numpy as jnp
from jax import lax
import numpy as np

D_MODEL = 1024
BATCH = 1
SEQ = 512
DEPTH = 1

N_HEADS_DIFF = 8
HEAD_DIM_DIFF = 64
N_HEADS_DSA = 8
HEAD_DIM_DSA = 128
KV_LATENT = 256
N_HEADS_IDX = 16
HEAD_DIM_IDX = 64
TOPK_MAX = 256
N_BUCKETS = 32
MAX_DISTANCE = 128
N_EXPERTS = 32
TOP_K_EXPERTS = 4
D_EXPERT = 1024
SWIGLU_LIMIT = 7.0
SWIGLU_ALPHA = 1.702
MOE_BLOCK = 128
Q_BLOCK = 128
EPS = 1e-6

W_DIFF_Q = N_HEADS_DIFF * 2 * HEAD_DIM_DIFF
W_DIFF_K = N_HEADS_DIFF * 2 * HEAD_DIM_DIFF
W_DIFF_V = N_HEADS_DIFF * 2 * HEAD_DIM_DIFF
W_DSA_Q = N_HEADS_DSA * HEAD_DIM_DSA
W_IDX_Q = N_HEADS_IDX * HEAD_DIM_IDX
W_DIFF_OUT = N_HEADS_DIFF * 2 * HEAD_DIM_DIFF
W_DSA_OUT = N_HEADS_DSA * HEAD_DIM_DSA
IN_SPLIT_SIZES = (W_DIFF_Q, W_DIFF_K, W_DIFF_V, W_DSA_Q, KV_LATENT, W_IDX_Q, HEAD_DIM_IDX, N_HEADS_IDX, D_MODEL, D_MODEL)
IN_WIDTH = 7 * 1024 + KV_LATENT + HEAD_DIM_IDX + N_HEADS_IDX

kernel_name = "hybrid_diffattn_dsa_gated_moe"

def rmsnorm(x, g):
    xf = x.astype(jnp.float32)
    y = xf * lax.rsqrt(jnp.mean(xf * xf, axis=-1, keepdims=True) + EPS)
    return (y * g.astype(jnp.float32)).astype(x.dtype)

def t5_bucket(dist):
    n = jnp.maximum(dist, 0)
    max_exact = N_BUCKETS // 2
    nf = jnp.maximum(n, 1).astype(jnp.float32)
    large = max_exact + (jnp.log(nf / max_exact) / math.log(MAX_DISTANCE / max_exact)
                         * (N_BUCKETS - max_exact)).astype(jnp.int32)
    large = jnp.minimum(large, N_BUCKETS - 1)
    return jnp.where(n < max_exact, n, large)

def split_cols(p):
    outs, off = [], 0
    for sz in IN_SPLIT_SIZES:
        outs.append(p[..., off:off + sz])
        off += sz
    return outs

def diff_attention(q, k, v, bias_tab, lam, lam_init, subln_g):
    B, S = q.shape[0], q.shape[1]
    H, d = N_HEADS_DIFF, HEAD_DIM_DIFF
    nblk = S // Q_BLOCK
    q = q * (d ** -0.5)
    qb = q.reshape(B, nblk, Q_BLOCK, H, 2, d).swapaxes(0, 1)
    kpos = jnp.arange(S, dtype=jnp.int32)

    def one_block(args):
        qi, i = args
        qpos = i * Q_BLOCK + jnp.arange(Q_BLOCK, dtype=jnp.int32)
        dist = qpos[:, None] - kpos[None, :]
        bias = bias_tab[t5_bucket(dist)].astype(jnp.float32).transpose(2, 0, 1)
        s = jnp.einsum('bqhcd,bkhcd->bhcqk', qi, k).astype(jnp.float32) + bias[None, :, None]
        s = jnp.where((dist >= 0)[None, None, None], s, -jnp.inf)
        p = jax.nn.softmax(s, axis=-1)
        a = p[:, :, 0] - lam * p[:, :, 1]
        return jnp.einsum('bhqk,bkhe->bqhe', a.astype(v.dtype), v)

    o = lax.map(one_block, (qb, jnp.arange(nblk, dtype=jnp.int32)))
    o = o.swapaxes(0, 1).reshape(B, S, H, 2 * d)
    o = rmsnorm(o, subln_g) * (1.0 - lam_init)
    return o.reshape(B, S, H * 2 * d)

def dsa_attention(q, c, q_idx, k_idx, w_idx, bias_tab, w_uk, w_uv):
    B, S = q.shape[0], q.shape[1]
    topk = min(TOPK_MAX, S // 4)
    nblk = S // Q_BLOCK
    blk = lambda a: a.reshape((B, nblk, Q_BLOCK) + a.shape[2:]).swapaxes(0, 1)
    w_idx = w_idx * (N_HEADS_IDX ** -0.5) * (HEAD_DIM_IDX ** -0.5)
    kpos = jnp.arange(S, dtype=jnp.int32)
    scale = HEAD_DIM_DSA ** -0.5

    def one_block(args):
        qi, qii, wi, i = args
        qpos = i * Q_BLOCK + jnp.arange(Q_BLOCK, dtype=jnp.int32)
        causal = kpos[None, :] <= qpos[:, None]
        dots = jnp.einsum('bqhd,bsd->bqhs', qii, k_idx)
        score = jnp.einsum('bqhs,bqh->bqs', jax.nn.relu(dots), wi).astype(jnp.float32)
        score = jnp.where(causal[None], score, -jnp.inf)
        _, idx = lax.top_k(score, topk)
        valid = idx <= qpos[None, :, None]
        sel = jax.vmap(lambda cb, ib: cb[ib])(c, idx)
        bias = bias_tab[t5_bucket(qpos[None, :, None] - idx)].astype(jnp.float32)
        ql = jnp.einsum('bqhd,hcd->bqhc', qi, w_uk)
        s = jnp.einsum('bqhc,bqkc->bqhk', ql, sel).astype(jnp.float32) * scale + bias.transpose(0, 1, 3, 2)
        s = jnp.where(valid[:, :, None, :], s, -jnp.inf)
        p = jax.nn.softmax(s, axis=-1).astype(c.dtype)
        ol = jnp.einsum('bqhk,bqkc->bqhc', p, sel)
        return jnp.einsum('bqhc,hcd->bqhd', ol, w_uv)

    o = lax.map(one_block, (blk(q), blk(q_idx), blk(w_idx), jnp.arange(nblk, dtype=jnp.int32)))
    return o.swapaxes(0, 1).reshape(B, S, N_HEADS_DSA * HEAD_DIM_DSA)

def moe(h, w_router, b_router, w_gu, b_gu, w_down, b_down):
    B, S, D = h.shape
    N = B * S
    E, K = N_EXPERTS, TOP_K_EXPERTS
    xf = h.reshape(N, D)
    logits = (xf @ w_router + b_router).astype(jnp.float32)
    top_vals, top_idx = lax.top_k(logits, K)
    gates = jax.nn.softmax(top_vals, axis=-1)
    A = N * K
    a_exp = top_idx.reshape(A).astype(jnp.int32)
    a_tok = jnp.repeat(jnp.arange(N, dtype=jnp.int32), K)
    a_w = gates.reshape(A)
    order = jnp.argsort(a_exp)
    s_exp, s_tok, s_w = a_exp[order], a_tok[order], a_w[order]
    counts = jnp.bincount(a_exp, length=E).astype(jnp.int32)
    padded = (counts + MOE_BLOCK - 1) // MOE_BLOCK * MOE_BLOCK
    starts = jnp.cumsum(counts) - counts
    pends = jnp.cumsum(padded)
    pstarts = pends - padded
    dest = pstarts[s_exp] + jnp.arange(A, dtype=jnp.int32) - starts[s_exp]
    nblk = -(-(A + E * (MOE_BLOCK - 1)) // MOE_BLOCK)
    P = nblk * MOE_BLOCK
    row_tok = jnp.full((P,), N, jnp.int32).at[dest].set(s_tok)
    row_w = jnp.zeros((P,), jnp.float32).at[dest].set(s_w)
    blk_exp = jnp.minimum(jnp.searchsorted(pends, jnp.arange(nblk, dtype=jnp.int32) * MOE_BLOCK, side='right'), E - 1)
    x_pad = jnp.concatenate([xf, jnp.zeros((1, D), xf.dtype)], axis=0)
    xb = x_pad[row_tok].reshape(nblk, MOE_BLOCK, D)

    def expert_block(args):
        xi, e = args
        gu = xi @ w_gu[e] + b_gu[e]
        gate = jnp.minimum(gu[:, 0::2], SWIGLU_LIMIT)
        up = jnp.clip(gu[:, 1::2], -SWIGLU_LIMIT, SWIGLU_LIMIT)
        glu = gate * jax.nn.sigmoid(gate * SWIGLU_ALPHA)
        return ((up + 1.0) * glu) @ w_down[e] + b_down[e]

    yb = lax.map(expert_block, (xb, blk_exp)).reshape(P, D)
    out = jnp.zeros((N + 1, D), yb.dtype).at[row_tok].add(yb * row_w[:, None].astype(yb.dtype))
    return out[:N].reshape(B, S, D).astype(h.dtype)

def setup_inputs(seed: int = 0) -> dict:
    key = jax.random.key(seed)
    ks = jax.random.split(key, 24)
    nrm = lambda k, shape, s: jax.random.normal(k, shape, jnp.float32) * s
    gain = lambda k, shape: 1.0 + 0.02 * jax.random.normal(k, shape, jnp.float32)
    Lz = DEPTH
    return {
        "x": nrm(ks[0], (BATCH, SEQ, D_MODEL), 1.0),
        "norm_attn_g": gain(ks[1], (Lz, D_MODEL)),
        "w_in": nrm(ks[2], (Lz, D_MODEL, IN_WIDTH), D_MODEL ** -0.5),
        "rel_bias": nrm(ks[3], (N_BUCKETS, N_HEADS_DIFF + N_HEADS_DSA), 0.5),
        "lam_q1": nrm(ks[4], (Lz, HEAD_DIM_DIFF), 0.1),
        "lam_k1": nrm(ks[5], (Lz, HEAD_DIM_DIFF), 0.1),
        "lam_q2": nrm(ks[6], (Lz, HEAD_DIM_DIFF), 0.1),
        "lam_k2": nrm(ks[7], (Lz, HEAD_DIM_DIFF), 0.1),
        "diff_subln_g": gain(ks[8], (Lz, 2 * HEAD_DIM_DIFF)),
        "kv_norm_g": gain(ks[9], (Lz, KV_LATENT)),
        "w_uk": nrm(ks[10], (Lz, N_HEADS_DSA, KV_LATENT, HEAD_DIM_DSA), KV_LATENT ** -0.5),
        "w_uv": nrm(ks[11], (Lz, N_HEADS_DSA, KV_LATENT, HEAD_DIM_DSA), KV_LATENT ** -0.5),
        "w_branch_diff": nrm(ks[12], (Lz, W_DIFF_OUT, D_MODEL), W_DIFF_OUT ** -0.5),
        "w_branch_dsa": nrm(ks[13], (Lz, W_DSA_OUT, D_MODEL), W_DSA_OUT ** -0.5),
        "w_out": nrm(ks[14], (Lz, D_MODEL, D_MODEL), D_MODEL ** -0.5),
        "norm_ffn_g": gain(ks[15], (Lz, D_MODEL)),
        "w_router": nrm(ks[16], (Lz, D_MODEL, N_EXPERTS), D_MODEL ** -0.5),
        "b_router": nrm(ks[17], (Lz, N_EXPERTS), 0.01),
        "w_gate_up": nrm(ks[18], (Lz, N_EXPERTS, D_MODEL, 2 * D_EXPERT), D_MODEL ** -0.5),
        "b_gate_up": nrm(ks[19], (Lz, N_EXPERTS, 2 * D_EXPERT), 0.01),
        "w_down": nrm(ks[20], (Lz, N_EXPERTS, D_EXPERT, D_MODEL), D_EXPERT ** -0.5),
        "b_down": nrm(ks[21], (Lz, N_EXPERTS, D_MODEL), 0.01),
        "norm_final_g": gain(ks[22], (D_MODEL,)),
    }

def reference(x, norm_attn_g, w_in, rel_bias, lam_q1, lam_k1, lam_q2, lam_k2, diff_subln_g,
              kv_norm_g, w_uk, w_uv, w_branch_diff, w_branch_dsa, w_out, norm_ffn_g,
              w_router, b_router, w_gate_up, b_gate_up, w_down, b_down, norm_final_g):
    B, S, D = x.shape
    h = x
    bias_diff = rel_bias[:, :N_HEADS_DIFF]
    bias_dsa = rel_bias[:, N_HEADS_DIFF:]
    for l in range(DEPTH):
        xn = rmsnorm(h, norm_attn_g[l])
        proj = xn @ w_in[l]
        dq, dk, dv, sq, ckv, iq, ik, iw, ga, gb = split_cols(proj)
        lam_init = 0.8 - 0.6 * math.exp(-0.3 * l)
        lam = (jnp.exp(jnp.sum(lam_q1[l].astype(jnp.float32) * lam_k1[l].astype(jnp.float32)))
               - jnp.exp(jnp.sum(lam_q2[l].astype(jnp.float32) * lam_k2[l].astype(jnp.float32)))
               + lam_init)
        y_diff = diff_attention(
            dq.reshape(B, S, N_HEADS_DIFF, 2, HEAD_DIM_DIFF),
            dk.reshape(B, S, N_HEADS_DIFF, 2, HEAD_DIM_DIFF),
            dv.reshape(B, S, N_HEADS_DIFF, 2 * HEAD_DIM_DIFF),
            bias_diff, lam, lam_init, diff_subln_g[l])
        y_dsa = dsa_attention(
            sq.reshape(B, S, N_HEADS_DSA, HEAD_DIM_DSA),
            rmsnorm(ckv, kv_norm_g[l]),
            iq.reshape(B, S, N_HEADS_IDX, HEAD_DIM_IDX),
            ik, iw, bias_dsa, w_uk[l], w_uv[l])
        merged = (jax.nn.sigmoid(ga) * (y_diff @ w_branch_diff[l])
                  + jax.nn.sigmoid(gb) * (y_dsa @ w_branch_dsa[l]))
        h = h + merged @ w_out[l]
        hn = rmsnorm(h, norm_ffn_g[l])
        h = h + moe(hn, w_router[l], b_router[l], w_gate_up[l], b_gate_up[l], w_down[l], b_down[l])
    return rmsnorm(h, norm_final_g)


_drawn_inputs = setup_inputs


def setup_inputs(seed=0):
    import zlib

    import numpy as np

    out = dict(_drawn_inputs(seed))
    spreads = {}
    factors = {'kv_norm_g': 4.597,
     'b_gate_up': 8.0,
     'b_down': 21.956,
     'norm_final_g': 7.99,
     'lam_k1': 4.043,
     'lam_q2': 3.924,
     'diff_subln_g': 5.627,
     'norm_ffn_g': 2.676,
     'b_router': 4.093}
    for name, (base, spread) in spreads.items():
        noise = np.random.default_rng([zlib.crc32(name.encode()), seed]).standard_normal(out[name].shape)
        drawn = base * np.exp(spread * noise) if base else spread * noise
        out[name] = __import__('jax').numpy.asarray(drawn.astype(out[name].dtype))
    for name, factor in factors.items():
        out[name] = (out[name] * factor).astype(out[name].dtype)
    return out
```

```python
from contextlib import ExitStack

import numpy as np

import concourse.bass as bass
from concourse import mybir
from concourse.alu_op_type import AluOpType as ALU

ACT = mybir.ActivationFunctionType
F32 = mybir.dt.float32
BF16 = mybir.dt.bfloat16
I32 = mybir.dt.int32
U32 = mybir.dt.uint32
X = mybir.AxisListType.X

P = 128
D = 1024
S = 512
NT = S // P
KD = D // P
NH = 8
LAT = 256
KL = LAT // P
NI, DI = 16, 64
TOPK = min(256, S // 4)
NB = 32
MAXD = 128
NE, NK = 32, 4
F = 1024
EPS = 1e-6
LIMIT, ALPHA = 7.0, 1.702
OUT_SCALE = 1.0 - (0.8 - 0.6)
LAM_INIT = 0.8 - 0.6
MASK = -1e30
TAKEN = -3e38
NX = S * NK // P - 1
NBLK = NE + NX + 1
RLEN = S + P
IN_COLS = dict(dq=0, dk=1024, dv=2048, sq=3072, ckv=4096, iq=4352, ik=5376, iw=5440, ga=5456, gb=6480)

C_ID, C_TRI, C_ONE, C_SU, C_SUI = 0, 128, 256, 384, 416
C_E, C_EB, C_XB, C_TOK, C_J, C_P32 = 448, 480, 512, 544, 548, 564
C_CAUS = 692
C_LEN = 820


def constants():
    c = np.zeros((P, C_LEN), np.float32)
    p = np.arange(P)
    c[:, C_ID:C_ID + P] = np.eye(P)
    c[:, C_TRI:C_TRI + P] = p[:, None] < p[None, :]
    c[:, C_ONE:C_ONE + P] = 1.0
    e = np.arange(NE)
    c[:NE, C_SU:C_SU + NE] = e[:, None] < e[None, :]
    c[:NE, C_SUI:C_SUI + NE] = e[:, None] <= e[None, :]
    c[:, C_E:C_E + NE] = e
    c[:, C_EB:C_EB + NE] = P * e
    c[:, C_XB:C_XB + NE] = P * (NE - 1) - P * e
    c[:, C_TOK:C_TOK + NT] = p[:, None] + P * np.arange(NT)[None, :]
    c[:, C_J:C_J + 16] = np.arange(16)
    c[:, C_P32:C_P32 + P] = (p % NE)[:, None]
    c[:, C_CAUS:C_CAUS + P] = np.where(p[None, :] <= p[:, None], 0.0, MASK)
    return c


def bucket_onehot():
    dist = S - 1 - np.arange(RLEN)
    n = np.maximum(dist, 0)
    half = NB // 2
    nf = np.maximum(n, 1).astype(np.float32)
    large = half + (np.log(nf / np.float32(half)) / np.float32(np.log(MAXD / half)) * np.float32(NB - half)).astype(np.int32)
    b = np.where(n < half, n, np.minimum(large, NB - 1))
    b = np.where(dist < 0, NB, b)
    return (np.arange(NB + 1)[:, None] == b[None, :]).astype(np.float32)


def build(nc, a, out):
    ctx = ExitStack()
    with ctx:
        def sb(name, cols, dt=F32, parts=P):
            return ctx.enter_context(nc.sbuf_tensor(name, [parts, cols], dt))

        def sem(name):
            return ctx.enter_context(nc.semaphore(name))

        def dram(name, shape, dt=F32):
            return nc.dram_tensor(name, shape, dt).ap()

        KB = 256
        arena = sb("arena", 176 * KB)

        def area(at_kb, kb):
            return arena[:, at_kb * KB:(at_kb + kb) * KB]

        def tiles(ap, n):
            return ap.rearrange("p (a b) -> p a b", a=n)

        xnT = tiles(area(0, 16), KD)
        dqT = tiles(area(16, 16), NH)
        dkT = tiles(area(32, 16), NH)
        dv = tiles(area(48, 16), NT)
        iqT = tiles(area(64, 16), NH)
        khT = tiles(area(64, 16), NH)
        xbuf = tiles(area(80, 16), NT)
        vh = tiles(area(80, 16), NT)
        ydT = tiles(area(96, 16), NH)
        ysT = tiles(area(16, 16), NH)
        sqT = tiles(area(32, 16), NH)
        mergedT = tiles(area(48, 16), KD)
        hbuf = tiles(area(96, 16), NT)
        bsplit = area(96, 12)
        NW = 3
        wring = [area(112 + 16 * i, 16) for i in range(NW)]
        strips = tiles(area(160, 16), NH)
        sgate = tiles(area(160, 16), 2 * NT)
        hn = tiles(area(160, 8), 2)
        hnT = tiles(area(168, 8), 2)
        NSLOT = 12
        eslot = [area(8 * i, 8) for i in range(NSLOT)]
        xg = area(112, 4)
        xgT = tiles(area(116, 4), KD)
        gate_h = [area(120 + 8 * i, 2) for i in range(2)]
        sg_h = [area(122 + 8 * i, 2) for i in range(2)]
        up_h = [area(124 + 8 * i, 2) for i in range(2)]
        act_h = [area(126 + 8 * i, 2) for i in range(2)]
        hT = tiles(area(136, 4), KD)
        ybuf = area(140, 4)
        NYG = 4
        yg = [area(4 * i, 4) for i in range(NYG)]
        outb = [area(16 + 4 * i, 4) for i in range(NT)]

        work = sb("work", 8 * KB)
        srow = [[work[:, (2 * i + c) * 512:(2 * i + c + 1) * 512] for c in range(2)] for i in range(2)]
        cbuf = tiles(work[:, 0:4 * KB], NT)
        topacc = [None] + [work[:, 0:256], work[:, 256:640], work[:, 640:1152]]
        gffn = work[:, 0:D]
        gfin = work[:, D:2 * D]
        ptb = sb("ptb", 4 * KB)
        PT = [ptb[:, i * 512:(i + 1) * 512] for i in range(2)]
        merge_tmp = [ptb[:, i * 512:(i + 1) * 512] for i in range(2)]
        cT = tiles(sb("cT", 4 * KB)[:, :], KL)
        topmask = [None] + [sb(f"topmask{t}", (t + 1) * P, BF16) for t in range(1, NT)]
        bparts = sb("bparts", 3 * D, BF16, 96)
        con = sb("con", C_LEN)
        ident = con[:, C_ID:C_ID + P]
        tri = con[:, C_TRI:C_TRI + P]
        ones = con[:, C_ONE:C_ONE + P]
        identb = sb("identb", P, BF16)
        zeros = area(56, 8)
        ikT = area(52, 2)
        iw = tiles(area(54, 1)[:, 0:NT * NI], NT)
        gcols = sb("gcols", KD + KL + 1)
        lamv = area(67, 1)
        lamj = sb("lamj", DI)
        lam = sb("lam", 4)
        tabx = sb("tabx", 2 * NH, F32, NB + 1)
        oh33 = area(64, 3)[0:NB + 1, 0:RLEN]
        rvec = area(108, 4)[0:2 * NH, 0:RLEN]
        stat = sb("stat", 64)
        v8 = sb("v8", 8)
        row_max = [sb(f"rowmax{i}", 2) for i in range(2)]
        row_sum = [sb(f"rowsum{i}", 2) for i in range(3)]
        ratio = [sb(f"ratio{i}", 4) for i in range(3)]
        orow = [cT[:, i, :] for i in range(2)]
        ojunk = sb("ojunk", P)
        late = [144 * KB]

        def after(cols, parts=P):
            late[0] += cols
            return arena[0:parts, late[0] - cols:late[0]]

        logit, chosen = tiles(after(NT * NE), NT), tiles(after(NT * NE), NT)
        top_v, top_f = tiles(after(NT * 8), NT), tiles(after(NT * 8), NT)
        pick = after(NT * NK * NE).rearrange("p (t k e) -> p t k e", t=NT, k=NK)
        ptmp = after(NK * NE).rearrange("p (k e) -> p k e", k=NK)
        extra, extra2, before = after(P, NE), after(P, NE), after(16, NE)
        xbase, over, slot_e, vneg = after(NE), after(NE), after(NE), after(NT)
        slot_f = tiles(after(NT * NK), NT)
        brt = after(NE)
        wr = tiles(after(KD * NE), KD)
        top_i = tiles(sb("top_i", NT * 8, U32)[:, :], NT)
        gate = tiles(sb("gate", NT * NK)[:, :], NT)
        gsum = sb("gsum", NT)
        slot_i = tiles(sb("slot_i", NT * NK, I32)[:, :], NT)
        tok_i = sb("tok_i", NT, I32)
        evals = sb("evals", NE + 16)
        evals_i = sb("evals_i", NE + 16, I32)
        nextra_i = sb("nextra_i", 2, I32)
        zero_i = sb("zero_i", NBLK, I32)
        ids = sb("ids", 2, I32)
        carrier = sb("carrier", 2, F32, 1)
        ohe = sb("ohe", P, BF16, 96)

        psum = ctx.enter_context(nc.psum_tensor("psum", [P, 8 * 512], F32))
        bank = [psum[:, 512 * i:512 * (i + 1)] for i in range(8)]

        rv_d = dram("rv_d", (2 * NH, RLEN))
        skew_d = dram("skew_d", (2 * NH, P, RLEN))
        hn_d = dram("hn_d", (S, D))
        rowtok_d = dram("rowtok_d", (NBLK * P, 1), I32)
        y_d = dram("y_d", ((NE + NX) * P, D))
        rest = y_d[NE * P:, :].rearrange("(p r) d -> p (r d)", p=P)

        full = [sem(f"bank{i}_full") for i in range(8)]
        free = [sem(f"bank{i}_free") for i in range(8)]
        x_in, x_in2, const_in, small_in, wr_in, gbc_in = (sem(n) for n in ("x_in", "x_in2", "const_in", "small_in", "wr_in", "gbc_in"))
        mask_row, bsplit_in, bparts_ready = sem("mask_row"), sem("bsplit_in"), sem("bparts_ready")
        wring_in = [sem(f"wring{i}_in") for i in range(NW)]
        act_step, dve_step, pool_step = sem("act_step"), sem("dve_step"), sem("pool_step")
        x_sq, x_norm, c_sq, c_norm = sem("x_sq"), sem("x_norm"), sem("c_sq"), sem("c_norm")
        identb_ready, tok_ready = sem("identb_ready"), sem("tok_ready")
        y_zero = sem("y_zero")
        skew_out, carried = sem("skew_out"), sem("carried")
        rvec_out, strip_in, strip2_in = sem("rvec_out"), sem("strip_in"), sem("strip2_in")
        relu_used, mask_ready = sem("relu_used"), sem("mask_ready")
        lam_dot, lam_exp = sem("lam_dot"), sem("lam_exp")
        score_ready, exp_ready, a_ready, y_ready = sem("score_ready"), sem("exp_ready"), sem("a_ready"), sem("y_ready")
        sscore_ready, sexp_ready, p_ready = sem("sscore_ready"), sem("sexp_ready"), sem("p_ready")
        merge_ready, h_sq, hn_ready = sem("merge_ready"), sem("h_sq"), sem("hn_ready")
        hn_out = [sem(f"hn_out{i}") for i in range(2)]
        top_ready, chosen_ready, gate_exp = (
            sem(n) for n in ("top_ready", "chosen_ready", "gate_exp"))
        slots_ready, evals_ready, zero_out, scat_out = sem("slots_ready"), sem("evals_ready"), sem("zero_out"), sem("scat_out")
        e_in = [sem(f"eslot{i}_in") for i in range(NSLOT)]
        e_used, ids_in, xg_in, ohe_ready = sem("e_used"), sem("ids_in"), sem("xg_in"), sem("ohe_ready")
        g_ready, sg_ready, glu_ready, act_ready = sem("g_ready"), sem("sg_ready"), sem("glu_ready"), sem("act_ready")
        y_out = sem("y_out")
        yg_in = [sem(f"yg{i}_in") for i in range(NYG)]
        yg_used, o_sq, o_ready, out_done = sem("yg_used"), sem("o_sq"), sem("o_ready"), sem("out_done")

        CH = ["ckv", "iq0", "iq1", "ikw", "dq0", "dq1", "dk0", "dk1", "dv0", "dv1", "ukv", "sq0", "sq1"]
        for j in range(2):
            CH += [f"ga{j}", f"bd{j}", f"gb{j}", f"bs{j}"]
        CH += ["wo0", "wo1"]
        w_in_v = a["w_in"][0].rearrange("(k p) n -> p k n", p=P)

        def chunk_view(name, cols=512):
            return wring[CH.index(name) % NW][:, 0:KD * cols].rearrange("p (k n) -> p k n", k=KD)

        uses, count = {}, [0] * 8

        def plan(key, b):
            uses[key] = (b, count[b])
            count[b] += 1

        n_group = [0]
        groups = {}

        def plan_groups(keys):
            for k in keys:
                groups[k] = n_group[0]
                plan(k, n_group[0] % 2)
                n_group[0] += 1

        plan("rv0", 6)
        plan("rv1", 7)
        for k in range(KD):
            plan(("xT", k), 2 + k % 2)
        G_CKV = [("ckv", t) for t in range(NT)]
        G_IQ = [("iq", j) for j in range(NH)]
        G_IK = [("ik", 0)]
        G_IW = [("iw", t) for t in range(NT)]
        G_DQ = [("dq", j) for j in range(NH)]
        G_DK = [("dk", j) for j in range(NH)]
        G_DV = [("dv", h, t) for h in range(2) for t in range(NT)]
        G_UK = [("uk", h) for h in range(NH)]
        G_UV = [("uv", h, t) for h in range(2) for t in range(NT)]
        G_SQ = [("sq", j) for j in range(NH)]
        plan_groups(G_CKV + G_IQ + G_IK + G_IW)
        for k in range(KL):
            plan(("cT", k), 6 + k)
        INDEX = [(t, h) for t in range(1, NT) for h in range(NI)]
        for m, key in enumerate(INDEX):
            plan(("ix",) + key, 2 + m % 2)
        plan_groups(G_DQ + G_DK + G_DV + G_UK + G_UV)
        UNITS = [(h, t) for h in range(NH) for t in range(NT)]
        NU = len(UNITS)
        for u in range(NU + 2):
            if u < NU:
                for c in range(2):
                    plan(("s", u, c), 2 + 2 * (u % 2) + c)
            if 1 <= u <= NU:
                plan(("pt", u - 1), 6)
                plan(("o", u - 1), (u - 1) % 2)
            if u >= 2 and UNITS[u - 2][1] == NT - 1:
                plan(("yt", UNITS[u - 2][0]), 7)
        plan_groups(G_SQ)
        for u in range(NU + 1):
            if u < NU:
                plan(("ss", u), 2 + u % 2)
            if u >= 1:
                plan(("spt", u - 1), 6 + (u - 1) % 2)
                plan(("so", u - 1), (u - 1) % 2 + 4)
        G_MERGE = [(n, j, i) for j in range(2) for n in ("ga", "bd", "gb", "bs") for i in range(NT)]
        plan_groups(G_MERGE)
        G_WO = [("wo", j, t) for j in range(2) for t in range(NT)]
        plan_groups(G_WO)
        for t in range(NT):
            plan(("hT", t, 0), 2)
            plan(("hT", t, 1), 3)
            plan(("lg", t), 4)
        for t in range(NT):
            plan(("rank", t), 5 + t % 2)
        plan("cntT", 7)
        plan("xb", 4)
        plan("xeT", 7)
        plan("xe", 4)
        base_use = list(count)
        LAST = {"ckv": G_CKV[-1], "iq0": G_IQ[3], "iq1": G_IQ[7], "ikw": G_IW[-1], "ukv": G_UV[-1]}
        for j in range(2):
            LAST.update({f"dq{j}": G_DQ[4 * j + 3], f"dk{j}": G_DK[4 * j + 3], f"sq{j}": G_SQ[4 * j + 3],
                         f"dv{j}": G_DV[4 * j + 3], f"wo{j}": ("wo", j, NT - 1)})
            LAST.update({f"{n}{j}": (n, j, NT - 1) for n in ("ga", "bd", "gb", "bs")})

        def filled(eng, key):
            b, n = uses[key]
            eng.wait_ge(full[b], n + 1)
            return bank[b]

        def taken(eng, key):
            b, n = uses[key]
            eng.wait_ge(free[b], n + 1)

        def free_of(key):
            return free[uses[key][0]]


        block = ctx.enter_context(nc.Block())

        @block.sync
        def _(sp):
            x_v = a["x"][0].rearrange("(t p) d -> p t d", p=P)
            for t in range(NT):
                sp.dma_start(xbuf[:, t, :], x_v[:, t, :]).then_inc(x_in, 16)
            for n, name in enumerate(CH):
                if n >= NW:
                    filled(sp, LAST[CH[n - NW]])
                done = wring_in[n % NW]
                if name == "ukv":
                    slot = wring[n % NW].rearrange("p (u k h d) -> p u k h d", u=2, k=KL, h=NH)
                    for u, w in enumerate(("w_uk", "w_uv")):
                        for k in range(KL):
                            sp.dma_start(slot[:, u, k], a[w][0].rearrange("h (k p) d -> k p h d", p=P)[k]).then_inc(done, 16)
                elif name == "ikw":
                    v = chunk_view("ikw", 2 * DI + NI)
                    c0 = IN_COLS["ik"]
                    sp.dma_start(v[:, :, 0:DI], w_in_v[:, :, c0:c0 + DI]).then_inc(done, 16)
                    sp.dma_start(v[:, :, DI:2 * DI + NI], w_in_v[:, :, c0:c0 + DI + NI]).then_inc(done, 16)
                else:
                    cols = LAT if name == "ckv" else 512
                    j = 0 if name == "ckv" else int(name[-1])
                    kind = name if name == "ckv" else name[:-1]
                    if kind in IN_COLS:
                        c0 = IN_COLS[kind] + 512 * j
                        src = w_in_v[:, :, c0:c0 + cols]
                    else:
                        w = {"bd": "w_branch_diff", "bs": "w_branch_dsa", "wo": "w_out"}[kind]
                        src = a[w][0].rearrange("(k p) n -> p k n", p=P)[:, :, 512 * j:512 * j + 512]
                    sp.dma_start(chunk_view(name, cols), src).then_inc(done, 16)
                if name == "wo0":
                    filled(sp, LAST["bd1"])
                    sp.dma_start(hbuf, x_v).then_inc(x_in2, 16)

            gu_v = a["w_gate_up"][0].rearrange("e (c k p) n -> e c p k n", p=P, k=2)
            dn_v = a["w_down"][0].rearrange("e (c k p) n -> e c p k n", p=P, k=2)

            def load_expert(e, i, first=False):
                for s in range(NSLOT):
                    if not first:
                        sp.wait_ge(e_used, i * NSLOT + (s + 1 - NSLOT))
                    src = gu_v[e, s % 4][:, :, (s // 4) * D:(s // 4 + 1) * D] if s < 8 else dn_v[e, s - 8]
                    sp.dma_start(eslot[s].rearrange("p (k n) -> p k n", k=2), src).then_inc(e_in[s], 16)

            filled(sp, LAST["wo1"])
            taken(sp, LAST["wo1"])
            load_expert(0, 0, first=True)
            with sp.Fori(1, NE) as i:
                load_expert(i, i)
            sp.wait_ge(evals_ready, 2)
            n_extra = sp.value_load(nextra_i[0:1, 0:1], min_val=0, max_val=NX)
            with sp.If(n_extra > 0):
                with sp.Fori(0, n_extra) as j:
                    e = sp.value_load(evals_i[0:1, bass.ds(j + NE, 1)], min_val=0, max_val=NE - 1)
                    load_expert(e, j + NE)
            for t in range(NT):
                sp.wait_ge(o_ready, t + 1)
                sp.dma_start(out[0, t * P:(t + 1) * P, :], outb[t]).then_inc(out_done, 16)
            sp.wait_ge(out_done, 16 * NT)

        @block.gpsimd
        def _(pool):
            pool.memset(zero_i[:, :], 0).then_inc(pool_step, 1)
            pool.dma_start(tabx[0:NB, :], a["rel_bias"]).then_inc(small_in, 16)
            pool.dma_start(oh33[:, :], a["oh33"]).then_inc(small_in, 16)
            for v, c0, n in (("norm_attn_g", 0, KD), ("kv_norm_g", KD, KL), ("diff_subln_g", KD + KL, 1)):
                with nc.allow_non_contiguous_dma("gains, one per partition"):
                    pool.dma_start(gcols[:, c0:c0 + n], a[v][0].rearrange("(k p) -> p k", p=P)).then_inc(small_in, 16)
            for i, v in enumerate(("lam_q1", "lam_k1", "lam_q2", "lam_k2")):
                pool.dma_start(lamv[:, i * DI:(i + 1) * DI], a[v].broadcast_to([P, DI])).then_inc(small_in, 16)
            for r in range(3):
                pool.dma_start(bsplit[NE * r:NE * (r + 1), 0:2 * D], a["b_gate_up"][0]).then_inc(bsplit_in, 16)
                pool.dma_start(bsplit[NE * r:NE * (r + 1), 2 * D:3 * D], a["b_down"][0]).then_inc(bsplit_in, 16)
            pool.wait_ge(pool_step, 1)
            pool.dma_start(rowtok_d.rearrange("(p b) o -> p (b o)", p=P), zero_i[:, :]).then_inc(zero_out, 16)
            pool.wait_ge(const_in, 16)
            pool.tensor_copy(tok_i[:, :], con[:, C_TOK:C_TOK + NT]).then_inc(tok_ready, 1)

            pool.wait_ge(bsplit_in, 16 * 6)
            n = 1
            pool.tensor_copy(bparts[:, :], bsplit[0:96, :]).then_inc(pool_step, 1)
            for r in (1, 2):
                rows = slice(NE * r, NE * (r + 1))
                for q in range(r):
                    n += 1
                    pool.wait_ge(pool_step, n)
                    pool.tensor_tensor(bsplit[rows, :], bsplit[rows, :], bparts[rows, :], ALU.subtract).then_inc(pool_step, 1)
                    n += 1
                    pool.wait_ge(pool_step, n)
                    pool.tensor_copy(bparts[rows, :], bsplit[rows, :]).then_inc(bparts_ready if (r, q) == (2, 1) else pool_step, 1)

            pool.wait_ge(mask_row, 3)
            taken(pool, "rv0")
            taken(pool, "rv1")
            pool.dma_start(rv_d, rvec[:, :]).then_inc(rvec_out, 16)
            pool.wait_ge(rvec_out, 16)

            pool.dma_start(skew_d, rv_d.unsqueeze(1).broadcast_to([2 * NH, P, RLEN])).then_inc(skew_out, 16)
            pool.wait_ge(skew_out, 16)

            def load_strips(h0, done):
                src = bass.AP(tensor=skew_d.tensor, offset=h0 * P * RLEN + P - 1, ap=[[RLEN - 1, P], [P * RLEN, NH], [1, S]])
                pool.dma_start(strips, src).then_inc(done, 16)

            load_strips(0, strip_in)
            for r in range(2, NX, 2):
                n = min(2, NX - r) * D
                pool.dma_start(rest[:, r * D:r * D + n], zeros[:, 0:n]).then_inc(y_zero, 16)
            pool.wait_ge(score_ready, 2 * NU)
            load_strips(NH, strip2_in)
            taken(pool, ("so", NU - 1))
            pool.dma_start(gffn, a["norm_ffn_g"].broadcast_to([P, D])).then_inc(gbc_in, 16)
            pool.dma_start(gfin, a["norm_final_g"].rearrange("(o d) -> o d", o=1).broadcast_to([P, D])).then_inc(gbc_in, 16)
            filled(pool, LAST["bs1"])
            pool.dma_start(wr, a["w_router"][0].rearrange("(k p) e -> p k e", p=P)).then_inc(wr_in, 16)
            pool.dma_start(brt[:, :], a["b_router"].broadcast_to([P, NE])).then_inc(wr_in, 16)

            for t in range(NT):
                pool.wait_ge(hn_ready, t + 1)
                pool.dma_start(hn_d[t * P:(t + 1) * P, :], hn[:, t % 2, :]).then_inc(hn_out[t % 2], 16)
            for r in range(2):
                pool.wait_ge(hn_out[r], 16 * NT // 2)
            pool.wait_ge(zero_out, 16)
            pool.wait_ge(tok_ready, 1)
            for t in range(NT):
                pool.wait_ge(slots_ready, t + 1)
                for k in range(NK):
                    pool.indirect_dma_start(rowtok_d, bass.IndirectOffsetOnAxis(ap=slot_i[:, t, k:k + 1], axis=0),
                                            tok_i[:, t:t + 1], None).then_inc(scat_out, 16)
            pool.wait_ge(scat_out, 16 * NT * NK)

            def settle():
                pool.tensor_tensor(carrier[:, 1:2], carrier[:, 0:1], carrier[:, 0:1], ALU.add).then_inc(carried, 1)

            def gather_block(i, first=False):
                if not first:
                    pool.wait_ge(xg_in, i * 16)
                pool.dma_start(ids[:, 0:1], rowtok_d[bass.ds(i * P, P), :]).then_inc(ids_in, 16)
                pool.wait_ge(ids_in, i * 16 + 16)
                if not first:
                    pool.wait_ge(carried, i)
                    pool.wait_ge(full[7], i * 2 + base_use[7])
                settle()
                pool.indirect_dma_start(xg, None, hn_d, bass.IndirectOffsetOnAxis(ap=ids[:, 0:1], axis=0)).then_inc(xg_in, 16)

            gather_block(0, first=True)
            with pool.Fori(1, NE + 1) as i:
                gather_block(i)
            pool.wait_ge(evals_ready, 2)
            n_extra = pool.value_load(nextra_i[0:1, 0:1], min_val=0, max_val=NX)
            with pool.If(n_extra > 0):
                with pool.Fori(0, n_extra) as j:
                    gather_block(j + (NE + 1))
            pool.wait_ge(xg_in, n_extra * 16 + 16 * (NE + 1))

            pool.wait_ge(carried, n_extra + NE + 1)
            pool.wait_ge(y_out, n_extra * 16 + 16 * (NE + 1))
            settle()
            for m in range(NT * NK):
                t, k = m // NK, m % NK
                if m >= NYG:
                    pool.wait_ge(yg_used, m - NYG + 1)
                pool.indirect_dma_start(yg[m % NYG], None, y_d,
                                        bass.IndirectOffsetOnAxis(ap=slot_i[:, t, k:k + 1], axis=0)).then_inc(yg_in[m % NYG], 16)

        @block.tensor
        def _(pe):
            def empty(key):
                b, n = uses[key]
                if n:
                    pe.wait_ge(free[b], n)
                return bank[b]

            def full_of(key):
                return full[uses[key][0]]

            def chunk_in(name):
                n = CH.index(name)
                pe.wait_ge(wring_in[n % NW], sum(16 * {"ukv": 4, "ikw": 2}.get(CH[m], 1) for m in range(n % NW, n + 1, NW)))

            def transposed(keys, chunk, src):
                chunk_in(chunk)
                w = chunk_view(chunk)
                for i, key in enumerate(keys):
                    o = empty(key)
                    for k in range(KD):
                        ins = pe.matmul(o[:, :], w[:, k, i * P:(i + 1) * P], src[:, k, :], start=(k == 0), stop=(k == KD - 1))
                    ins.then_inc(full_of(key), 1)

            def by_token(keys, chunk, src, cols=512, c0=0, width=512):
                chunk_in(chunk)
                w = chunk_view(chunk, width)
                for t, key in enumerate(keys):
                    o = empty(key)
                    for k in range(KD):
                        ins = pe.matmul(o[:, 0:cols], src[:, k, t * P:(t + 1) * P], w[:, k, c0:c0 + cols], start=(k == 0), stop=(k == KD - 1))
                    ins.then_inc(full_of(key), 1)

            pe.wait_ge(small_in, 16 * 9)
            pe.wait_ge(mask_row, 1)
            pe.matmul(empty("rv0")[0:2 * NH, :], tabx[:, :], oh33[:, 0:512], start=True, stop=True).then_inc(full_of("rv0"), 1)
            pe.matmul(empty("rv1")[0:2 * NH, 0:RLEN - 512], tabx[:, :], oh33[:, 512:RLEN], start=True, stop=True).then_inc(full_of("rv1"), 1)

            pe.wait_ge(const_in, 16)
            pe.wait_ge(x_norm, NT)
            for k in range(KD):
                o = empty(("xT", k))
                for t in range(NT):
                    ins = pe.transpose(o[:, t * P:(t + 1) * P], xbuf[:, t, k * P:(k + 1) * P], ident)
                ins.then_inc(full_of(("xT", k)), 1)

            for k in range(KD - 2, KD):
                taken(pe, ("xT", k))
            by_token(G_CKV, "ckv", xnT, cols=LAT, width=LAT)
            transposed(G_IQ[0:4], "iq0", xnT)
            transposed(G_IQ[4:8], "iq1", xnT)
            chunk_in("ikw")
            w = chunk_view("ikw", 2 * DI + NI)
            o = empty(G_IK[0])
            for k in range(KD):
                ins = pe.matmul(o[:, :], w[:, k, 0:2 * DI], xnT[:, k, :], start=(k == 0), stop=(k == KD - 1))
            ins.then_inc(full_of(G_IK[0]), 1)
            by_token(G_IW, "ikw", xnT, cols=NI, c0=2 * DI, width=2 * DI + NI)

            pe.wait_ge(c_norm, NT)
            for k in range(KL):
                o = empty(("cT", k))
                for t in range(NT):
                    ins = pe.transpose(o[:, t * P:(t + 1) * P], cbuf[:, t, k * P:(k + 1) * P], ident)
                ins.then_inc(full_of(("cT", k)), 1)

            taken(pe, G_IW[-1])
            taken(pe, G_IW[-2])
            for t, h in INDEX:
                o = empty(("ix", t, h))
                half = slice((h % 2) * DI, (h % 2 + 1) * DI)
                n = (t + 1) * P
                pe.matmul(o[:, 0:n], iqT[half, h // 2, t * P:(t + 1) * P], ikT[half, 0:n],
                          start=True, stop=True).then_inc(full_of(("ix", t, h)), 1)

            for g, c in ((G_DQ, "dq"), (G_DK, "dk")):
                for j in range(2):
                    transposed(g[4 * j:4 * j + 4], f"{c}{j}", xnT)
            for j in range(2):
                by_token(G_DV[NT * j:NT * (j + 1)], f"dv{j}", xnT)
            chunk_in("ukv")
            ukv = wring[CH.index("ukv") % NW].rearrange("p (u k n) -> p u k n", u=2, k=KL)
            for k in range(KL):
                taken(pe, ("cT", k))
            for key in G_UK:
                o = empty(key)
                for k in range(KL):
                    ins = pe.matmul(o[:, :], ukv[:, 0, k, key[1] * P:(key[1] + 1) * P], cT[:, k, :], start=(k == 0), stop=(k == KL - 1))
                ins.then_inc(full_of(key), 1)
            for key in G_UV:
                _, j, t = key
                o = empty(key)
                for k in range(KL):
                    ins = pe.matmul(o[:, :], cT[:, k, t * P:(t + 1) * P], ukv[:, 1, k, j * 512:(j + 1) * 512], start=(k == 0), stop=(k == KL - 1))
                ins.then_inc(full_of(key), 1)

            taken(pe, G_UV[-1])
            taken(pe, G_UV[-2])
            for u in range(NU + 2):
                if u < NU:
                    h, t = UNITS[u]
                    n = (t + 1) * P
                    for c in range(2):
                        o = empty(("s", u, c))
                        half = slice(c * 64, c * 64 + 64)
                        pe.matmul(o[:, 0:n], dqT[half, h, t * P:(t + 1) * P], dkT[half, h, 0:n],
                                  start=True, stop=True).then_inc(full_of(("s", u, c)), 1)
                if 1 <= u <= NU:
                    v = u - 1
                    h, t = UNITS[v]
                    pe.wait_ge(a_ready, v + 1)
                    o = empty(("pt", v))
                    for k in range(t + 1):
                        ins = pe.transpose(o[:, k * P:(k + 1) * P], srow[v % 2][0][:, k * P:(k + 1) * P], ident)
                    ins.then_inc(full_of(("pt", v)), 1)
                    taken(pe, ("pt", v))
                    o = empty(("o", v))
                    for k in range(t + 1):
                        ins = pe.matmul(o[:, 0:P], PT[v % 2][:, k * P:(k + 1) * P], dv[:, k, h * P:(h + 1) * P], start=(k == 0), stop=(k == t))
                    ins.then_inc(full_of(("o", v)), 1)
                if u >= 2 and UNITS[u - 2][1] == NT - 1:
                    h = UNITS[u - 2][0]
                    pe.wait_ge(y_ready, NT * (h + 1))
                    o = empty(("yt", h))
                    for t in range(NT):
                        ins = pe.transpose(o[:, t * P:(t + 1) * P], orow[h % 2][:, t * P:(t + 1) * P], ident)
                    ins.then_inc(full_of(("yt", h)), 1)

            for j in range(2):
                transposed(G_SQ[4 * j:4 * j + 4], f"sq{j}", xnT)

            taken(pe, G_SQ[-1])
            taken(pe, G_SQ[-2])
            pe.wait_ge(identb_ready, 1)
            pe.wait_ge(mask_ready, NT - 1)
            for u in range(NU + 1):
                if u < NU:
                    h, t = UNITS[u]
                    n = (t + 1) * P
                    o = empty(("ss", u))
                    ins = pe.matmul(o[:, 0:n], sqT[:, h, t * P:(t + 1) * P], khT[:, h, 0:n], start=True, stop=(t == 0))
                    if t:
                        ins = pe.matmul(o[:, 0:n], identb[:, :], topmask[t][:, :], start=False, stop=True)
                    ins.then_inc(full_of(("ss", u)), 1)
                if u >= 1:
                    v = u - 1
                    h, t = UNITS[v]
                    pe.wait_ge(p_ready, v + 1)
                    o = empty(("spt", v))
                    for k in range(t + 1):
                        ins = pe.transpose(o[:, k * P:(k + 1) * P], srow[v % 2][0][:, k * P:(k + 1) * P], ident)
                    ins.then_inc(full_of(("spt", v)), 1)
                    taken(pe, ("spt", v))
                    o = empty(("so", v))
                    for k in range(t + 1):
                        ins = pe.matmul(o[:, 0:P], vh[:, k, h * P:(h + 1) * P], PT[v % 2][:, k * P:(k + 1) * P], start=(k == 0), stop=(k == t))
                    ins.then_inc(full_of(("so", v)), 1)

            for v in (NU - 2, NU - 1):
                taken(pe, ("so", v))
            taken(pe, ("yt", NH - 1))
            for j in range(2):
                for name, src in (("ga", xnT), ("bd", ydT), ("gb", xnT), ("bs", ysT)):
                    transposed([(name, j, i) for i in range(NT)], f"{name}{j}", src)
            pe.wait_ge(merge_ready, KD)
            for j in range(2):
                by_token([("wo", j, t) for t in range(NT)], f"wo{j}", mergedT)

            pe.wait_ge(wr_in, 32)
            for t in range(NT):
                pe.wait_ge(hn_ready, t + 1)
                for g in range(2):
                    o = empty(("hT", t, g))
                    for k in range(4):
                        c = (4 * g + k) * P
                        ins = pe.transpose(o[:, k * P:(k + 1) * P], hn[:, t % 2, c:c + P], ident)
                    ins.then_inc(full_of(("hT", t, g)), 1)
                for g in range(2):
                    taken(pe, ("hT", t, g))
                o = empty(("lg", t))
                for k in range(KD):
                    ins = pe.matmul(o[:, 0:NE], hnT[:, t % 2, k * P:(k + 1) * P], wr[:, k, :], start=(k == 0), stop=(k == KD - 1))
                ins.then_inc(full_of(("lg", t)), 1)

            pe.wait_ge(chosen_ready, NT)
            c = empty("cntT")
            for q in range(NT):
                ins = pe.matmul(c[0:NE, 0:P], chosen[:, q, :], ones, start=(q == 0), stop=(q == NT - 1))
            ins.then_inc(full_of("cntT"), 1)

            def rank(t):
                o = empty(("rank", t))
                for q in range(t + 1):
                    ins = pe.matmul(o[:, 0:NE], tri if q == t else ones, chosen[:, q, :], start=(q == 0), stop=(q == t))
                ins.then_inc(full_of(("rank", t)), 1)

            rank(0)
            rank(1)
            taken(pe, "cntT")
            pe.matmul(empty("xb")[:, 0:NE], extra[:, :], con[0:NE, C_SU:C_SU + NE], start=True, stop=True).then_inc(full_of("xb"), 1)
            pe.matmul(empty("xeT")[0:NE, 0:P], con[0:NE, C_SUI:C_SUI + NE], extra[:, :], start=True, stop=True).then_inc(full_of("xeT"), 1)
            taken(pe, "xeT")
            o = empty("xe")
            pe.matmul(o[:, 0:16], ones[0:NE, :], before[:, :], start=True, stop=True)
            pe.matmul(o[:, 16:17], ones[0:NE, :], extra[:, 0:1], start=True, stop=True).then_inc(full_of("xe"), 1)
            rank(2)
            rank(3)

            pe.wait_ge(bparts_ready, 1)
            for b in (1, 3, 5):
                pe.wait_ge(free[b], base_use[b])

            def expert_block(i):
                pe.wait_ge(xg_in, i * 16 + 16)
                for g in range(2):
                    pe.wait_ge(free[7], i * 2 + (base_use[7] + g))
                    for k in range(4):
                        c = (4 * g + k) * P
                        ins = pe.transpose(bank[7][:, k * P:(k + 1) * P], xg[:, c:c + P], ident)
                    ins.then_inc(full[7], 1)
                pe.wait_ge(ohe_ready, i + 1)
                for half in range(2):
                    pe.wait_ge(free[2 * half], i + base_use[2 * half])
                    for q in range(2):
                        c = half * D + q * 512
                        pe.matmul(bank[2 * half + q], ohe[:, :], bparts[:, c:c + 512], start=True, stop=False)
                    if half == 0:
                        pe.wait_ge(free[7], i * 2 + (base_use[7] + 2))
                    for s in range(4):
                        slot = 4 * half + s
                        pe.wait_ge(e_in[slot], i * 16 + 16)
                        w = eslot[slot].rearrange("p (k n) -> p k n", k=2)
                        for k in range(2):
                            for q in range(2):
                                ins = pe.matmul(bank[2 * half + q], xgT[:, 2 * s + k, :], w[:, k, q * 512:(q + 1) * 512],
                                                start=False, stop=(s == 3 and k == 1))
                        ins.then_inc(e_used, 1)
                turn_hidden(i, 0)
                pe.wait_ge(free[4], i + base_use[4])
                for q in range(2):
                    pe.matmul(bank[4 + q], ohe[:, :], bparts[:, 2 * D + q * 512:2 * D + (q + 1) * 512], start=True, stop=False)
                for half in range(2):
                    if half == 1:
                        turn_hidden(i, 1)
                    pe.wait_ge(free[6], i * 2 + (base_use[6] + half + 1))
                    for s in range(2):
                        slot = 8 + 2 * half + s
                        pe.wait_ge(e_in[slot], i * 16 + 16)
                        w = eslot[slot].rearrange("p (k n) -> p k n", k=2)
                        for k in range(2):
                            for q in range(2):
                                ins = pe.matmul(bank[4 + q], hT[:, 4 * half + 2 * s + k, :], w[:, k, q * 512:(q + 1) * 512],
                                                start=False, stop=(half == 1 and s == 1 and k == 1))
                        ins.then_inc(e_used, 1)

            def turn_hidden(i, half):
                pe.wait_ge(act_ready, i * 2 + (half + 1))
                pe.wait_ge(free[6], i * 2 + (base_use[6] + half))
                for k in range(4):
                    ins = pe.transpose(bank[6][:, k * P:(k + 1) * P], act_h[half][:, k * P:(k + 1) * P], ident)
                ins.then_inc(full[6], 1)

            with pe.Fori(0, NE) as i:
                expert_block(i)
            pe.wait_ge(evals_ready, 2)
            n_extra = pe.value_load(nextra_i[0:1, 0:1], min_val=0, max_val=NX)
            with pe.If(n_extra > 0):
                with pe.Fori(0, n_extra) as j:
                    expert_block(j + NE)

        @block.scalar
        def _(act):
            act.dma_start(con[:, :], a["consts"]).then_inc(const_in, 16)
            act.wait_ge(mask_row, 3)
            act.dma_start(rest[:, 0:2 * D], zeros).then_inc(y_out, 16)
            for t in range(NT):
                act.wait_ge(x_in, 16 * NT)
                act.activation(area(16 + 4 * t, 4), xbuf[:, t, :], ACT.Square, accum_out=stat[:, t:t + 1]).then_inc(x_sq, 1)
            act.wait_ge(lam_dot, 2)
            act.activation(lam[:, 0:2], lam[:, 0:2], ACT.Exp).then_inc(lam_exp, 1)
            act.wait_ge(small_in, 16 * 9)
            for k in range(KD):
                act.activation(xnT[:, k, :], filled(act, ("xT", k)), ACT.Copy, scale=gcols[:, k:k + 1]).then_inc(free_of(("xT", k)), 1)
            for key in G_CKV:
                act.activation(cbuf[:, key[1], :], filled(act, key)[:, 0:LAT], ACT.Copy).then_inc(free_of(key), 1)
            for t in range(NT):
                taken(act, G_CKV[t])
                act.activation(area(48 + t, 1), cbuf[:, t, :], ACT.Square, accum_out=stat[:, 8 + t:9 + t]).then_inc(c_sq, 1)
            for key in G_IQ:
                act.activation(iqT[:, key[1], :], filled(act, key), ACT.Copy).then_inc(free_of(key), 1)
            act.activation(ikT, filled(act, G_IK[0]), ACT.Copy).then_inc(free_of(G_IK[0]), 1)
            for key in G_IW:
                act.activation(iw[:, key[1], :], filled(act, key)[:, 0:NI], ACT.Copy, scale=(NI * DI) ** -0.5).then_inc(free_of(key), 1)
            for k in range(KL):
                act.activation(cT[:, k, :], filled(act, ("cT", k)), ACT.Copy, scale=gcols[:, KD + k:KD + k + 1]).then_inc(free_of(("cT", k)), 1)
            for m, (t, h) in enumerate(INDEX):
                key = ("ix", t, h)
                n = (t + 1) * P
                if m >= 2:
                    act.wait_ge(relu_used, m - 1)
                act.activation(PT[m % 2][:, 0:n], filled(act, key)[:, 0:n], ACT.Relu).then_inc(free_of(key), 1)
            for key in G_DQ:
                act.activation(dqT[:, key[1], :], filled(act, key), ACT.Copy, scale=64 ** -0.5).then_inc(free_of(key), 1)
            for key in G_DK:
                act.activation(dkT[:, key[1], :], filled(act, key), ACT.Copy).then_inc(free_of(key), 1)
            act.wait_ge(y_zero, 16 * (NX // 2))
            act.wait_ge(y_out, 16)
            act.wait_ge(relu_used, len(INDEX))
            for key in G_DV:
                act.activation(dv[:, key[2], key[1] * 512:(key[1] + 1) * 512], filled(act, key), ACT.Copy).then_inc(free_of(key), 1)
            for key in G_UK:
                act.activation(khT[:, key[1], :], filled(act, key), ACT.Copy).then_inc(free_of(key), 1)
            for key in G_UV:
                act.activation(vh[:, key[2], key[1] * 512:(key[1] + 1) * 512], filled(act, key), ACT.Copy).then_inc(free_of(key), 1)

            act.wait_ge(bparts_ready, 1)
            for u in range(NU + 2):
                if u < NU:
                    n = (UNITS[u][1] + 1) * P
                    for c in range(2):
                        act.wait_ge(score_ready, 2 * u + c + 1)
                        row = srow[u % 2][c][:, 0:n]
                        act.activation(row, row, ACT.Exp, bias=row_max[u % 2][:, c:c + 1],
                                       accum_out=row_sum[u % 3][:, c:c + 1]).then_inc(exp_ready, 1)
                if 1 <= u <= NU:
                    v = u - 1
                    n = (UNITS[v][1] + 1) * P
                    if v >= 2:
                        filled(act, ("o", v - 2))
                    act.activation(PT[v % 2][:, 0:n], filled(act, ("pt", v))[:, 0:n], ACT.Copy).then_inc(free_of(("pt", v)), 1)
                if u >= 2 and UNITS[u - 2][1] == NT - 1:
                    h = UNITS[u - 2][0]
                    act.activation(ydT[:, h, :], filled(act, ("yt", h)), ACT.Copy, scale=lam[:, 3:4]).then_inc(free_of(("yt", h)), 1)
            for key in G_SQ:
                act.activation(sqT[:, key[1], :], filled(act, key), ACT.Copy).then_inc(free_of(key), 1)

            for u in range(NU + 1):
                if u < NU:
                    n = (UNITS[u][1] + 1) * P
                    act.wait_ge(sscore_ready, u + 1)
                    row = srow[u % 2][0][:, 0:n]
                    act.activation(row, row, ACT.Exp, bias=row_max[u % 2][:, 0:1],
                                   accum_out=row_sum[u % 3][:, 0:1]).then_inc(sexp_ready, 1)
                if u >= 1:
                    v = u - 1
                    h, t = UNITS[v]
                    n = (t + 1) * P
                    act.activation(PT[v % 2][:, 0:n], filled(act, ("spt", v))[:, 0:n], ACT.Copy).then_inc(free_of(("spt", v)), 1)
                    act.activation(ysT[:, h, t * P:(t + 1) * P], filled(act, ("so", v))[:, 0:P], ACT.Copy).then_inc(free_of(("so", v)), 1)

            for j in range(2):
                for g, name in enumerate(("ga", "gb")):
                    for i in range(NT):
                        key = (name, j, i)
                        if j:
                            taken(act, (("bd", "bs")[g], 0, i))
                        act.activation(sgate[:, NT * g + i, :], filled(act, key), ACT.Sigmoid).then_inc(free_of(key), 1)

            def square_h(t):
                taken(act, ("wo", 0, t))
                taken(act, ("wo", 1, t))
                if t:
                    act.wait_ge(h_sq, t)
                act.activation(ptb[:, :], hbuf[:, t, :], ACT.Square, accum_out=stat[:, 16 + t:17 + t]).then_inc(h_sq, 1)

            act.wait_ge(merge_ready, KD)
            square_h(0)
            for t in range(NT):
                if t + 1 < NT:
                    square_h(t + 1)
                for g in range(2):
                    if t >= 2:
                        filled(act, ("lg", t - 2))
                    act.activation(hnT[:, t % 2, g * 512:(g + 1) * 512], filled(act, ("hT", t, g)), ACT.Copy).then_inc(free_of(("hT", t, g)), 1)
            for t in range(NT):
                act.wait_ge(top_ready, t + 1)
                act.activation(gate[:, t, :], top_v[:, t, 0:NK], ACT.Exp, bias=vneg[:, t:t + 1],
                               accum_out=gsum[:, t:t + 1]).then_inc(gate_exp, 1)

            def expert_block(i):
                for g in range(2):
                    act.wait_ge(full[7], i * 2 + (base_use[7] + g + 1))
                    act.activation(xgT[:, 4 * g:4 * g + 4, :], bank[7].rearrange("p (k n) -> p k n", k=4), ACT.Copy).then_inc(free[7], 1)
                for half in range(2):
                    act.wait_ge(g_ready, i * 2 + (half + 1))
                    act.activation(sg_h[half], gate_h[half], ACT.Sigmoid, scale=ALPHA).then_inc(sg_ready, 1)
                    act.wait_ge(full[6], i * 2 + (base_use[6] + half + 1))
                    act.activation(hT[:, 4 * half:4 * half + 4, :], bank[6].rearrange("p (k n) -> p k n", k=4), ACT.Copy).then_inc(free[6], 1)
                act.wait_ge(e_used, i * NSLOT + NSLOT)
                act.wait_ge(y_out, i * 16 + 16)
                act.activation(ybuf, psum[:, 4 * 512:6 * 512], ACT.Copy).then_inc(free[4], 1)
                act.wait_ge(free[4], i + (base_use[4] + 1))
                act.dma_start(y_d[bass.ds(i * P, P), :], ybuf).then_inc(y_out, 16)

            with act.Fori(0, NE) as i:
                expert_block(i)
            act.wait_ge(evals_ready, 2)
            n_extra = act.value_load(nextra_i[0:1, 0:1], min_val=0, max_val=NX)
            with act.If(n_extra > 0):
                with act.Fori(0, n_extra) as j:
                    expert_block(j + NE)

            for t in range(NT):
                act.wait_ge(yg_used, NK * (t + 1))
                if t:
                    act.wait_ge(o_sq, t)
                act.activation(ptb[:, :], hbuf[:, t, :], ACT.Square, accum_out=stat[:, 24 + t:25 + t]).then_inc(o_sq, 1)

        @block.vector
        def _(dve):
            n_step = [0]

            def step(ins):
                n_step[0] += 1
                ins.then_inc(dve_step, 1)
                dve.wait_ge(dve_step, n_step[0])

            def inv_rms(src, n, width):
                m, y, t = s_ms[:, 0:n], s_rs[:, 0:n], s_nt[:, 0:n]
                step(dve.tensor_scalar(m, src, 1.0 / width, EPS, ALU.mult, ALU.add))
                step(dve.tensor_scalar(y.bitcast(I32), m.bitcast(I32), -0.5, float(0x5F3759DF), ALU.mult, ALU.add))
                for _ in range(3):
                    step(dve.tensor_tensor(t, y, y, ALU.mult))
                    step(dve.tensor_tensor(t, t, m, ALU.mult))
                    step(dve.tensor_scalar(t, t, -0.5, 1.5, ALU.mult, ALU.add))
                    step(dve.tensor_tensor(y, y, t, ALU.mult))

            s_ms, s_rs, s_nt, s_sq = (stat[:, 32 + 4 * i:36 + 4 * i] for i in range(4))
            dve.memset(tabx[NB:NB + 1, :], MASK).then_inc(mask_row, 1)
            dve.memset(carrier[:, :], 0.0).then_inc(mask_row, 1)
            dve.memset(zeros, 0.0).then_inc(mask_row, 1)
            dve.wait_ge(small_in, 16 * 9)
            for i in range(2):
                dve.tensor_tensor_reduce(lamj[:, :], lamv[:, 2 * i * DI:(2 * i + 1) * DI], lamv[:, (2 * i + 1) * DI:(2 * i + 2) * DI],
                                         1.0, 0.0, ALU.mult, ALU.add, lam[:, i:i + 1]).then_inc(lam_dot, 1)
                dve.wait_ge(lam_dot, i + 1)
            for t in range(NT):
                dve.wait_ge(x_sq, t + 1)
                inv_rms(stat[:, t:t + 1], 1, D)
                dve.tensor_scalar(xbuf[:, t, :], xbuf[:, t, :], s_rs[:, 0:1], None, ALU.mult).then_inc(x_norm, 1)
                dve.wait_ge(x_norm, t + 1)
            dve.wait_ge(const_in, 16)
            dve.tensor_copy(identb[:, :], ident).then_inc(identb_ready, 1)
            dve.tensor_copy(rvec[:, 0:512], filled(dve, "rv0")[0:2 * NH, :]).then_inc(free_of("rv0"), 1)
            dve.tensor_copy(rvec[:, 512:RLEN], filled(dve, "rv1")[0:2 * NH, 0:RLEN - 512]).then_inc(free_of("rv1"), 1)
            dve.wait_ge(lam_exp, 1)
            step(dve.tensor_tensor(lam[:, 2:3], lam[:, 1:2], lam[:, 0:1], ALU.subtract))
            step(dve.tensor_scalar(lam[:, 2:3], lam[:, 2:3], -LAM_INIT, None, ALU.add))
            step(dve.tensor_scalar(lam[:, 3:4], gcols[:, KD + KL:KD + KL + 1], OUT_SCALE, None, ALU.mult))
            for t in range(NT):
                dve.wait_ge(c_sq, t + 1)
                inv_rms(stat[:, 8 + t:9 + t], 1, LAT)
                dve.tensor_scalar(cbuf[:, t, :], cbuf[:, t, :], s_rs[:, 0:1], None, ALU.mult).then_inc(c_norm, 1)
                dve.wait_ge(c_norm, t + 1)

            for k in range(KL):
                filled(dve, ("cT", k))
            taken(dve, G_IW[-1])
            taken(dve, G_IW[-2])
            for m, (t, h) in enumerate(INDEX):
                n = (t + 1) * P
                taken(dve, ("ix", t, h))
                if m:
                    dve.wait_ge(relu_used, m)
                r, w = PT[m % 2][:, 0:n], iw[:, t, h:h + 1]
                if h == 0:
                    ins = dve.tensor_scalar(topacc[t], r, w, None, ALU.mult)
                else:
                    ins = dve.scalar_tensor_tensor(out=topacc[t], in0=r, scalar=w, in1=topacc[t], op0=ALU.mult, op1=ALU.add)
                ins.then_inc(relu_used, 1)
            dve.wait_ge(relu_used, len(INDEX))
            for t in range(1, NT):
                diag = topacc[t][:, t * P:(t + 1) * P]
                step(dve.tensor_tensor(diag, diag, con[:, C_CAUS:C_CAUS + P], ALU.add))
                for _ in range(TOPK // 8):
                    step(dve.max(v8[:, :], topacc[t]))
                    step(dve.match_replace(topacc[t], v8[:, :], topacc[t], TAKEN))
                dve.tensor_scalar(topmask[t][:, :], topacc[t], TAKEN * 0.9, MASK, ALU.is_gt, ALU.mult).then_inc(mask_ready, 1)

            dve.wait_ge(mask_ready, NT - 1)
            dve.wait_ge(strip_in, 16)
            for u in range(NU + 2):
                if u < NU:
                    h, t = UNITS[u]
                    n = (t + 1) * P
                    if u >= 2:
                        filled(dve, ("pt", u - 2))
                    for c in range(2):
                        dve.tensor_tensor(srow[u % 2][c][:, 0:n], filled(dve, ("s", u, c))[:, 0:n], strips[:, h, S - n:S],
                                          ALU.add).then_inc(free_of(("s", u, c)), 1)
                    for c in range(2):
                        taken(dve, ("s", u, c))
                        dve.tensor_reduce(row_max[u % 2][:, c:c + 1], srow[u % 2][c][:, 0:n], X, ALU.max, negate=True).then_inc(score_ready, 1)
                if 1 <= u <= NU:
                    v = u - 1
                    n = (UNITS[v][1] + 1) * P
                    r, q = row_sum[v % 3], ratio[v % 3]
                    dve.wait_ge(exp_ready, 2 * v + 2)
                    step(dve.reciprocal(q[:, 0:2], r[:, :]))
                    step(dve.tensor_scalar(q[:, 2:3], q[:, 1:2], r[:, 0:1], lam[:, 2:3], ALU.mult, ALU.mult))
                    dve.scalar_tensor_tensor(out=srow[v % 2][0][:, 0:n], in0=srow[v % 2][1][:, 0:n], scalar=q[:, 2:3],
                                             in1=srow[v % 2][0][:, 0:n], op0=ALU.mult, op1=ALU.add).then_inc(a_ready, 1)
                if u >= 2:
                    v = u - 2
                    h, t = UNITS[v]
                    if t == 0 and h >= 2:
                        filled(dve, ("yt", h - 2))
                    row = orow[h % 2][:, t * P:(t + 1) * P]
                    dve.tensor_scalar(row, filled(dve, ("o", v))[:, 0:P], ratio[v % 3][:, 0:1], None, ALU.mult).then_inc(free_of(("o", v)), 1)
                    taken(dve, ("o", v))
                    step(dve.tensor_tensor_reduce(ojunk[:, :], row, row, 1.0, 0.0, ALU.mult, ALU.add, s_sq[:, t:t + 1]))
                    if t == NT - 1:
                        inv_rms(s_sq, NT, 2 * 64)
                        for q in range(NT):
                            row = orow[h % 2][:, q * P:(q + 1) * P]
                            dve.tensor_scalar(row, row, s_rs[:, q:q + 1], None, ALU.mult).then_inc(y_ready, 1)

            dve.wait_ge(strip2_in, 16)
            for u in range(NU + 1):
                if u < NU:
                    h, t = UNITS[u]
                    n = (t + 1) * P
                    if u >= 2:
                        filled(dve, ("spt", u - 2))
                    row = srow[u % 2][0][:, 0:n]
                    dve.scalar_tensor_tensor(out=row, in0=filled(dve, ("ss", u))[:, 0:n], scalar=P ** -0.5, in1=strips[:, h, S - n:S],
                                             op0=ALU.mult, op1=ALU.add).then_inc(free_of(("ss", u)), 1)
                    taken(dve, ("ss", u))
                    dve.tensor_reduce(row_max[u % 2][:, 0:1], row, X, ALU.max, negate=True).then_inc(sscore_ready, 1)
                if u >= 1:
                    v = u - 1
                    n = (UNITS[v][1] + 1) * P
                    dve.wait_ge(sexp_ready, v + 1)
                    step(dve.reciprocal(ratio[v % 3][:, 0:1], row_sum[v % 3][:, 0:1]))
                    row = srow[v % 2][0][:, 0:n]
                    dve.tensor_scalar(row, row, ratio[v % 3][:, 0:1], None, ALU.mult).then_inc(p_ready, 1)

            for j in range(2):
                for i in range(NT):
                    taken(dve, ("ga", j, i))
                    dve.tensor_tensor(mergedT[:, NT * j + i, :], filled(dve, ("bd", j, i)), sgate[:, i, :], ALU.mult).then_inc(free_of(("bd", j, i)), 1)
                for i in range(NT):
                    taken(dve, ("gb", j, i))
                    m = mergedT[:, NT * j + i, :]
                    if NT * j + i >= 2:
                        dve.wait_ge(merge_ready, NT * j + i - 1)
                    dve.tensor_tensor(merge_tmp[i % 2], filled(dve, ("bs", j, i)), sgate[:, NT + i, :], ALU.mult).then_inc(free_of(("bs", j, i)), 1)
                    taken(dve, ("bs", j, i))
                    taken(dve, ("bd", j, i))
                    dve.tensor_tensor(m, m, merge_tmp[i % 2], ALU.add).then_inc(merge_ready, 1)
            dve.wait_ge(x_in2, 16)
            for j in range(2):
                for t in range(NT):
                    hcol = hbuf[:, t, j * 512:(j + 1) * 512]
                    dve.tensor_tensor(hcol, filled(dve, ("wo", j, t)), hcol, ALU.add).then_inc(free_of(("wo", j, t)), 1)

            dve.wait_ge(gbc_in, 32)
            dve.wait_ge(wr_in, 32)

            def norm_h(t):
                dve.wait_ge(h_sq, t + 1)
                inv_rms(stat[:, 16 + t:17 + t], 1, D)
                if t >= 2:
                    filled(dve, ("hT", t - 2, 1))
                    dve.wait_ge(hn_out[t % 2], 16 * (t // 2))
                dve.scalar_tensor_tensor(out=hn[:, t % 2, :], in0=hbuf[:, t, :], scalar=s_rs[:, 0:1], in1=gffn, op0=ALU.mult, op1=ALU.mult).then_inc(hn_ready, 1)
                dve.wait_ge(hn_ready, t + 1)

            def route(t):
                dve.tensor_tensor(logit[:, t, :], filled(dve, ("lg", t))[:, 0:NE], brt[:, :], ALU.add).then_inc(free_of(("lg", t)), 1)
                taken(dve, ("lg", t))
                step(dve.max(top_v[:, t, :], logit[:, t, :]))
                step(dve.max_index(top_i[:, t, :], top_v[:, t, :], logit[:, t, :]))
                dve.tensor_scalar(vneg[:, t:t + 1], top_v[:, t, 0:1], -1.0, None, ALU.mult).then_inc(top_ready, 1)
                step(dve.tensor_copy(top_f[:, t, :], top_i[:, t, :]))
                for k in range(NK):
                    step(dve.tensor_scalar(pick[:, t, k, :], con[:, C_E:C_E + NE], top_f[:, t, k:k + 1], None, ALU.is_equal))
                dve.tensor_reduce(chosen[:, t, :], pick[:, t].rearrange("p k e -> p e k"), X, ALU.add).then_inc(chosen_ready, 1)

            norm_h(0)
            norm_h(1)
            for t in range(NT):
                route(t)
                if t + 2 < NT:
                    norm_h(t + 2)

            cnt = filled(dve, "cntT")[0:NE, 0:P]
            step(dve.tensor_scalar(extra[:, :], cnt, P + 0.5, None, ALU.is_gt))
            step(dve.scalar_tensor_tensor(out=extra2[:, :], in0=cnt, scalar=2 * P + 0.5, in1=extra[:, :], op0=ALU.is_gt, op1=ALU.add))
            dve.scalar_tensor_tensor(out=extra[:, :], in0=cnt, scalar=3 * P + 0.5, in1=extra2[:, :], op0=ALU.is_gt, op1=ALU.add).then_inc(free_of("cntT"), 1)
            dve.scalar_tensor_tensor(out=xbase[:, :], in0=filled(dve, "xb")[:, 0:NE], scalar=float(P), in1=con[:, C_XB:C_XB + NE],
                                     op0=ALU.mult, op1=ALU.add).then_inc(free_of("xb"), 1)
            dve.tensor_tensor(before[:, :], filled(dve, "xeT")[0:NE, 0:16], con[0:NE, C_J:C_J + 16], ALU.is_le).then_inc(free_of("xeT"), 1)
            step(dve.tensor_copy(evals[:, 0:NE], con[:, C_E:C_E + NE]))
            o = filled(dve, "xe")
            dve.tensor_copy(nextra_i[:, 0:1], o[:, 16:17]).then_inc(evals_ready, 1)
            dve.tensor_scalar(evals[:, NE:NE + 16], o[:, 0:16], float(NE - 1), None, ALU.min).then_inc(free_of("xe"), 1)
            taken(dve, "xe")
            dve.tensor_copy(evals_i[:, :], evals[:, :]).then_inc(evals_ready, 1)
            taken(dve, "xb")
            for t in range(NT):
                o = filled(dve, ("rank", t))[:, 0:NE]
                step(dve.scalar_tensor_tensor(out=over[:, :], in0=o, scalar=P - 0.5, in1=xbase[:, :], op0=ALU.is_gt, op1=ALU.mult))
                dve.tensor_tensor(slot_e[:, :], o, con[:, C_EB:C_EB + NE], ALU.add).then_inc(free_of(("rank", t)), 1)
                taken(dve, ("rank", t))
                step(dve.tensor_tensor(slot_e[:, :], slot_e[:, :], over[:, :], ALU.add))
                step(dve.tensor_tensor(ptmp, pick[:, t], slot_e[:, :].unsqueeze(1).broadcast_to([P, NK, NE]), ALU.mult))
                step(dve.tensor_reduce(slot_f[:, t, :], ptmp, X, ALU.add))
                dve.tensor_copy(slot_i[:, t, :], slot_f[:, t, :]).then_inc(slots_ready, 1)
            for t in range(NT):
                dve.wait_ge(gate_exp, t + 1)
                step(dve.reciprocal(gsum[:, t:t + 1], gsum[:, t:t + 1]))
                step(dve.tensor_scalar(gate[:, t, :], gate[:, t, :], gsum[:, t:t + 1], None, ALU.mult))

            def pick_bias(i):
                dve.tensor_scalar(ohe[:, :], con[0:96, C_P32:C_P32 + P], evals[0:96, bass.ds(i, 1)], None, ALU.is_equal).then_inc(ohe_ready, 1)

            def expert_block(i):
                for half in range(2):
                    dve.wait_ge(e_used, i * NSLOT + 4 * (half + 1))
                    gu = psum[:, 1024 * half:1024 * (half + 1)].rearrange("p (n two) -> p n two", two=2)
                    dve.tensor_scalar(gate_h[half], gu[:, :, 0], LIMIT, None, ALU.min).then_inc(g_ready, 1)
                    dve.tensor_scalar(up_h[half], gu[:, :, 1], LIMIT, -LIMIT, ALU.min, ALU.max).then_inc(free[2 * half], 1)
                    dve.wait_ge(sg_ready, i * 2 + (half + 1))
                    dve.tensor_tensor(sg_h[half], gate_h[half], sg_h[half], ALU.mult).then_inc(glu_ready, 1)
                    dve.wait_ge(glu_ready, i * 2 + (half + 1))
                    dve.wait_ge(free[2 * half], i + (base_use[2 * half] + 1))
                    dve.scalar_tensor_tensor(out=act_h[half], in0=up_h[half], scalar=1.0, in1=sg_h[half],
                                             op0=ALU.add, op1=ALU.mult).then_inc(act_ready, 1)
                dve.wait_ge(e_used, i * NSLOT + 9)
                pick_bias(i + 1)

            pick_bias(0)
            with dve.Fori(0, NE) as i:
                expert_block(i)
            n_extra = dve.value_load(nextra_i[0:1, 0:1], min_val=0, max_val=NX)
            with dve.If(n_extra > 0):
                with dve.Fori(0, n_extra) as j:
                    expert_block(j + NE)

            for m in range(NT * NK):
                t, k = m // NK, m % NK
                if m:
                    dve.wait_ge(yg_used, m)
                dve.wait_ge(yg_in[m % NYG], 16 * (m // NYG + 1))
                dve.scalar_tensor_tensor(out=hbuf[:, t, :], in0=yg[m % NYG], scalar=gate[:, t, k:k + 1], in1=hbuf[:, t, :],
                                         op0=ALU.mult, op1=ALU.add).then_inc(yg_used, 1)
                if k == NK - 1:
                    dve.wait_ge(o_sq, t + 1)
                    inv_rms(stat[:, 24 + t:25 + t], 1, D)
                    dve.scalar_tensor_tensor(out=outb[t], in0=hbuf[:, t, :], scalar=s_rs[:, 0:1], in1=gfin, op0=ALU.mult, op1=ALU.mult).then_inc(o_ready, 1)
                    dve.wait_ge(o_ready, t + 1)


_INS = ["x", "norm_attn_g", "w_in", "rel_bias", "lam_q1", "lam_k1", "lam_q2", "lam_k2", "diff_subln_g", "kv_norm_g",
        "w_uk", "w_uv", "w_branch_diff", "w_branch_dsa", "w_out", "norm_ffn_g", "w_router", "b_router",
        "w_gate_up", "b_gate_up", "w_down", "b_down", "norm_final_g"]


def kernel(**inputs):
    import concourse.bacc as bacc
    from concourse.bass_utils import run_bass_kernel_spmd

    nc = bacc.Bacc("TRN2", target_bir_lowering=False, num_devices=1)
    arrays, args = {}, {}
    given = {n: np.ascontiguousarray(inputs[n]) for n in _INS}
    given["consts"] = constants()
    given["oh33"] = bucket_onehot()
    for name, v in given.items():
        arrays[f"in_{name}_dram"] = v
        args[name] = nc.dram_tensor(f"in_{name}_dram", v.shape, mybir.dt.from_np(v.dtype), kind="ExternalInput").ap()
    out = nc.dram_tensor("out_dram", (1, S, D), F32, kind="ExternalOutput").ap()
    build(nc, args, out)
    r = run_bass_kernel_spmd(nc, [arrays], core_ids=[0])
    return r.results[0]["out_dram"]
```

```python
from contextlib import ExitStack

import numpy as np

import concourse.bass as bass
from concourse import mybir
from concourse.alu_op_type import AluOpType as ALU

ACT = mybir.ActivationFunctionType
F32 = mybir.dt.float32
BF16 = mybir.dt.bfloat16
F32R = mybir.dt.float32r
I32 = mybir.dt.int32
U32 = mybir.dt.uint32
X = mybir.AxisListType.X

P = 128
D = 1024
S = 512
NT = S // P
KD = D // P
NH = 8
LAT = 256
KL = LAT // P
NI, DI = 16, 64
TOPK = min(256, S // 4)
NB = 32
MAXD = 128
NE, NK = 32, 4
F = 1024
EPS = 1e-6
LIMIT, ALPHA = 7.0, 1.702
OUT_SCALE = 1.0 - (0.8 - 0.6)
LAM_INIT = 0.8 - 0.6
MASK = -1e30
TAKEN = -3e38
NX = S * NK // P - 1
NBLK = NE + NX + 1
RLEN = S + P
IN_COLS = dict(dq=0, dk=1024, dv=2048, sq=3072, ckv=4096, iq=4352, ik=5376, iw=5440, ga=5456, gb=6480)

C_ID, C_CAUS, C_TOK, C_P32 = 0, 128, 256, 260
C_LEN = 264
C_TRI, C_ONE, C_SU, C_SUI, C_E, C_EB, C_XB, C_J = 0, 128, 256, 288, 320, 352, 384, 416
C_RLEN = 432


def constants():
    c = np.zeros((P, C_LEN + C_RLEN), np.float32)
    r = c[:, C_LEN:]
    p = np.arange(P)
    c[:, C_ID:C_ID + P] = np.eye(P)
    r[:, C_TRI:C_TRI + P] = p[:, None] < p[None, :]
    r[:, C_ONE:C_ONE + P] = 1.0
    e = np.arange(NE)
    r[:NE, C_SU:C_SU + NE] = e[:, None] < e[None, :]
    r[:NE, C_SUI:C_SUI + NE] = e[:, None] <= e[None, :]
    r[:, C_E:C_E + NE] = e
    r[:, C_EB:C_EB + NE] = P * e
    r[:, C_XB:C_XB + NE] = P * (NE - 1) - P * e
    c[:, C_TOK:C_TOK + NT] = p[:, None] + P * np.arange(NT)[None, :]
    r[:, C_J:C_J + 16] = np.arange(16)
    c[:, C_P32] = p % NE
    c[:, C_CAUS:C_CAUS + P] = np.where(p[None, :] <= p[:, None], 0.0, MASK)
    return c


def bucket_onehot():
    dist = S - 1 - np.arange(RLEN)
    n = np.maximum(dist, 0)
    half = NB // 2
    nf = np.maximum(n, 1).astype(np.float32)
    large = half + (np.log(nf / np.float32(half)) / np.float32(np.log(MAXD / half)) * np.float32(NB - half)).astype(np.int32)
    b = np.where(n < half, n, np.minimum(large, NB - 1))
    b = np.where(dist < 0, NB, b)
    return (np.arange(NB + 1)[:, None] == b[None, :]).astype(np.float32)


def build(nc, a, out):
    ctx = ExitStack()
    with ctx:
        def sb(name, cols, dt=F32, parts=P):
            return ctx.enter_context(nc.sbuf_tensor(name, [parts, cols], dt))

        def sem(name):
            return ctx.enter_context(nc.semaphore(name))

        def dram(name, shape, dt=F32):
            return nc.dram_tensor(name, shape, dt).ap()

        KB = 256
        arena_at = nc.sbuf_base
        arena_at += -arena_at % 32
        arena = sb("arena", 176 * KB)

        def area(at_kb, kb):
            return arena[:, at_kb * KB:(at_kb + kb) * KB]

        def tiles(ap, n):
            return ap.rearrange("p (a b) -> p a b", a=n)

        def typed(name, at_kb, cols, dt):
            return nc.alloc_sbuf_tensor_at(name, [P, cols], dt, offset=arena_at + at_kb * 1024)[:, :]

        xnT = tiles(area(0, 16), KD)
        zero_i = typed("zero_i", 70, NBLK, I32)
        dqT = tiles(area(16, 16), NH)
        dkT = tiles(area(32, 16), NH)
        dv = tiles(area(48, 16), NT)
        iqT = tiles(area(64, 16), NH)
        khT = tiles(area(64, 16), NH)
        xbuf = tiles(area(80, 16), NT)
        vh = tiles(area(80, 16), NT)
        ydT = tiles(area(96, 16), NH)
        ysT = tiles(area(16, 16), NH)
        sqT = tiles(area(32, 16), NH)
        mergedT = tiles(area(48, 16), KD)
        hbuf = tiles(area(96, 16), NT)
        bsplit = area(96, 12)
        NW = 3
        wring = [area(112 + 16 * i, 16) for i in range(NW)]
        strips = tiles(area(160, 16), NH)
        sgate = tiles(area(160, 16), 2 * NT)
        hn = tiles(area(160, 8), 2)
        hnT = tiles(area(168, 8), 2)
        NCH = 12
        NRAW, NSP = 6, 4
        raw = [area(8 * i, 8) for i in range(NRAW)]
        xg = area(48, 4)
        ybuf = area(52, 4)
        gate_h = [area(56 + 8 * i, 2) for i in range(2)]
        sg_h = [area(58 + 8 * i, 2) for i in range(2)]
        up_h = [area(60 + 8 * i, 2) for i in range(2)]
        act_h = [area(62 + 8 * i, 2) for i in range(2)]

        def parts_at(name, at_kb, kb):
            return typed(name, at_kb, kb * KB, F32R)

        wh = [parts_at(f"wh{i}", 72 + 8 * i, 8) if i < 3 else parts_at(f"wh{i}", 112, 8) for i in range(NSP)]
        wl = [parts_at(f"wl{i}", 120 + 8 * i, 8) for i in range(NSP)]
        xgh, xgl = (tiles(parts_at(n, 152 + 4 * i, 4), KD) for i, n in enumerate(("xgh", "xgl")))
        hTh, hTl = (tiles(parts_at(n, 160 + 4 * i, 4), KD) for i, n in enumerate(("hTh", "hTl")))
        NYG = 4
        yg = [area(4 * i, 4) for i in range(NYG)]
        outb = [area(16 + 4 * i, 4) for i in range(NT)]

        work = sb("work", 12 * KB)
        srow = [[work[:, (2 * i + c) * 512:(2 * i + c + 1) * 512] for c in range(2)] for i in range(3)]
        cbuf = tiles(work[:, 0:4 * KB], NT)
        topacc = [None] + [work[:, 0:256], work[:, 256:640], work[:, 640:1152]]
        gffn = work[:, 0:D]
        gfin = work[:, D:2 * D]
        ptb = sb("ptb", 4 * KB)
        PT = [ptb[:, i * 512:(i + 1) * 512] for i in range(2)]
        merge_tmp = [ptb[:, i * 512:(i + 1) * 512] for i in range(2)]
        cT = tiles(sb("cT", 4 * KB)[:, :], KL)
        topmask = [None] + [sb(f"topmask{t}", (t + 1) * P, BF16) for t in range(1, NT)]
        bparts = sb("bparts", 3 * D, BF16, 96)
        con = sb("con", C_LEN)
        ident = con[:, C_ID:C_ID + P]
        identb = sb("identb", P, BF16)
        zeros = area(56, 8)
        ikT = area(52, 2)
        iw = tiles(area(54, 1)[:, 0:NT * NI], NT)
        gcols = sb("gcols", KD + KL + 1)
        lamv = area(67, 1)
        lamj = area(68, 1)[:, 0:DI]
        lam = sb("lam", 4)
        tabx = area(69, 1)[0:NB + 1, 0:2 * NH]
        oh33 = area(64, 3)[0:NB + 1, 0:RLEN]
        rvec = area(108, 4)[0:2 * NH, 0:RLEN]
        stat = sb("stat", 64)
        v8 = sb("v8", 8)
        row_max = [sb(f"rowmax{i}", 4) for i in range(2)]
        row_sum = [sb(f"rowsum{i}", 2) for i in range(3)]
        ratio = [sb(f"ratio{i}", 4) for i in range(4)]
        orow = [cT[:, i, :] for i in range(2)]
        ojunk = sb("ojunk", P)
        late = [144 * KB]

        def after(cols, parts=P):
            late[0] += cols
            return arena[0:parts, late[0] - cols:late[0]]

        logit, chosen = tiles(after(NT * NE), NT), tiles(after(NT * NE), NT)
        top_v, top_f = tiles(after(NT * 8), NT), tiles(after(NT * 8), NT)
        pick = after(NT * NK * NE).rearrange("p (t k e) -> p t k e", t=NT, k=NK)
        ptmp = after(NK * NE).rearrange("p (k e) -> p k e", k=NK)
        extra, extra2, before = after(P, NE), after(P, NE), after(16, NE)
        xbase, over, slot_e, vneg = after(NE), after(NE), after(NE), after(NT)
        slot_f = tiles(after(NT * NK), NT)
        brt = after(NE)
        rcon = after(C_RLEN)
        tri = rcon[:, C_TRI:C_TRI + P]
        ones = rcon[:, C_ONE:C_ONE + P]
        wr = tiles(after(KD * NE), KD)
        top_i = tiles(typed("top_i", 158, NT * 8, U32), NT)
        evals = area(168, 1)[:, 0:NE + 16]
        evals_i = typed("evals_i", 169, NE + 16, I32)
        nextra_i = typed("nextra_i", 170, 2, I32)
        ids = typed("ids", 171, 2, I32)
        ohe = typed("ohe", 172, P, BF16)[0:96, :]
        slot_i = tiles(typed("slot_i", 173, NT * NK, I32), NT)
        gate = tiles(sb("gate", NT * NK)[:, :], NT)
        gsum = sb("gsum", NT)
        tok_i = sb("tok_i", NT, I32)
        carrier = sb("carrier", 2, F32, 1)

        psum = ctx.enter_context(nc.psum_tensor("psum", [P, 8 * 512], F32))
        bank = [psum[:, 512 * i:512 * (i + 1)] for i in range(8)]

        rv_d = dram("rv_d", (2 * NH, RLEN))
        skew_d = dram("skew_d", (2 * NH, P, RLEN))
        hn_d = dram("hn_d", (S, D))
        rowtok_d = dram("rowtok_d", (NBLK * P, 1), I32)
        y_d = dram("y_d", ((NE + NX) * P, D))
        rest = y_d[NE * P:, :].rearrange("(p r) d -> p (r d)", p=P)

        full = [sem(f"bank{i}_full") for i in range(8)]
        free = [sem(f"bank{i}_free") for i in range(8)]
        x_in, x_in2, const_in, small_in, wr_in, gbc_in = (sem(n) for n in ("x_in", "x_in2", "const_in", "small_in", "wr_in", "gbc_in"))
        mask_row, bsplit_in, bparts_ready = sem("mask_row"), sem("bsplit_in"), sem("bparts_ready")
        wring_in = [sem(f"wring{i}_in") for i in range(NW)]
        act_step, dve_step, pool_step = sem("act_step"), sem("dve_step"), sem("pool_step")
        x_sq, x_norm, c_sq, c_norm = sem("x_sq"), sem("x_norm"), sem("c_sq"), sem("c_norm")
        identb_ready, tok_ready = sem("identb_ready"), sem("tok_ready")
        y_zero = sem("y_zero")
        skew_out, carried = sem("skew_out"), sem("carried")
        rvec_out, strip_in, strip2_in = sem("rvec_out"), sem("strip_in"), sem("strip2_in")
        relu_used, mask_ready = sem("relu_used"), sem("mask_ready")
        lam_dot, lam_exp = sem("lam_dot"), sem("lam_exp")
        score_ready, exp_ready, a_ready, y_ready = sem("score_ready"), sem("exp_ready"), sem("a_ready"), sem("y_ready")
        sscore_ready, sexp_ready, p_ready = sem("sscore_ready"), sem("sexp_ready"), sem("p_ready")
        merge_ready, h_sq, hn_ready = sem("merge_ready"), sem("h_sq"), sem("hn_ready")
        hn_out = [sem(f"hn_out{i}") for i in range(2)]
        top_ready, chosen_ready, gate_exp = (
            sem(n) for n in ("top_ready", "chosen_ready", "gate_exp"))
        slots_ready, evals_ready, zero_out, scat_out = sem("slots_ready"), sem("evals_ready"), sem("zero_out"), sem("scat_out")
        raw_in = [sem(f"raw{i}_in") for i in range(NRAW)]
        wh_ready, wl_ready, hTh_ready, xgh_ready = sem("wh_ready"), sem("wl_ready"), sem("hTh_ready"), sem("xgh_ready")
        e_used, ids_in, xg_in, ohe_ready = sem("e_used"), sem("ids_in"), sem("xg_in"), sem("ohe_ready")
        g_ready, sg_ready, glu_ready, act_ready = sem("g_ready"), sem("sg_ready"), sem("glu_ready"), sem("act_ready")
        y_out = sem("y_out")
        yg_in = [sem(f"yg{i}_in") for i in range(NYG)]
        yg_used, o_sq, o_ready, out_done = sem("yg_used"), sem("o_sq"), sem("o_ready"), sem("out_done")

        CH = ["ckv", "iq0", "iq1", "ikw", "dq0", "dq1", "dk0", "dk1", "dv0", "dv1", "ukv", "sq0", "sq1"]
        for j in range(2):
            CH += [f"ga{j}", f"bd{j}", f"gb{j}", f"bs{j}"]
        CH += ["wo0", "wo1"]
        w_in_v = a["w_in"][0].rearrange("(k p) n -> p k n", p=P)

        def chunk_view(name, cols=512):
            return wring[CH.index(name) % NW][:, 0:KD * cols].rearrange("p (k n) -> p k n", k=KD)

        uses, count = {}, [0] * 8

        def plan(key, b):
            uses[key] = (b, count[b])
            count[b] += 1

        n_group = [0]
        groups = {}

        def plan_groups(keys):
            for k in keys:
                groups[k] = n_group[0]
                plan(k, n_group[0] % 2)
                n_group[0] += 1

        plan("rv0", 6)
        plan("rv1", 7)
        for k in range(KD):
            plan(("xT", k), 2 + k % 2)
        G_CKV = [("ckv", t) for t in range(NT)]
        G_IQ = [("iq", j) for j in range(NH)]
        G_IK = [("ik", 0)]
        G_IW = [("iw", t) for t in range(NT)]
        G_DQ = [("dq", j) for j in range(NH)]
        G_DK = [("dk", j) for j in range(NH)]
        G_DV = [("dv", h, t) for h in range(2) for t in range(NT)]
        G_UK = [("uk", h) for h in range(NH)]
        G_UV = [("uv", h, t) for h in range(2) for t in range(NT)]
        G_SQ = [("sq", j) for j in range(NH)]
        plan_groups(G_CKV + G_IQ + G_IK + G_IW)
        for k in range(KL):
            plan(("cT", k), 6 + k)
        INDEX = [(t, h) for t in range(1, NT) for h in range(NI)]
        for m, key in enumerate(INDEX):
            plan(("ix",) + key, 2 + m % 2)
        plan_groups(G_DQ + G_DK + G_DV + G_UK + G_UV)
        UNITS = [(h, t) for h in range(NH) for t in range(NT)]
        NU = len(UNITS)
        for u in range(NU + 6):
            if u < NU:
                for c in range(2):
                    plan(("s", u, c), 2 + 2 * (u % 2) + c)
            if 0 <= u - 2 < NU:
                plan(("pt", u - 2), 6)
            if 0 <= u - 3 < NU:
                plan(("o", u - 3), (u - 3) % 2)
            if 0 <= u - 5 < NU and UNITS[u - 5][1] == NT - 1:
                plan(("yt", UNITS[u - 5][0]), 7)
        plan_groups(G_SQ)
        for u in range(NU + 3):
            if u < NU:
                plan(("ss", u), 2 + u % 2)
            if 0 <= u - 2 < NU:
                plan(("spt", u - 2), 6 + u % 2)
            if 0 <= u - 3 < NU:
                plan(("so", u - 3), 4 + (u - 3) % 2)
        G_MERGE = [(n, j, i) for j in range(2) for n in ("ga", "bd", "gb", "bs") for i in range(NT)]
        plan_groups(G_MERGE)
        G_WO = [("wo", j, t) for j in range(2) for t in range(NT)]
        plan_groups(G_WO)
        for t in range(NT):
            plan(("hT", t, 0), 2)
            plan(("hT", t, 1), 3)
            plan(("lg", t), 4)
        for t in range(NT):
            plan(("rank", t), 5 + t % 2)
        plan("cntT", 7)
        plan("xb", 4)
        plan("xeT", 7)
        plan("xe", 4)
        base_use = list(count)
        LAST = {"ckv": G_CKV[-1], "iq0": G_IQ[3], "iq1": G_IQ[7], "ikw": G_IW[-1], "ukv": G_UV[-1]}
        for j in range(2):
            LAST.update({f"dq{j}": G_DQ[4 * j + 3], f"dk{j}": G_DK[4 * j + 3], f"sq{j}": G_SQ[4 * j + 3],
                         f"dv{j}": G_DV[4 * j + 3], f"wo{j}": ("wo", j, NT - 1)})
            LAST.update({f"{n}{j}": (n, j, NT - 1) for n in ("ga", "bd", "gb", "bs")})

        def filled(eng, key):
            b, n = uses[key]
            eng.wait_ge(full[b], n + 1)
            return bank[b]

        def taken(eng, key):
            b, n = uses[key]
            eng.wait_ge(free[b], n + 1)

        def free_of(key):
            return free[uses[key][0]]

        def ge(eng, s, value):
            if not isinstance(value, int) or value > 0:
                eng.wait_ge(s, value)

        def all_blocks(eng, one):
            one(0)
            with eng.Fori(1, NE) as i:
                one(i)
            eng.wait_ge(evals_ready, 2)
            n_extra = eng.value_load(nextra_i[0:1, 0:1], min_val=0, max_val=NX)
            with eng.If(n_extra > 0):
                with eng.Fori(0, n_extra) as j:
                    one(j + NE)
            return n_extra


        block = ctx.enter_context(nc.Block())

        @block.sync
        def _(sp):
            x_v = a["x"][0].rearrange("(t p) d -> p t d", p=P)
            for t in range(NT):
                sp.dma_start(xbuf[:, t, :], x_v[:, t, :]).then_inc(x_in, 16)
            for n, name in enumerate(CH):
                if n >= NW:
                    filled(sp, LAST[CH[n - NW]])
                done = wring_in[n % NW]
                if name == "ukv":
                    slot = wring[n % NW].rearrange("p (u k h d) -> p u k h d", u=2, k=KL, h=NH)
                    for u, w in enumerate(("w_uk", "w_uv")):
                        for k in range(KL):
                            sp.dma_start(slot[:, u, k], a[w][0].rearrange("h (k p) d -> k p h d", p=P)[k]).then_inc(done, 16)
                elif name == "ikw":
                    v = chunk_view("ikw", 2 * DI + NI)
                    c0 = IN_COLS["ik"]
                    sp.dma_start(v[:, :, 0:DI], w_in_v[:, :, c0:c0 + DI]).then_inc(done, 16)
                    sp.dma_start(v[:, :, DI:2 * DI + NI], w_in_v[:, :, c0:c0 + DI + NI]).then_inc(done, 16)
                else:
                    cols = LAT if name == "ckv" else 512
                    j = 0 if name == "ckv" else int(name[-1])
                    kind = name if name == "ckv" else name[:-1]
                    if kind in IN_COLS:
                        c0 = IN_COLS[kind] + 512 * j
                        src = w_in_v[:, :, c0:c0 + cols]
                    else:
                        w = {"bd": "w_branch_diff", "bs": "w_branch_dsa", "wo": "w_out"}[kind]
                        src = a[w][0].rearrange("(k p) n -> p k n", p=P)[:, :, 512 * j:512 * j + 512]
                    sp.dma_start(chunk_view(name, cols), src).then_inc(done, 16)
                if name == "wo1":
                    filled(sp, LAST["bd1"])
                    sp.dma_start(hbuf, x_v).then_inc(x_in2, 16)

            filled(sp, LAST["bs1"])
            gu_v = a["w_gate_up"][0].rearrange("e (c k p) n -> e c p k n", p=P, k=2)
            dn_v = a["w_down"][0].rearrange("e (c k p) n -> e c p k n", p=P, k=2)

            def load_expert(i, further=False):
                e = sp.value_load(evals_i[0:1, bass.ds(i, 1)], min_val=0, max_val=NE - 1) if further else i
                for c in range(NCH):
                    ge(sp, wl_ready, i * NCH + (c + 1 - NRAW))
                    src = gu_v[e, c % 4][:, :, (c // 4) * D:(c // 4 + 1) * D] if c < 8 else dn_v[e, c - 8]
                    sp.dma_start(raw[c % NRAW].rearrange("p (k n) -> p k n", k=2), src).then_inc(raw_in[c % NRAW], 16)

            load_expert(0)
            with sp.Fori(1, NE) as i:
                load_expert(i)
            sp.wait_ge(evals_ready, 2)
            n_extra = sp.value_load(nextra_i[0:1, 0:1], min_val=0, max_val=NX)
            with sp.If(n_extra > 0):
                with sp.Fori(0, n_extra) as j:
                    load_expert(j + NE, further=True)
            for t in range(NT):
                sp.wait_ge(o_ready, t + 1)
                sp.dma_start(out[0, t * P:(t + 1) * P, :], outb[t]).then_inc(out_done, 16)
            sp.wait_ge(out_done, 16 * NT)

        @block.gpsimd
        def _(pool):
            pool.memset(zero_i[:, :], 0).then_inc(pool_step, 1)
            pool.dma_start(tabx[0:NB, :], a["rel_bias"]).then_inc(small_in, 16)
            pool.dma_start(oh33[:, :], a["oh33"]).then_inc(small_in, 16)
            for v, c0, n in (("norm_attn_g", 0, KD), ("kv_norm_g", KD, KL), ("diff_subln_g", KD + KL, 1)):
                with nc.allow_non_contiguous_dma("gains, one per partition"):
                    pool.dma_start(gcols[:, c0:c0 + n], a[v][0].rearrange("(k p) -> p k", p=P)).then_inc(small_in, 16)
            for i, v in enumerate(("lam_q1", "lam_k1", "lam_q2", "lam_k2")):
                pool.dma_start(lamv[:, i * DI:(i + 1) * DI], a[v].broadcast_to([P, DI])).then_inc(small_in, 16)
            for r in range(3):
                pool.dma_start(bsplit[NE * r:NE * (r + 1), 0:2 * D], a["b_gate_up"][0]).then_inc(bsplit_in, 16)
                pool.dma_start(bsplit[NE * r:NE * (r + 1), 2 * D:3 * D], a["b_down"][0]).then_inc(bsplit_in, 16)
            pool.wait_ge(pool_step, 1)
            pool.dma_start(rowtok_d.rearrange("(p b) o -> p (b o)", p=P), zero_i[:, :]).then_inc(zero_out, 16)
            pool.wait_ge(const_in, 16)
            pool.tensor_copy(tok_i[:, :], con[:, C_TOK:C_TOK + NT]).then_inc(tok_ready, 1)

            pool.wait_ge(bsplit_in, 16 * 6)
            n = 1
            pool.tensor_copy(bparts[:, :], bsplit[0:96, :]).then_inc(pool_step, 1)
            for r in (1, 2):
                rows = slice(NE * r, NE * (r + 1))
                for q in range(r):
                    n += 1
                    pool.wait_ge(pool_step, n)
                    pool.tensor_tensor(bsplit[rows, :], bsplit[rows, :], bparts[rows, :], ALU.subtract).then_inc(pool_step, 1)
                    n += 1
                    pool.wait_ge(pool_step, n)
                    pool.tensor_copy(bparts[rows, :], bsplit[rows, :]).then_inc(bparts_ready if (r, q) == (2, 1) else pool_step, 1)

            pool.wait_ge(mask_row, 3)
            taken(pool, "rv0")
            taken(pool, "rv1")
            pool.dma_start(rv_d, rvec[:, :]).then_inc(rvec_out, 16)
            pool.wait_ge(rvec_out, 16)

            pool.dma_start(skew_d, rv_d.unsqueeze(1).broadcast_to([2 * NH, P, RLEN])).then_inc(skew_out, 16)
            pool.wait_ge(skew_out, 16)

            def load_strips(h0, done):
                src = bass.AP(tensor=skew_d.tensor, offset=h0 * P * RLEN + P - 1, ap=[[RLEN - 1, P], [P * RLEN, NH], [1, S]])
                pool.dma_start(strips, src).then_inc(done, 16)

            load_strips(0, strip_in)
            for r in range(2, NX, 2):
                n = min(2, NX - r) * D
                pool.dma_start(rest[:, r * D:r * D + n], zeros[:, 0:n]).then_inc(y_zero, 16)
            pool.wait_ge(score_ready, NU)
            load_strips(NH, strip2_in)
            taken(pool, ("so", NU - 1))
            pool.dma_start(gffn, a["norm_ffn_g"].broadcast_to([P, D])).then_inc(gbc_in, 16)
            pool.dma_start(gfin, a["norm_final_g"].rearrange("(o d) -> o d", o=1).broadcast_to([P, D])).then_inc(gbc_in, 16)
            filled(pool, LAST["bs1"])
            pool.dma_start(wr, a["w_router"][0].rearrange("(k p) e -> p k e", p=P)).then_inc(wr_in, 16)
            pool.dma_start(brt[:, :], a["b_router"].broadcast_to([P, NE])).then_inc(wr_in, 16)
            pool.dma_start(rcon[:, :], a["consts"][:, C_LEN:C_LEN + C_RLEN]).then_inc(wr_in, 16)

            for t in range(NT):
                pool.wait_ge(hn_ready, t + 1)
                pool.dma_start(hn_d[t * P:(t + 1) * P, :], hn[:, t % 2, :]).then_inc(hn_out[t % 2], 16)
            for r in range(2):
                pool.wait_ge(hn_out[r], 16 * NT // 2)
            pool.wait_ge(zero_out, 16)
            pool.wait_ge(tok_ready, 1)
            for t in range(NT):
                pool.wait_ge(slots_ready, t + 1)
                for k in range(NK):
                    pool.indirect_dma_start(rowtok_d, bass.IndirectOffsetOnAxis(ap=slot_i[:, t, k:k + 1], axis=0),
                                            tok_i[:, t:t + 1], None).then_inc(scat_out, 16)
            pool.wait_ge(scat_out, 16 * NT * NK)

            def settle():
                pool.tensor_tensor(carrier[:, 1:2], carrier[:, 0:1], carrier[:, 0:1], ALU.add).then_inc(carried, 1)

            def gather_block(i, first=False):
                if not first:
                    pool.wait_ge(xg_in, i * 16)
                pool.dma_start(ids[:, 0:1], rowtok_d[bass.ds(i * P, P), :]).then_inc(ids_in, 16)
                pool.wait_ge(ids_in, i * 16 + 16)
                if not first:
                    pool.wait_ge(carried, i)
                    pool.wait_ge(full[7], i * 2 + base_use[7])
                settle()
                pool.indirect_dma_start(xg, None, hn_d, bass.IndirectOffsetOnAxis(ap=ids[:, 0:1], axis=0)).then_inc(xg_in, 16)

            gather_block(0, first=True)
            with pool.Fori(1, NE + 1) as i:
                gather_block(i)
            pool.wait_ge(evals_ready, 2)
            n_extra = pool.value_load(nextra_i[0:1, 0:1], min_val=0, max_val=NX)
            with pool.If(n_extra > 0):
                with pool.Fori(0, n_extra) as j:
                    gather_block(j + (NE + 1))
            pool.wait_ge(xg_in, n_extra * 16 + 16 * (NE + 1))

            pool.wait_ge(carried, n_extra + NE + 1)
            pool.wait_ge(y_out, n_extra * 16 + 16 * (NE + 1))
            settle()
            for m in range(NT * NK):
                t, k = m // NK, m % NK
                if m >= NYG:
                    pool.wait_ge(yg_used, m - NYG + 1)
                pool.indirect_dma_start(yg[m % NYG], None, y_d,
                                        bass.IndirectOffsetOnAxis(ap=slot_i[:, t, k:k + 1], axis=0)).then_inc(yg_in[m % NYG], 16)

        @block.tensor
        def _(pe):
            def empty(key):
                b, n = uses[key]
                if n:
                    pe.wait_ge(free[b], n)
                return bank[b]

            def full_of(key):
                return full[uses[key][0]]

            def chunk_in(name):
                n = CH.index(name)
                pe.wait_ge(wring_in[n % NW], sum(16 * {"ukv": 4, "ikw": 2}.get(CH[m], 1) for m in range(n % NW, n + 1, NW)))

            def transposed(keys, chunk, src):
                chunk_in(chunk)
                w = chunk_view(chunk)
                for i, key in enumerate(keys):
                    o = empty(key)
                    for k in range(KD):
                        ins = pe.matmul(o[:, :], w[:, k, i * P:(i + 1) * P], src[:, k, :], start=(k == 0), stop=(k == KD - 1))
                    ins.then_inc(full_of(key), 1)

            def by_token(keys, chunk, src, cols=512, c0=0, width=512):
                chunk_in(chunk)
                w = chunk_view(chunk, width)
                for t, key in enumerate(keys):
                    o = empty(key)
                    for k in range(KD):
                        ins = pe.matmul(o[:, 0:cols], src[:, k, t * P:(t + 1) * P], w[:, k, c0:c0 + cols], start=(k == 0), stop=(k == KD - 1))
                    ins.then_inc(full_of(key), 1)

            pe.wait_ge(small_in, 16 * 9)
            pe.wait_ge(mask_row, 1)
            pe.matmul(empty("rv0")[0:2 * NH, :], tabx[:, :], oh33[:, 0:512], start=True, stop=True).then_inc(full_of("rv0"), 1)
            pe.matmul(empty("rv1")[0:2 * NH, 0:RLEN - 512], tabx[:, :], oh33[:, 512:RLEN], start=True, stop=True).then_inc(full_of("rv1"), 1)

            pe.wait_ge(const_in, 16)
            pe.wait_ge(x_norm, NT)
            for k in range(KD):
                o = empty(("xT", k))
                for t in range(NT):
                    ins = pe.transpose(o[:, t * P:(t + 1) * P], xbuf[:, t, k * P:(k + 1) * P], ident)
                ins.then_inc(full_of(("xT", k)), 1)

            for k in range(KD - 2, KD):
                taken(pe, ("xT", k))
            by_token(G_CKV, "ckv", xnT, cols=LAT, width=LAT)
            transposed(G_IQ[0:4], "iq0", xnT)
            transposed(G_IQ[4:8], "iq1", xnT)
            chunk_in("ikw")
            w = chunk_view("ikw", 2 * DI + NI)
            o = empty(G_IK[0])
            for k in range(KD):
                ins = pe.matmul(o[:, :], w[:, k, 0:2 * DI], xnT[:, k, :], start=(k == 0), stop=(k == KD - 1))
            ins.then_inc(full_of(G_IK[0]), 1)
            by_token(G_IW, "ikw", xnT, cols=NI, c0=2 * DI, width=2 * DI + NI)

            pe.wait_ge(c_norm, NT)
            for k in range(KL):
                o = empty(("cT", k))
                for t in range(NT):
                    ins = pe.transpose(o[:, t * P:(t + 1) * P], cbuf[:, t, k * P:(k + 1) * P], ident)
                ins.then_inc(full_of(("cT", k)), 1)

            taken(pe, G_IW[-1])
            taken(pe, G_IW[-2])
            for t, h in INDEX:
                o = empty(("ix", t, h))
                half = slice((h % 2) * DI, (h % 2 + 1) * DI)
                n = (t + 1) * P
                pe.matmul(o[:, 0:n], iqT[half, h // 2, t * P:(t + 1) * P], ikT[half, 0:n],
                          start=True, stop=True).then_inc(full_of(("ix", t, h)), 1)

            for g, c in ((G_DQ, "dq"), (G_DK, "dk")):
                for j in range(2):
                    transposed(g[4 * j:4 * j + 4], f"{c}{j}", xnT)
            for j in range(2):
                by_token(G_DV[NT * j:NT * (j + 1)], f"dv{j}", xnT)
            chunk_in("ukv")
            ukv = wring[CH.index("ukv") % NW].rearrange("p (u k n) -> p u k n", u=2, k=KL)
            for k in range(KL):
                taken(pe, ("cT", k))
            for key in G_UK:
                o = empty(key)
                for k in range(KL):
                    ins = pe.matmul(o[:, :], ukv[:, 0, k, key[1] * P:(key[1] + 1) * P], cT[:, k, :], start=(k == 0), stop=(k == KL - 1))
                ins.then_inc(full_of(key), 1)
            for key in G_UV:
                _, j, t = key
                o = empty(key)
                for k in range(KL):
                    ins = pe.matmul(o[:, :], cT[:, k, t * P:(t + 1) * P], ukv[:, 1, k, j * 512:(j + 1) * 512], start=(k == 0), stop=(k == KL - 1))
                ins.then_inc(full_of(key), 1)

            taken(pe, G_UV[-1])
            taken(pe, G_UV[-2])
            for u in range(NU + 6):
                if u < NU:
                    h, t = UNITS[u]
                    n = (t + 1) * P
                    for c in range(2):
                        o = empty(("s", u, c))
                        half = slice(c * 64, c * 64 + 64)
                        pe.matmul(o[:, 0:n], dqT[half, h, t * P:(t + 1) * P], dkT[half, h, 0:n],
                                  start=True, stop=True).then_inc(full_of(("s", u, c)), 1)
                if 0 <= u - 2 < NU:
                    v = u - 2
                    h, t = UNITS[v]
                    pe.wait_ge(a_ready, v + 1)
                    o = empty(("pt", v))
                    for k in range(t + 1):
                        ins = pe.transpose(o[:, k * P:(k + 1) * P], srow[v % 3][0][:, k * P:(k + 1) * P], ident)
                    ins.then_inc(full_of(("pt", v)), 1)
                if 0 <= u - 3 < NU:
                    v = u - 3
                    h, t = UNITS[v]
                    taken(pe, ("pt", v))
                    o = empty(("o", v))
                    for k in range(t + 1):
                        ins = pe.matmul(o[:, 0:P], PT[v % 2][:, k * P:(k + 1) * P], dv[:, k, h * P:(h + 1) * P], start=(k == 0), stop=(k == t))
                    ins.then_inc(full_of(("o", v)), 1)
                if 0 <= u - 5 < NU and UNITS[u - 5][1] == NT - 1:
                    h = UNITS[u - 5][0]
                    pe.wait_ge(y_ready, NT * (h + 1))
                    o = empty(("yt", h))
                    for t in range(NT):
                        ins = pe.transpose(o[:, t * P:(t + 1) * P], orow[h % 2][:, t * P:(t + 1) * P], ident)
                    ins.then_inc(full_of(("yt", h)), 1)

            for j in range(2):
                transposed(G_SQ[4 * j:4 * j + 4], f"sq{j}", xnT)

            taken(pe, G_SQ[-1])
            taken(pe, G_SQ[-2])
            pe.wait_ge(identb_ready, 1)
            pe.wait_ge(mask_ready, NT - 1)
            for u in range(NU + 3):
                if u < NU:
                    h, t = UNITS[u]
                    n = (t + 1) * P
                    o = empty(("ss", u))
                    ins = pe.matmul(o[:, 0:n], sqT[:, h, t * P:(t + 1) * P], khT[:, h, 0:n], start=True, stop=(t == 0))
                    if t:
                        ins = pe.matmul(o[:, 0:n], identb[:, :], topmask[t][:, :], start=False, stop=True)
                    ins.then_inc(full_of(("ss", u)), 1)
                if 0 <= u - 2 < NU:
                    v = u - 2
                    h, t = UNITS[v]
                    pe.wait_ge(p_ready, v + 1)
                    o = empty(("spt", v))
                    for k in range(t + 1):
                        ins = pe.transpose(o[:, k * P:(k + 1) * P], srow[v % 3][0][:, k * P:(k + 1) * P], ident)
                    ins.then_inc(full_of(("spt", v)), 1)
                if 0 <= u - 3 < NU:
                    v = u - 3
                    h, t = UNITS[v]
                    taken(pe, ("spt", v))
                    o = empty(("so", v))
                    for k in range(t + 1):
                        ins = pe.matmul(o[:, 0:P], vh[:, k, h * P:(h + 1) * P], PT[v % 2][:, k * P:(k + 1) * P], start=(k == 0), stop=(k == t))
                    ins.then_inc(full_of(("so", v)), 1)

            for v in (NU - 2, NU - 1):
                taken(pe, ("so", v))
            taken(pe, ("yt", NH - 1))
            for j in range(2):
                for name, src in (("ga", xnT), ("bd", ydT), ("gb", xnT), ("bs", ysT)):
                    transposed([(name, j, i) for i in range(NT)], f"{name}{j}", src)
            pe.wait_ge(merge_ready, KD)
            for j in range(2):
                by_token([("wo", j, t) for t in range(NT)], f"wo{j}", mergedT)

            pe.wait_ge(wr_in, 48)
            for t in range(NT):
                pe.wait_ge(hn_ready, t + 1)
                for g in range(2):
                    o = empty(("hT", t, g))
                    for k in range(4):
                        c = (4 * g + k) * P
                        ins = pe.transpose(o[:, k * P:(k + 1) * P], hn[:, t % 2, c:c + P], ident)
                    ins.then_inc(full_of(("hT", t, g)), 1)
                for g in range(2):
                    taken(pe, ("hT", t, g))
                o = empty(("lg", t))
                for k in range(KD):
                    ins = pe.matmul(o[:, 0:NE], hnT[:, t % 2, k * P:(k + 1) * P], wr[:, k, :], start=(k == 0), stop=(k == KD - 1))
                ins.then_inc(full_of(("lg", t)), 1)

            pe.wait_ge(chosen_ready, NT)
            c = empty("cntT")
            for q in range(NT):
                ins = pe.matmul(c[0:NE, 0:P], chosen[:, q, :], ones, start=(q == 0), stop=(q == NT - 1))
            ins.then_inc(full_of("cntT"), 1)

            def rank(t):
                o = empty(("rank", t))
                for q in range(t + 1):
                    ins = pe.matmul(o[:, 0:NE], tri if q == t else ones, chosen[:, q, :], start=(q == 0), stop=(q == t))
                ins.then_inc(full_of(("rank", t)), 1)

            rank(0)
            rank(1)
            taken(pe, "cntT")
            pe.matmul(empty("xb")[:, 0:NE], extra[:, :], rcon[0:NE, C_SU:C_SU + NE], start=True, stop=True).then_inc(full_of("xb"), 1)
            pe.matmul(empty("xeT")[0:NE, 0:P], rcon[0:NE, C_SUI:C_SUI + NE], extra[:, :], start=True, stop=True).then_inc(full_of("xeT"), 1)
            taken(pe, "xeT")
            o = empty("xe")
            pe.matmul(o[:, 0:16], ones[0:NE, :], before[:, :], start=True, stop=True)
            pe.matmul(o[:, 16:17], ones[0:NE, :], extra[:, 0:1], start=True, stop=True).then_inc(full_of("xe"), 1)
            rank(2)
            rank(3)

            pe.wait_ge(bparts_ready, 1)
            for b in (1, 3, 5):
                pe.wait_ge(free[b], base_use[b])

            def turn_rows(i, g):
                if g == 0:
                    pe.wait_ge(xg_in, i * 16 + 16)
                pe.wait_ge(free[7], i * 2 + (base_use[7] + g))
                for k in range(4):
                    c = (4 * g + k) * P
                    ins = pe.transpose(bank[7][:, k * P:(k + 1) * P], xg[:, c:c + P], ident)
                ins.then_inc(full[7], 1)

            def turn_hidden(i, half):
                pe.wait_ge(act_ready, i * 2 + (half + 1))
                pe.wait_ge(free[6], i * 2 + (base_use[6] + half))
                for k in range(4):
                    ins = pe.transpose(bank[6][:, k * P:(k + 1) * P], act_h[half][:, k * P:(k + 1) * P], ident)
                ins.then_inc(full[6], 1)

            def chunk_products(i, c, xh, xl, k0, b, last):
                pe.wait_ge(wl_ready, i * NCH + (c + 1))
                h, l = (w[c % NSP].rearrange("p (k n) -> p k n", k=2) for w in (wh, wl))
                for k in range(2):
                    for x, w in ((xh, h), (xh, l), (xl, h)):
                        for q in range(2):
                            ins = pe.matmul(bank[b + q], x[:, k0 + k, :], w[:, k, q * 512:(q + 1) * 512],
                                            start=False, stop=(last and k == 1 and x is xl))
                ins.then_inc(e_used, 1)

            def expert_block(i):
                pe.wait_ge(ohe_ready, i + 1)
                for half in range(2):
                    pe.wait_ge(free[2 * half], i + base_use[2 * half])
                    for q in range(2):
                        c = half * D + q * 512
                        pe.matmul(bank[2 * half + q], ohe[:, :], bparts[:, c:c + 512], start=True, stop=False)
                    if half == 0:
                        pe.wait_ge(free[7], i * 2 + (base_use[7] + 2))
                    for c in range(4):
                        chunk_products(i, 4 * half + c, xgh, xgl, 2 * c, 2 * half, c == 3)
                turn_hidden(i, 0)
                turn_rows(i + 1, 0)
                pe.wait_ge(free[4], i + base_use[4])
                for q in range(2):
                    pe.matmul(bank[4 + q], ohe[:, :], bparts[:, 2 * D + q * 512:2 * D + (q + 1) * 512], start=True, stop=False)
                for half in range(2):
                    if half == 1:
                        turn_hidden(i, 1)
                        turn_rows(i + 1, 1)
                    pe.wait_ge(free[6], i * 2 + (base_use[6] + half + 1))
                    for c in range(2):
                        chunk_products(i, 8 + 2 * half + c, hTh, hTl, 4 * half + 2 * c, 4, half == 1 and c == 1)

            turn_rows(0, 0)
            turn_rows(0, 1)
            all_blocks(pe, expert_block)

        @block.scalar
        def _(act):
            act.dma_start(con[:, :], a["consts"][:, 0:C_LEN]).then_inc(const_in, 16)
            act.wait_ge(mask_row, 3)
            act.dma_start(rest[:, 0:2 * D], zeros).then_inc(y_out, 16)
            for t in range(NT):
                act.wait_ge(x_in, 16 * NT)
                act.activation(area(16 + 4 * t, 4), xbuf[:, t, :], ACT.Square, accum_out=stat[:, t:t + 1]).then_inc(x_sq, 1)
            act.wait_ge(lam_dot, 2)
            act.activation(lam[:, 0:2], lam[:, 0:2], ACT.Exp).then_inc(lam_exp, 1)
            act.wait_ge(small_in, 16 * 9)
            for k in range(KD):
                act.activation(xnT[:, k, :], filled(act, ("xT", k)), ACT.Copy, scale=gcols[:, k:k + 1]).then_inc(free_of(("xT", k)), 1)
            for key in G_CKV:
                act.activation(cbuf[:, key[1], :], filled(act, key)[:, 0:LAT], ACT.Copy).then_inc(free_of(key), 1)
            for t in range(NT):
                taken(act, G_CKV[t])
                act.activation(area(48 + t, 1), cbuf[:, t, :], ACT.Square, accum_out=stat[:, 8 + t:9 + t]).then_inc(c_sq, 1)
            act.wait_ge(zero_out, 16)
            for key in G_IQ:
                act.activation(iqT[:, key[1], :], filled(act, key), ACT.Copy).then_inc(free_of(key), 1)
            act.activation(ikT, filled(act, G_IK[0]), ACT.Copy).then_inc(free_of(G_IK[0]), 1)
            for key in G_IW:
                act.activation(iw[:, key[1], :], filled(act, key)[:, 0:NI], ACT.Copy, scale=(NI * DI) ** -0.5).then_inc(free_of(key), 1)
            for k in range(KL):
                act.activation(cT[:, k, :], filled(act, ("cT", k)), ACT.Copy, scale=gcols[:, KD + k:KD + k + 1]).then_inc(free_of(("cT", k)), 1)
            for m, (t, h) in enumerate(INDEX):
                key = ("ix", t, h)
                n = (t + 1) * P
                if m >= 2:
                    act.wait_ge(relu_used, m - 1)
                act.activation(PT[m % 2][:, 0:n], filled(act, key)[:, 0:n], ACT.Relu).then_inc(free_of(key), 1)
            for key in G_DQ:
                act.activation(dqT[:, key[1], :], filled(act, key), ACT.Copy, scale=64 ** -0.5).then_inc(free_of(key), 1)
            for key in G_DK:
                act.activation(dkT[:, key[1], :], filled(act, key), ACT.Copy).then_inc(free_of(key), 1)
            act.wait_ge(y_zero, 16 * (NX // 2))
            act.wait_ge(y_out, 16)
            act.wait_ge(relu_used, len(INDEX))
            for key in G_DV:
                act.activation(dv[:, key[2], key[1] * 512:(key[1] + 1) * 512], filled(act, key), ACT.Copy).then_inc(free_of(key), 1)
            for key in G_UK:
                act.activation(khT[:, key[1], :], filled(act, key), ACT.Copy).then_inc(free_of(key), 1)
            for key in G_UV:
                act.activation(vh[:, key[2], key[1] * 512:(key[1] + 1) * 512], filled(act, key), ACT.Copy).then_inc(free_of(key), 1)

            act.wait_ge(bparts_ready, 1)
            for u in range(NU + 6):
                if u < NU:
                    n = (UNITS[u][1] + 1) * P
                    act.wait_ge(score_ready, u + 1)
                    for c in range(2):
                        row = srow[u % 3][c][:, 0:n]
                        act.activation(row, row, ACT.Exp, bias=row_max[u % 2][:, 2 + c:3 + c],
                                       accum_out=row_sum[u % 3][:, c:c + 1]).then_inc(exp_ready, 1)
                if 0 <= u - 2 < NU:
                    v = u - 2
                    n = (UNITS[v][1] + 1) * P
                    if v >= 2:
                        filled(act, ("o", v - 2))
                    act.activation(PT[v % 2][:, 0:n], filled(act, ("pt", v))[:, 0:n], ACT.Copy).then_inc(free_of(("pt", v)), 1)
                if 0 <= u - 5 < NU and UNITS[u - 5][1] == NT - 1:
                    h = UNITS[u - 5][0]
                    act.activation(ydT[:, h, :], filled(act, ("yt", h)), ACT.Copy, scale=lam[:, 3:4]).then_inc(free_of(("yt", h)), 1)
            for key in G_SQ:
                act.activation(sqT[:, key[1], :], filled(act, key), ACT.Copy, scale=P ** -0.5).then_inc(free_of(key), 1)

            for u in range(NU + 3):
                if u < NU:
                    n = (UNITS[u][1] + 1) * P
                    act.wait_ge(sscore_ready, u + 1)
                    row = srow[u % 3][0][:, 0:n]
                    act.activation(row, row, ACT.Exp, bias=row_max[u % 2][:, 2:3],
                                   accum_out=row_sum[u % 3][:, 0:1]).then_inc(sexp_ready, 1)
                if 0 <= u - 2 < NU:
                    v = u - 2
                    n = (UNITS[v][1] + 1) * P
                    if v >= 2:
                        filled(act, ("so", v - 2))
                    act.activation(PT[v % 2][:, 0:n], filled(act, ("spt", v))[:, 0:n], ACT.Copy).then_inc(free_of(("spt", v)), 1)

            for j in range(2):
                for g, name in enumerate(("ga", "gb")):
                    for i in range(NT):
                        key = (name, j, i)
                        if j:
                            taken(act, (("bd", "bs")[g], 0, i))
                        act.activation(sgate[:, NT * g + i, :], filled(act, key), ACT.Sigmoid).then_inc(free_of(key), 1)

            def square_h(t):
                taken(act, ("wo", 0, t))
                taken(act, ("wo", 1, t))
                if t:
                    act.wait_ge(h_sq, t)
                act.activation(ptb[:, :], hbuf[:, t, :], ACT.Square, accum_out=stat[:, 16 + t:17 + t]).then_inc(h_sq, 1)

            act.wait_ge(merge_ready, KD)
            square_h(0)
            for t in range(NT):
                if t + 1 < NT:
                    square_h(t + 1)
                for g in range(2):
                    if t >= 2:
                        filled(act, ("lg", t - 2))
                    act.activation(hnT[:, t % 2, g * 512:(g + 1) * 512], filled(act, ("hT", t, g)), ACT.Copy).then_inc(free_of(("hT", t, g)), 1)
            for t in range(NT):
                act.wait_ge(top_ready, t + 1)
                act.activation(gate[:, t, :], top_v[:, t, 0:NK], ACT.Exp, bias=vneg[:, t:t + 1],
                               accum_out=gsum[:, t:t + 1]).then_inc(gate_exp, 1)

            def lead(i, c):
                act.wait_ge(raw_in[c % NRAW], i * (16 * NCH // NRAW) + 16 * (c // NRAW + 1))
                ge(act, e_used, i * NCH + (c + 1 - NSP))
                act.activation(wh[c % NSP], raw[c % NRAW], ACT.Copy).then_inc(wh_ready, 1)

            def lead_rows(i, g):
                act.wait_ge(full[7], i * 2 + (base_use[7] + g + 1))
                act.activation(xgh[:, 4 * g:4 * g + 4, :], bank[7].rearrange("p (k n) -> p k n", k=4), ACT.Copy).then_inc(xgh_ready, 1)

            def lead_hidden(i, half):
                act.wait_ge(full[6], i * 2 + (base_use[6] + half + 1))
                act.activation(hTh[:, 4 * half:4 * half + 4, :], bank[6].rearrange("p (k n) -> p k n", k=4), ACT.Copy).then_inc(hTh_ready, 1)

            def sigmoid(i, half):
                act.wait_ge(g_ready, i * 2 + (half + 1))
                act.activation(sg_h[half], gate_h[half], ACT.Sigmoid, scale=ALPHA).then_inc(sg_ready, 1)

            def store_rows(i):
                act.wait_ge(e_used, i * NCH + NCH)
                act.wait_ge(y_out, i * 16 + 16)
                act.activation(ybuf, psum[:, 4 * 512:6 * 512], ACT.Copy).then_inc(free[4], 1)
                act.wait_ge(free[4], i + (base_use[4] + 1))
                act.dma_start(y_d[bass.ds(i * P, P), :], ybuf).then_inc(y_out, 16)

            def expert_block(i):
                for c in range(4):
                    lead(i, c)
                if not isinstance(i, int):
                    store_rows(i - 1)
                for c in range(4, 8):
                    lead(i, c)
                sigmoid(i, 0)
                for c in range(8, 11):
                    lead(i, c)
                lead_hidden(i, 0)
                sigmoid(i, 1)
                lead(i, 11)
                lead_rows(i + 1, 0)
                lead_hidden(i, 1)
                lead_rows(i + 1, 1)

            lead_rows(0, 0)
            lead_rows(0, 1)
            n_extra = all_blocks(act, expert_block)
            store_rows(n_extra + (NE - 1))

            for t in range(NT):
                act.wait_ge(yg_used, NK * (t + 1))
                if t:
                    act.wait_ge(o_sq, t)
                act.activation(ptb[:, :], hbuf[:, t, :], ACT.Square, accum_out=stat[:, 24 + t:25 + t]).then_inc(o_sq, 1)

        @block.vector
        def _(dve):
            n_step = [0]

            def step(ins):
                n_step[0] += 1
                ins.then_inc(dve_step, 1)
                dve.wait_ge(dve_step, n_step[0])

            def inv_rms(src, n, width):
                m, y, t = s_ms[:, 0:n], s_rs[:, 0:n], s_nt[:, 0:n]
                step(dve.tensor_scalar(m, src, 1.0 / width, EPS, ALU.mult, ALU.add))
                step(dve.tensor_scalar(y.bitcast(I32), m.bitcast(I32), -0.5, float(0x5F3759DF), ALU.mult, ALU.add))
                for _ in range(3):
                    step(dve.tensor_tensor(t, y, y, ALU.mult))
                    step(dve.tensor_tensor(t, t, m, ALU.mult))
                    step(dve.tensor_scalar(t, t, -0.5, 1.5, ALU.mult, ALU.add))
                    step(dve.tensor_tensor(y, y, t, ALU.mult))

            s_ms, s_rs, s_nt, s_sq = (stat[:, 32 + 4 * i:36 + 4 * i] for i in range(4))
            dve.memset(tabx[NB:NB + 1, :], MASK).then_inc(mask_row, 1)
            dve.memset(carrier[:, :], 0.0).then_inc(mask_row, 1)
            dve.memset(zeros, 0.0).then_inc(mask_row, 1)
            dve.wait_ge(small_in, 16 * 9)
            for i in range(2):
                dve.tensor_tensor_reduce(lamj[:, :], lamv[:, 2 * i * DI:(2 * i + 1) * DI], lamv[:, (2 * i + 1) * DI:(2 * i + 2) * DI],
                                         1.0, 0.0, ALU.mult, ALU.add, lam[:, i:i + 1]).then_inc(lam_dot, 1)
                dve.wait_ge(lam_dot, i + 1)
            for t in range(NT):
                dve.wait_ge(x_sq, t + 1)
                inv_rms(stat[:, t:t + 1], 1, D)
                dve.tensor_scalar(xbuf[:, t, :], xbuf[:, t, :], s_rs[:, 0:1], None, ALU.mult).then_inc(x_norm, 1)
                dve.wait_ge(x_norm, t + 1)
            dve.wait_ge(const_in, 16)
            dve.tensor_copy(identb[:, :], ident).then_inc(identb_ready, 1)
            dve.tensor_copy(rvec[:, 0:512], filled(dve, "rv0")[0:2 * NH, :]).then_inc(free_of("rv0"), 1)
            dve.tensor_copy(rvec[:, 512:RLEN], filled(dve, "rv1")[0:2 * NH, 0:RLEN - 512]).then_inc(free_of("rv1"), 1)
            dve.wait_ge(lam_exp, 1)
            step(dve.tensor_tensor(lam[:, 2:3], lam[:, 1:2], lam[:, 0:1], ALU.subtract))
            step(dve.tensor_scalar(lam[:, 2:3], lam[:, 2:3], -LAM_INIT, None, ALU.add))
            step(dve.tensor_scalar(lam[:, 3:4], gcols[:, KD + KL:KD + KL + 1], OUT_SCALE, None, ALU.mult))
            for t in range(NT):
                dve.wait_ge(c_sq, t + 1)
                inv_rms(stat[:, 8 + t:9 + t], 1, LAT)
                dve.tensor_scalar(cbuf[:, t, :], cbuf[:, t, :], s_rs[:, 0:1], None, ALU.mult).then_inc(c_norm, 1)
                dve.wait_ge(c_norm, t + 1)

            for k in range(KL):
                filled(dve, ("cT", k))
            taken(dve, G_IW[-1])
            taken(dve, G_IW[-2])
            for m, (t, h) in enumerate(INDEX):
                n = (t + 1) * P
                taken(dve, ("ix", t, h))
                if m:
                    dve.wait_ge(relu_used, m)
                r, w = PT[m % 2][:, 0:n], iw[:, t, h:h + 1]
                if h == 0:
                    ins = dve.tensor_scalar(topacc[t], r, w, None, ALU.mult)
                else:
                    ins = dve.scalar_tensor_tensor(out=topacc[t], in0=r, scalar=w, in1=topacc[t], op0=ALU.mult, op1=ALU.add)
                ins.then_inc(relu_used, 1)
            dve.wait_ge(relu_used, len(INDEX))
            for t in range(1, NT):
                diag = topacc[t][:, t * P:(t + 1) * P]
                step(dve.tensor_tensor(diag, diag, con[:, C_CAUS:C_CAUS + P], ALU.add))
                for _ in range(TOPK // 8):
                    step(dve.max(v8[:, :], topacc[t]))
                    step(dve.match_replace(topacc[t], v8[:, :], topacc[t], TAKEN))
                dve.tensor_scalar(topmask[t][:, :], topacc[t], TAKEN * 0.9, MASK, ALU.is_gt, ALU.mult).then_inc(mask_ready, 1)

            dve.wait_ge(mask_ready, NT - 1)
            dve.wait_ge(strip_in, 16)
            for u in range(NU + 6):
                if u < NU:
                    h, t = UNITS[u]
                    n = (t + 1) * P
                    if u >= 3:
                        filled(dve, ("pt", u - 3))
                    for c in range(2):
                        dve.tensor_tensor_reduce(srow[u % 3][c][:, 0:n], filled(dve, ("s", u, c))[:, 0:n], strips[:, h, S - n:S], 1.0, 3 * MASK,
                                                 ALU.add, ALU.max, row_max[u % 2][:, c:c + 1]).then_inc(free_of(("s", u, c)), 1)
                    for c in range(2):
                        taken(dve, ("s", u, c))
                    dve.tensor_scalar(row_max[u % 2][:, 2:4], row_max[u % 2][:, 0:2], -1.0, None, ALU.mult).then_inc(score_ready, 1)
                if 1 <= u <= NU:
                    v = u - 1
                    n = (UNITS[v][1] + 1) * P
                    r, q = row_sum[v % 3], ratio[v % 4]
                    dve.wait_ge(exp_ready, 2 * v + 2)
                    step(dve.reciprocal(q[:, 0:2], r[:, :]))
                    step(dve.tensor_scalar(q[:, 2:3], q[:, 1:2], r[:, 0:1], lam[:, 2:3], ALU.mult, ALU.mult))
                    dve.scalar_tensor_tensor(out=srow[v % 3][0][:, 0:n], in0=srow[v % 3][1][:, 0:n], scalar=q[:, 2:3],
                                             in1=srow[v % 3][0][:, 0:n], op0=ALU.mult, op1=ALU.add).then_inc(a_ready, 1)
                if 0 <= u - 4 < NU:
                    v = u - 4
                    h, t = UNITS[v]
                    if t == 0 and h >= 2:
                        filled(dve, ("yt", h - 2))
                    row = orow[h % 2][:, t * P:(t + 1) * P]
                    dve.tensor_scalar(row, filled(dve, ("o", v))[:, 0:P], ratio[v % 4][:, 0:1], None, ALU.mult).then_inc(free_of(("o", v)), 1)
                    taken(dve, ("o", v))
                    step(dve.tensor_tensor_reduce(ojunk[:, :], row, row, 1.0, 0.0, ALU.mult, ALU.add, s_sq[:, t:t + 1]))
                    if t == NT - 1:
                        inv_rms(s_sq, NT, 2 * 64)
                        for q in range(NT):
                            row = orow[h % 2][:, q * P:(q + 1) * P]
                            dve.tensor_scalar(row, row, s_rs[:, q:q + 1], None, ALU.mult).then_inc(y_ready, 1)

            dve.wait_ge(strip2_in, 16)
            for u in range(NU + 4):
                if u < NU:
                    h, t = UNITS[u]
                    n = (t + 1) * P
                    if u >= 3:
                        filled(dve, ("spt", u - 3))
                    dve.tensor_tensor_reduce(srow[u % 3][0][:, 0:n], filled(dve, ("ss", u))[:, 0:n], strips[:, h, S - n:S], 1.0, 3 * MASK,
                                             ALU.add, ALU.max, row_max[u % 2][:, 0:1]).then_inc(free_of(("ss", u)), 1)
                    taken(dve, ("ss", u))
                    dve.tensor_scalar(row_max[u % 2][:, 2:3], row_max[u % 2][:, 0:1], -1.0, None, ALU.mult).then_inc(sscore_ready, 1)
                if 1 <= u <= NU:
                    v = u - 1
                    n = (UNITS[v][1] + 1) * P
                    dve.wait_ge(sexp_ready, v + 1)
                    step(dve.reciprocal(ratio[v % 4][:, 0:1], row_sum[v % 3][:, 0:1]))
                    row = srow[v % 3][0][:, 0:n]
                    dve.tensor_scalar(row, row, ratio[v % 4][:, 0:1], None, ALU.mult).then_inc(p_ready, 1)
                if 0 <= u - 4 < NU:
                    v = u - 4
                    h, t = UNITS[v]
                    dve.tensor_copy(ysT[:, h, t * P:(t + 1) * P], filled(dve, ("so", v))[:, 0:P]).then_inc(free_of(("so", v)), 1)

            for j in range(2):
                for i in range(NT):
                    taken(dve, ("ga", j, i))
                    dve.tensor_tensor(mergedT[:, NT * j + i, :], filled(dve, ("bd", j, i)), sgate[:, i, :], ALU.mult).then_inc(free_of(("bd", j, i)), 1)
                for i in range(NT):
                    taken(dve, ("gb", j, i))
                    m = mergedT[:, NT * j + i, :]
                    if NT * j + i >= 2:
                        dve.wait_ge(merge_ready, NT * j + i - 1)
                    dve.tensor_tensor(merge_tmp[i % 2], filled(dve, ("bs", j, i)), sgate[:, NT + i, :], ALU.mult).then_inc(free_of(("bs", j, i)), 1)
                    taken(dve, ("bs", j, i))
                    taken(dve, ("bd", j, i))
                    dve.tensor_tensor(m, m, merge_tmp[i % 2], ALU.add).then_inc(merge_ready, 1)
            dve.wait_ge(x_in2, 16)
            for j in range(2):
                for t in range(NT):
                    hcol = hbuf[:, t, j * 512:(j + 1) * 512]
                    dve.tensor_tensor(hcol, filled(dve, ("wo", j, t)), hcol, ALU.add).then_inc(free_of(("wo", j, t)), 1)

            dve.wait_ge(gbc_in, 32)
            dve.wait_ge(wr_in, 48)

            def norm_h(t):
                dve.wait_ge(h_sq, t + 1)
                inv_rms(stat[:, 16 + t:17 + t], 1, D)
                if t >= 2:
                    filled(dve, ("hT", t - 2, 1))
                    dve.wait_ge(hn_out[t % 2], 16 * (t // 2))
                dve.scalar_tensor_tensor(out=hn[:, t % 2, :], in0=hbuf[:, t, :], scalar=s_rs[:, 0:1], in1=gffn, op0=ALU.mult, op1=ALU.mult).then_inc(hn_ready, 1)
                dve.wait_ge(hn_ready, t + 1)

            def route(t):
                dve.tensor_tensor(logit[:, t, :], filled(dve, ("lg", t))[:, 0:NE], brt[:, :], ALU.add).then_inc(free_of(("lg", t)), 1)
                taken(dve, ("lg", t))
                step(dve.max(top_v[:, t, :], logit[:, t, :]))
                step(dve.max_index(top_i[:, t, :], top_v[:, t, :], logit[:, t, :]))
                dve.tensor_scalar(vneg[:, t:t + 1], top_v[:, t, 0:1], -1.0, None, ALU.mult).then_inc(top_ready, 1)
                step(dve.tensor_copy(top_f[:, t, :], top_i[:, t, :]))
                for k in range(NK):
                    step(dve.tensor_scalar(pick[:, t, k, :], rcon[:, C_E:C_E + NE], top_f[:, t, k:k + 1], None, ALU.is_equal))
                dve.tensor_reduce(chosen[:, t, :], pick[:, t].rearrange("p k e -> p e k"), X, ALU.add).then_inc(chosen_ready, 1)

            norm_h(0)
            norm_h(1)
            for t in range(NT):
                route(t)
                if t + 2 < NT:
                    norm_h(t + 2)

            cnt = filled(dve, "cntT")[0:NE, 0:P]
            step(dve.tensor_scalar(extra[:, :], cnt, P + 0.5, None, ALU.is_gt))
            step(dve.scalar_tensor_tensor(out=extra2[:, :], in0=cnt, scalar=2 * P + 0.5, in1=extra[:, :], op0=ALU.is_gt, op1=ALU.add))
            dve.scalar_tensor_tensor(out=extra[:, :], in0=cnt, scalar=3 * P + 0.5, in1=extra2[:, :], op0=ALU.is_gt, op1=ALU.add).then_inc(free_of("cntT"), 1)
            dve.scalar_tensor_tensor(out=xbase[:, :], in0=filled(dve, "xb")[:, 0:NE], scalar=float(P), in1=rcon[:, C_XB:C_XB + NE],
                                     op0=ALU.mult, op1=ALU.add).then_inc(free_of("xb"), 1)
            dve.tensor_tensor(before[:, :], filled(dve, "xeT")[0:NE, 0:16], rcon[0:NE, C_J:C_J + 16], ALU.is_le).then_inc(free_of("xeT"), 1)
            step(dve.tensor_copy(evals[:, 0:NE], rcon[:, C_E:C_E + NE]))
            o = filled(dve, "xe")
            dve.tensor_copy(nextra_i[:, 0:1], o[:, 16:17]).then_inc(evals_ready, 1)
            dve.tensor_scalar(evals[:, NE:NE + 16], o[:, 0:16], float(NE - 1), None, ALU.min).then_inc(free_of("xe"), 1)
            taken(dve, "xe")
            dve.tensor_copy(evals_i[:, :], evals[:, :]).then_inc(evals_ready, 1)
            taken(dve, "xb")
            for t in range(NT):
                o = filled(dve, ("rank", t))[:, 0:NE]
                step(dve.scalar_tensor_tensor(out=over[:, :], in0=o, scalar=P - 0.5, in1=xbase[:, :], op0=ALU.is_gt, op1=ALU.mult))
                dve.tensor_tensor(slot_e[:, :], o, rcon[:, C_EB:C_EB + NE], ALU.add).then_inc(free_of(("rank", t)), 1)
                taken(dve, ("rank", t))
                step(dve.tensor_tensor(slot_e[:, :], slot_e[:, :], over[:, :], ALU.add))
                step(dve.tensor_tensor(ptmp, pick[:, t], slot_e[:, :].unsqueeze(1).broadcast_to([P, NK, NE]), ALU.mult))
                step(dve.tensor_reduce(slot_f[:, t, :], ptmp, X, ALU.add))
                dve.tensor_copy(slot_i[:, t, :], slot_f[:, t, :]).then_inc(slots_ready, 1)
            for t in range(NT):
                dve.wait_ge(gate_exp, t + 1)
                step(dve.reciprocal(gsum[:, t:t + 1], gsum[:, t:t + 1]))
                step(dve.tensor_scalar(gate[:, t, :], gate[:, t, :], gsum[:, t:t + 1], None, ALU.mult))

            def pick_bias(i):
                dve.tensor_scalar(ohe[:, :], con[0:96, C_P32:C_P32 + 1].broadcast_to([96, P]), evals[0:96, bass.ds(i, 1)], None, ALU.is_equal).then_inc(ohe_ready, 1)

            def rest_of(i, c):
                dve.wait_ge(wh_ready, i * NCH + (c + 1))
                dve.tensor_tensor(wl[c % NSP], raw[c % NRAW], wh[c % NSP].bitcast(F32), ALU.subtract).then_inc(wl_ready, 1)

            def rest_rows(i, g):
                dve.wait_ge(xgh_ready, i * 2 + (g + 1))
                dve.tensor_tensor(xgl[:, 4 * g:4 * g + 4, :], bank[7].rearrange("p (k n) -> p k n", k=4),
                                  xgh[:, 4 * g:4 * g + 4, :].bitcast(F32), ALU.subtract).then_inc(free[7], 1)

            def rest_hidden(i, half):
                dve.wait_ge(hTh_ready, i * 2 + (half + 1))
                dve.tensor_tensor(hTl[:, 4 * half:4 * half + 4, :], bank[6].rearrange("p (k n) -> p k n", k=4),
                                  hTh[:, 4 * half:4 * half + 4, :].bitcast(F32), ALU.subtract).then_inc(free[6], 1)

            def clamp(i, half):
                dve.wait_ge(e_used, i * NCH + 4 * (half + 1))
                gu = psum[:, 1024 * half:1024 * (half + 1)].rearrange("p (n two) -> p n two", two=2)
                dve.tensor_scalar(gate_h[half], gu[:, :, 0], LIMIT, None, ALU.min).then_inc(g_ready, 1)
                dve.tensor_scalar(up_h[half], gu[:, :, 1], LIMIT, -LIMIT, ALU.min, ALU.max).then_inc(free[2 * half], 1)

            def activate(i, half):
                dve.wait_ge(sg_ready, i * 2 + (half + 1))
                dve.tensor_tensor(sg_h[half], gate_h[half], sg_h[half], ALU.mult).then_inc(glu_ready, 1)
                dve.wait_ge(glu_ready, i * 2 + (half + 1))
                dve.wait_ge(free[2 * half], i + (base_use[2 * half] + 1))
                dve.scalar_tensor_tensor(out=act_h[half], in0=up_h[half], scalar=1.0, in1=sg_h[half],
                                         op0=ALU.add, op1=ALU.mult).then_inc(act_ready, 1)

            def expert_block(i):
                for c in range(7):
                    rest_of(i, c)
                clamp(i, 0)
                rest_of(i, 7)
                activate(i, 0)
                for c in range(8, 11):
                    rest_of(i, c)
                rest_hidden(i, 0)
                clamp(i, 1)
                rest_of(i, 11)
                activate(i, 1)
                rest_rows(i + 1, 0)
                rest_hidden(i, 1)
                rest_rows(i + 1, 1)
                dve.wait_ge(e_used, i * NCH + 9)
                pick_bias(i + 1)

            pick_bias(0)
            rest_rows(0, 0)
            rest_rows(0, 1)
            all_blocks(dve, expert_block)

            for m in range(NT * NK):
                t, k = m // NK, m % NK
                if m:
                    dve.wait_ge(yg_used, m)
                dve.wait_ge(yg_in[m % NYG], 16 * (m // NYG + 1))
                dve.scalar_tensor_tensor(out=hbuf[:, t, :], in0=yg[m % NYG], scalar=gate[:, t, k:k + 1], in1=hbuf[:, t, :],
                                         op0=ALU.mult, op1=ALU.add).then_inc(yg_used, 1)
                if k == NK - 1:
                    dve.wait_ge(o_sq, t + 1)
                    inv_rms(stat[:, 24 + t:25 + t], 1, D)
                    dve.scalar_tensor_tensor(out=outb[t], in0=hbuf[:, t, :], scalar=s_rs[:, 0:1], in1=gfin, op0=ALU.mult, op1=ALU.mult).then_inc(o_ready, 1)
                    dve.wait_ge(o_ready, t + 1)


_INS = ["x", "norm_attn_g", "w_in", "rel_bias", "lam_q1", "lam_k1", "lam_q2", "lam_k2", "diff_subln_g", "kv_norm_g",
        "w_uk", "w_uv", "w_branch_diff", "w_branch_dsa", "w_out", "norm_ffn_g", "w_router", "b_router",
        "w_gate_up", "b_gate_up", "w_down", "b_down", "norm_final_g"]


def kernel(**inputs):
    import concourse.bacc as bacc
    from concourse.bass_utils import run_bass_kernel_spmd

    nc = bacc.Bacc("TRN2", target_bir_lowering=False, num_devices=1)
    arrays, args = {}, {}
    given = {n: np.ascontiguousarray(inputs[n]) for n in _INS}
    given["consts"] = constants()
    given["oh33"] = bucket_onehot()
    for name, v in given.items():
        arrays[f"in_{name}_dram"] = v
        args[name] = nc.dram_tensor(f"in_{name}_dram", v.shape, mybir.dt.from_np(v.dtype), kind="ExternalInput").ap()
    out = nc.dram_tensor("out_dram", (1, S, D), F32, kind="ExternalOutput").ap()
    build(nc, args, out)
    r = run_bass_kernel_spmd(nc, [arrays], core_ids=[0])
    return r.results[0]["out_dram"]
```

```python
from contextlib import ExitStack

import numpy as np

import concourse.bass as bass
from concourse import mybir
from concourse.alu_op_type import AluOpType as ALU

ACT = mybir.ActivationFunctionType
F32 = mybir.dt.float32
BF16 = mybir.dt.bfloat16
F32R = mybir.dt.float32r
I32 = mybir.dt.int32
U32 = mybir.dt.uint32
X = mybir.AxisListType.X

P = 128
D = 1024
S = 512
NT = S // P
KD = D // P
NH = 8
LAT = 256
KL = LAT // P
NI, DI = 16, 64
TOPK = min(256, S // 4)
NB = 32
MAXD = 128
NE, NK = 32, 4
F = 1024
EPS = 1e-6
LIMIT, ALPHA = 7.0, 1.702
OUT_SCALE = 1.0 - (0.8 - 0.6)
LAM_INIT = 0.8 - 0.6
MASK = -1e30
TAKEN = -3e38
NX = S * NK // P - 1
NBLK = NE + NX + 1
RLEN = S + P
IN_COLS = dict(dq=0, dk=1024, dv=2048, sq=3072, ckv=4096, iq=4352, ik=5376, iw=5440, ga=5456, gb=6480)

C_ID, C_CAUS, C_TOK, C_P32 = 0, 128, 256, 260
C_LEN = 264
C_TRI, C_ONE, C_SU, C_SUI, C_E, C_EB, C_XB, C_J = 0, 128, 256, 288, 320, 352, 384, 416
C_RLEN = 432


def constants():
    c = np.zeros((P, C_LEN + C_RLEN), np.float32)
    r = c[:, C_LEN:]
    p = np.arange(P)
    c[:, C_ID:C_ID + P] = np.eye(P)
    r[:, C_TRI:C_TRI + P] = p[:, None] < p[None, :]
    r[:, C_ONE:C_ONE + P] = 1.0
    e = np.arange(NE)
    r[:NE, C_SU:C_SU + NE] = e[:, None] < e[None, :]
    r[:NE, C_SUI:C_SUI + NE] = e[:, None] <= e[None, :]
    r[:, C_E:C_E + NE] = e
    r[:, C_EB:C_EB + NE] = P * e
    r[:, C_XB:C_XB + NE] = P * (NE - 1) - P * e
    c[:, C_TOK:C_TOK + NT] = p[:, None] + P * np.arange(NT)[None, :]
    r[:, C_J:C_J + 16] = np.arange(16)
    c[:, C_P32] = p % NE
    c[:, C_CAUS:C_CAUS + P] = np.where(p[None, :] <= p[:, None], 0.0, MASK)
    return c


def bucket_onehot():
    dist = S - 1 - np.arange(RLEN)
    n = np.maximum(dist, 0)
    half = NB // 2
    nf = np.maximum(n, 1).astype(np.float32)
    large = half + (np.log(nf / np.float32(half)) / np.float32(np.log(MAXD / half)) * np.float32(NB - half)).astype(np.int32)
    b = np.where(n < half, n, np.minimum(large, NB - 1))
    b = np.where(dist < 0, NB, b)
    return (np.arange(NB + 1)[:, None] == b[None, :]).astype(np.float32)


def build(nc, a, out):
    ctx = ExitStack()
    with ctx:
        def sb(name, cols, dt=F32, parts=P):
            return ctx.enter_context(nc.sbuf_tensor(name, [parts, cols], dt))

        def sem(name):
            return ctx.enter_context(nc.semaphore(name))

        def dram(name, shape, dt=F32):
            return nc.dram_tensor(name, shape, dt).ap()

        KB = 256
        arena_at = nc.sbuf_base
        arena_at += -arena_at % 32
        arena = sb("arena", 176 * KB)
        work = sb("work", 12 * KB)
        latent = sb("latent", 4 * KB)
        ptb = sb("ptb", 4 * KB)

        def tiles(ap, n):
            return ap.rearrange("p (a b) -> p a b", a=n)

        def area(at_kb, kb):
            return arena[:, at_kb * KB:(at_kb + kb) * KB]

        def typed(name, at_kb, cols, dt):
            return nc.alloc_sbuf_tensor_at(name, [P, cols], dt, offset=arena_at + at_kb * 1024)[:, :]

        cT = tiles(latent[:, :], KL)
        xnT = tiles(area(0, 16), KD)
        def parts_at(name, at_kb, kb):
            return typed(name, at_kb, kb * KB, F32R)

        zero_i = typed("zero_i", 70, NBLK, I32)
        dqT = tiles(area(16, 16), NH)
        dkT = tiles(area(32, 16), NH)
        dv = tiles(area(48, 16), NT)
        iqT = tiles(area(64, 16), NH)
        khT = tiles(area(64, 16), NH)
        xbuf = tiles(area(80, 16), NT)
        vh = tiles(area(80, 16), NT)
        ydT = tiles(area(96, 16), NH)
        ysT = tiles(area(16, 16), NH)
        sqT = tiles(area(32, 16), NH)
        mergedT = tiles(area(48, 16), KD)
        hbuf = tiles(area(96, 16), NT)
        bsplit = area(96, 12)
        NW = 3
        wring = [area(112 + 16 * i, 16) for i in range(NW)]
        strips = tiles(area(160, 16), NH)
        sgate = tiles(area(160, 16), 2 * NT)
        hn = tiles(area(160, 8), 2)
        hnT = tiles(area(168, 8), 2)
        ERING = 4
        ring_h, ring_l = ([[parts_at(f"{n}{at}_{i}", at + 2 * i, 2) for i in range(ERING)] for at in ats]
                          for n, ats in (("early_h", (16, 96)), ("early_l", (24, 104))))
        xe_h, xe_l = (tiles(parts_at(n, at, 16), KD) for n, at in (("xe_h", 80), ("xe_l", 160)))
        PK = 2
        PIECES = KD // PK
        late_ring = [area(128, 16), area(112, 16)]
        piece_h = [tiles(parts_at(f"piece_h{i}", 80 + 4 * i, 4), PK) for i in range(PIECES)]
        piece_l = [tiles(parts_at(f"piece_l{i}", 144 + 4 * i, 4), PK) for i in range(PIECES)]
        xn_h, xn_l = (tiles(parts_at(n, at, 16), KD) for n, at in (("xn_h", 0), ("xn_l", 32)))
        ys_h, ys_l = (tiles(parts_at(n, at, 16), KD) for n, at in (("ys_h", 16), ("ys_l", 64)))
        yd_h, yd_l = (tiles(parts_at(n, at, 16), KD) for n, at in (("yd_h", 96), ("yd_l", 176)))
        m_h, m_l = tiles(parts_at("m_h", 48, 16), KD), yd_l
        NCH = 12
        NRAW, NSP = 6, 4
        raw = [area(8 * i, 8) for i in range(NRAW)]
        xg = area(48, 4)
        ybuf = area(52, 4)
        gate_h = [area(56 + 8 * i, 2) for i in range(2)]
        sg_h = [area(58 + 8 * i, 2) for i in range(2)]
        up_h = [area(60 + 8 * i, 2) for i in range(2)]
        act_h = [area(62 + 8 * i, 2) for i in range(2)]

        wh = [parts_at(f"wh{i}", 72 + 8 * i, 8) if i < 3 else parts_at(f"wh{i}", 112, 8) for i in range(NSP)]
        wl = [parts_at(f"wl{i}", 120 + 8 * i, 8) for i in range(NSP)]
        xgh, xgl = (tiles(parts_at(n, 152 + 4 * i, 4), KD) for i, n in enumerate(("xgh", "xgl")))
        hTh, hTl = (tiles(parts_at(n, 160 + 4 * i, 4), KD) for i, n in enumerate(("hTh", "hTl")))
        NYG = 4
        yg = [area(4 * i, 4) for i in range(NYG)]
        gfin = area(32, 4)
        outb = [area(16 + 4 * i, 4) for i in range(NT)]

        srow = [[work[:, (2 * i + c) * 512:(2 * i + c + 1) * 512] for c in range(2)] for i in range(3)]
        cbuf = tiles(work[:, 0:4 * KB], NT)
        topacc = [None] + [work[:, 0:256], work[:, 256:640], work[:, 640:1152]]
        gffn = area(76, 4)
        PT = [ptb[:, i * 512:(i + 1) * 512] for i in range(2)]
        sparse_PT = [srow[i][1] for i in range(3)]
        merge_tmp = [ptb[:, i * 512:(i + 1) * 512] for i in range(2)]
        lead_tmp = [nc.alloc_sbuf_tensor_at(f"lead_tmp{i}", [P, 512], F32R, offset=arena_at + (192 + 2 * i) * 1024)[:, :] for i in range(2)]
        topmask = [None] + [sb(f"topmask{t}", (t + 1) * P, BF16) for t in range(1, NT)]
        bparts = sb("bparts", 3 * D, BF16, 96)
        con = sb("con", C_LEN)
        ident = con[:, C_ID:C_ID + P]
        identb = sb("identb", P, BF16)
        zeros = area(56, 8)
        ikT = area(52, 2)
        iw = tiles(area(54, 1)[:, 0:NT * NI], NT)
        gcols = sb("gcols", KD + KL + 1)
        lamv = area(67, 1)
        lamj = area(68, 1)[:, 0:DI]
        lam = sb("lam", 4)
        tabx = area(69, 1)[0:NB + 1, 0:2 * NH]
        oh33 = area(64, 3)[0:NB + 1, 0:RLEN]
        rvec = area(108, 4)[0:2 * NH, 0:RLEN]
        stat = sb("stat", 64)
        v8 = sb("v8", 8)
        row_max = [sb(f"rowmax{i}", 4) for i in range(2)]
        row_sum = [sb(f"rowsum{i}", 2) for i in range(3)]
        ratio = [sb(f"ratio{i}", 4) for i in range(4)]
        orow = [cT[:, i, :] for i in range(2)]
        ojunk = sb("ojunk", P)
        late = [64 * KB]

        def after(cols, parts=P):
            late[0] += cols
            return arena[0:parts, late[0] - cols:late[0]]

        logit, chosen = tiles(after(NT * NE), NT), tiles(after(NT * NE), NT)
        top_v, top_f = tiles(after(NT * 8), NT), tiles(after(NT * 8), NT)
        pick = after(NT * NK * NE).rearrange("p (t k e) -> p t k e", t=NT, k=NK)
        ptmp = after(NK * NE).rearrange("p (k e) -> p k e", k=NK)
        extra, before = after(P, NE), after(16, NE)
        extra2 = arena[0:NE, late[0] - P - 16 - NK * NE:late[0] - P - 16]
        xbase, over, slot_e, vneg = after(NE), after(NE), after(NE), after(NT)
        slot_f = tiles(after(NT * NK), NT)
        brt = after(NE)
        rcon = after(C_RLEN)
        tri = rcon[:, C_TRI:C_TRI + P]
        ones = rcon[:, C_ONE:C_ONE + P]
        wr = tiles(after(KD * NE), KD)
        top_i = tiles(typed("top_i", 158, NT * 8, U32), NT)
        evals = area(168, 1)[:, 0:NE + 16]
        evals_i = typed("evals_i", 169, NE + 16, I32)
        nextra_i = typed("nextra_i", 170, 2, I32)
        ids = typed("ids", 171, 2, I32)
        ohe = typed("ohe", 172, P, BF16)[0:96, :]
        slot_i = tiles(typed("slot_i", 173, NT * NK, I32), NT)
        gate = tiles(sb("gate", NT * NK)[:, :], NT)
        gsum = sb("gsum", NT)
        tok_i = sb("tok_i", NT, I32)
        carrier = sb("carrier", 2, F32, 1)

        psum = ctx.enter_context(nc.psum_tensor("psum", [P, 8 * 512], F32))
        bank = [psum[:, 512 * i:512 * (i + 1)] for i in range(8)]

        rv_d = dram("rv_d", (2 * NH, RLEN))
        skew_d = dram("skew_d", (2 * NH, P, RLEN))
        hn_d = dram("hn_d", (S, D))
        rowtok_d = dram("rowtok_d", (NBLK * P, 1), I32)
        y_d = dram("y_d", ((NE + NX) * P, D))
        rest = y_d[NE * P:, :].rearrange("(p r) d -> p (r d)", p=P)

        full = [sem(f"bank{i}_full") for i in range(8)]
        free = [sem(f"bank{i}_free") for i in range(8)]
        x_in = [sem(f"x{t}_in") for t in range(NT)]
        x_in2, const_in, gain_in, small_in, wr_in, gbc_in = (sem(n) for n in ("x_in2", "const_in", "gain_in", "small_in", "wr_in", "gbc_in"))
        mask_row, bsplit_in, bparts_ready = sem("mask_row"), sem("bsplit_in"), sem("bparts_ready")
        wring_in = [sem(f"wring{i}_in") for i in range(NW)]
        act_step, dve_step, pool_step = sem("act_step"), sem("dve_step"), sem("pool_step")
        x_sq, x_norm, c_sq, c_norm = sem("x_sq"), sem("x_norm"), sem("c_sq"), sem("c_norm")
        identb_ready, tok_ready = sem("identb_ready"), sem("tok_ready")
        y_zero = sem("y_zero")
        skew_out, carried = sem("skew_out"), sem("carried")
        rvec_out, strip_in, strip2_in = sem("rvec_out"), sem("strip_in"), sem("strip2_in")
        relu_used, mask_ready = sem("relu_used"), sem("mask_ready")
        lam_dot, lam_exp = sem("lam_dot"), sem("lam_exp")
        score_ready, exp_ready, a_ready, y_ready = sem("score_ready"), sem("exp_ready"), sem("a_ready"), sem("y_ready")
        sscore_ready, sexp_ready, p_ready = sem("sscore_ready"), sem("sexp_ready"), sem("p_ready")
        early_h_ready, early_l_ready, early_used = sem("early_h_ready"), sem("early_l_ready"), sem("early_used")
        xeh_ready, xel_ready = sem("xeh_ready"), sem("xel_ready")
        late_in = [sem(f"late{i}_in") for i in range(2)]
        piece_h_ready, piece_l_ready, piece_used = sem("piece_h_ready"), sem("piece_l_ready"), sem("piece_used")
        lead_tmp_ready, rest_ready, lead_ready = sem("lead_tmp_ready"), sem("rest_ready"), sem("lead_ready")
        mh_ready, ml_ready = sem("mh_ready"), sem("ml_ready")
        merge_ready, h_sq, hn_ready = sem("merge_ready"), sem("h_sq"), sem("hn_ready")
        hn_out = [sem(f"hn_out{i}") for i in range(2)]
        top_ready, chosen_ready, gate_exp = (
            sem(n) for n in ("top_ready", "chosen_ready", "gate_exp"))
        slots_ready, evals_ready, zero_out, scat_out = sem("slots_ready"), sem("evals_ready"), sem("zero_out"), sem("scat_out")
        raw_in = [sem(f"raw{i}_in") for i in range(NRAW)]
        wh_ready, wl_ready, hTh_ready, xgh_ready = sem("wh_ready"), sem("wl_ready"), sem("hTh_ready"), sem("xgh_ready")
        e_used, ids_in, xg_in, ohe_ready = sem("e_used"), sem("ids_in"), sem("xg_in"), sem("ohe_ready")
        g_ready, sg_ready, glu_ready, act_ready = sem("g_ready"), sem("sg_ready"), sem("glu_ready"), sem("act_ready")
        y_out = sem("y_out")
        yg_in = [sem(f"yg{i}_in") for i in range(NYG)]
        yg_used, o_sq, o_ready, out_done = sem("yg_used"), sem("o_sq"), sem("o_ready"), sem("out_done")

        CH = ["ckv", "iq0", "iq1", "ikw", "dq0", "dq1", "dk0", "dk1", "dv0", "dv1", "ukv", "sq0", "sq1"]
        LATE = [f"{n}{j}" for j in range(2) for n in ("ga", "bd", "gb", "bs")] + ["wo0", "wo1"]
        EARLY = ["iq0", "iq1", "dq0", "dq1", "dk0", "dk1", "dv0", "dv1"]
        NEP = KD * len(EARLY)
        NQP = KD * 2
        NXP = NQP + 2 * NI * (NT - 1) // 3
        AHEAD = ERING - 1
        SPLIT_AT = ["ga0", "bd0", "bs0"]
        w_in_v = a["w_in"][0].rearrange("(k p) n -> p k n", p=P)

        def chunk_view(name, cols=512):
            return wring[CH.index(name) % NW][:, 0:KD * cols].rearrange("p (k n) -> p k n", k=KD)

        uses, count = {}, [0] * 8

        def plan(key, b):
            uses[key] = (b, count[b])
            count[b] += 1

        n_group = [0]

        def plan_groups(keys):
            for k in keys:
                plan(k, n_group[0] % 2)
                n_group[0] += 1

        def early_key(name, i):
            j = int(name[2])
            return ("dv", j, i) if name[:2] == "dv" else (name[:2], NT * j + i)

        plan("rv0", 6)
        plan("rv1", 7)
        for k in range(KD):
            plan(("xT", k), 2 + k % 2)
        G_CKV = [("ckv", t) for t in range(NT)]
        G_IQ = [("iq", j) for j in range(NH)]
        G_IK = [("ik", 0)]
        G_IW = [("iw", t) for t in range(NT)]
        G_DQ = [("dq", j) for j in range(NH)]
        G_DK = [("dk", j) for j in range(NH)]
        G_DV = [("dv", h, t) for h in range(2) for t in range(NT)]
        G_UK = [("uk", h) for h in range(NH)]
        G_UV = [("uv", h, t) for h in range(2) for t in range(NT)]
        G_SQ = [("sq", j) for j in range(NH)]
        plan_groups(G_CKV)
        for i in range(NT):
            plan(early_key("iq0", i), NT + i)
        for i in range(NT):
            plan(early_key("iq1", i), i)
        plan_groups(G_IK + G_IW)
        for k in range(KL):
            plan(("cT", k), 6 + k)
        INDEX = [(t, h) for t in range(1, NT) for h in range(NI)]
        for m, key in enumerate(INDEX):
            plan(("ix",) + key, 2 + m % 2)
        for name in EARLY[2:]:
            for i in range(NT):
                plan(early_key(name, i), i if name == "dv0" else NT + i)
        plan_groups(G_UK + G_UV)
        UNITS = [(h, t) for h in range(NH) for t in range(NT)]
        NU = len(UNITS)

        def sq_part(u):
            v = u - NT - 1
            return (v // NT, v % NT) if 0 <= v < NU else None

        for u in range(NU + 6):
            if u < NU:
                for c in range(2):
                    plan(("s", u, c), 2 + 2 * (u % 2) + c)
            if 0 <= u - 2 < NU:
                plan(("pt", u - 2), 6)
            if 0 <= u - 3 < NU:
                plan(("o", u - 3), (u - 3) % 2)
            if 0 <= u - 5 < NU and UNITS[u - 5][1] == NT - 1:
                plan(("yt", UNITS[u - 5][0]), 6)
            if sq_part(u) and sq_part(u)[1] == 0:
                plan(("sq", sq_part(u)[0]), 7)
        for u in range(NU + 4):
            if u < NU:
                plan(("ss", u), 2 + u % 2)
            if 0 <= u - 2 < NU:
                plan(("spt", u - 2), 6 + u % 2)
            if 0 <= u - 4 < NU:
                plan(("so", u - 4), 4 + (u - 4) % 2)
        for m, name in enumerate(LATE):
            for i in range(NT):
                plan((name[:2], int(name[2]), i), NT * (m % 2) + i)
        for t in range(NT):
            plan(("hT", t, 0), 2)
            plan(("hT", t, 1), 3)
            plan(("lg", t), 4)
        for t in range(NT):
            plan(("rank", t), 5 + t % 2)
        plan("cntT", 7)
        plan("xb", 4)
        plan("xeT", 7)
        plan("xe", 4)
        base_use = list(count)
        LAST = {"ckv": G_CKV[-1], "iq0": G_IQ[3], "iq1": G_IQ[7], "ikw": G_IW[-1], "ukv": G_UV[-1]}
        for j in range(2):
            LAST.update({f"dq{j}": G_DQ[4 * j + 3], f"dk{j}": G_DK[4 * j + 3], f"sq{j}": G_SQ[4 * j + 3],
                         f"dv{j}": G_DV[4 * j + 3], f"wo{j}": ("wo", j, NT - 1)})
            LAST.update({f"{n}{j}": (n, j, NT - 1) for n in ("ga", "bd", "gb", "bs")})

        def filled(eng, key):
            b, n = uses[key]
            eng.wait_ge(full[b], n + 1)
            return bank[b]

        def taken(eng, key):
            b, n = uses[key]
            eng.wait_ge(free[b], n + 1)

        def free_of(key):
            return free[uses[key][0]]

        def chunk_count(name):
            n = CH.index(name)
            return sum(16 * {"ukv": 4, "ikw": 2}.get(CH[m], 1) for m in range(n % NW, n + 1, NW))

        def early_done(eng, p):
            if p % KD == KD - 1:
                filled(eng, early_key(EARLY[p // KD], NT - 1))
            else:
                eng.wait_ge(early_used, (KD - 1) * (p // KD) + p % KD + 1)

        def early_h(p):
            return ring_h[p >= NQP][p % ERING]

        def early_l(p):
            return ring_l[p >= NQP][p % ERING]

        def piece_done(eng, m, q):
            if q == PIECES - 1:
                filled(eng, (LATE[m][:2], int(LATE[m][2]), NT - 1))
            else:
                eng.wait_ge(piece_used, (PIECES - 1) * m + q + 1)

        def ge(eng, s, value):
            if not isinstance(value, int) or value > 0:
                eng.wait_ge(s, value)

        def all_blocks(eng, one):
            one(0)
            with eng.Fori(1, NE) as i:
                one(i)
            eng.wait_ge(evals_ready, 2)
            n_extra = eng.value_load(nextra_i[0:1, 0:1], min_val=0, max_val=NX)
            with eng.If(n_extra > 0):
                with eng.Fori(0, n_extra) as j:
                    one(j + NE)
            return n_extra


        block = ctx.enter_context(nc.Block())

        @block.sync
        def _(sp):
            x_v = a["x"][0].rearrange("(t p) d -> p t d", p=P)
            for t in range(NT):
                sp.dma_start(xbuf[:, t, :], x_v[:, t, :]).then_inc(x_in[t], 16)
            for n, name in enumerate(CH):
                if n >= NW:
                    if CH[n - NW] in EARLY:
                        sp.wait_ge(early_l_ready, KD * (EARLY.index(CH[n - NW]) + 1))
                    else:
                        filled(sp, LAST[CH[n - NW]])
                done = wring_in[n % NW]
                if name == "ukv":
                    slot = wring[n % NW].rearrange("p (u k h d) -> p u k h d", u=2, k=KL, h=NH)
                    for u, w in enumerate(("w_uk", "w_uv")):
                        for k in range(KL):
                            sp.dma_start(slot[:, u, k], a[w][0].rearrange("h (k p) d -> k p h d", p=P)[k]).then_inc(done, 16)
                elif name == "ikw":
                    v = chunk_view("ikw", 2 * DI + NI)
                    c0 = IN_COLS["ik"]
                    sp.dma_start(v[:, :, 0:DI], w_in_v[:, :, c0:c0 + DI]).then_inc(done, 16)
                    sp.dma_start(v[:, :, DI:2 * DI + NI], w_in_v[:, :, c0:c0 + DI + NI]).then_inc(done, 16)
                else:
                    cols = LAT if name == "ckv" else 512
                    j = 0 if name == "ckv" else int(name[-1])
                    kind = name if name == "ckv" else name[:-1]
                    c0 = IN_COLS[kind] + 512 * j
                    sp.dma_start(chunk_view(name, cols), w_in_v[:, :, c0:c0 + cols]).then_inc(done, 16)
            for m, name in enumerate(LATE):
                if m < 2:
                    filled(sp, LAST[("ukv", "sq1")[m]])
                else:
                    sp.wait_ge(piece_l_ready, PIECES * (m - 1))
                c0 = 512 * int(name[2])
                if name[:2] in IN_COLS:
                    src = w_in_v[:, :, IN_COLS[name[:2]] + c0:IN_COLS[name[:2]] + c0 + 512]
                else:
                    w = {"bd": "w_branch_diff", "bs": "w_branch_dsa", "wo": "w_out"}[name[:2]]
                    src = a[w][0].rearrange("(k p) n -> p k n", p=P)[:, :, c0:c0 + 512]
                sp.dma_start(tiles(late_ring[m % 2], KD), src).then_inc(late_in[m % 2], 16)
            filled(sp, LAST["bd1"])
            sp.dma_start(hbuf, x_v).then_inc(x_in2, 16)

            filled(sp, LAST["bs1"])
            gu_v = a["w_gate_up"][0].rearrange("e (c k p) n -> e c p k n", p=P, k=2)
            dn_v = a["w_down"][0].rearrange("e (c k p) n -> e c p k n", p=P, k=2)

            def load_expert(i, further=False):
                e = sp.value_load(evals_i[0:1, bass.ds(i, 1)], min_val=0, max_val=NE - 1) if further else i
                for c in range(NCH):
                    ge(sp, wl_ready, i * NCH + (c + 1 - NRAW))
                    src = gu_v[e, c % 4][:, :, (c // 4) * D:(c // 4 + 1) * D] if c < 8 else dn_v[e, c - 8]
                    sp.dma_start(raw[c % NRAW].rearrange("p (k n) -> p k n", k=2), src).then_inc(raw_in[c % NRAW], 16)

            load_expert(0)
            with sp.Fori(1, NE) as i:
                load_expert(i)
            sp.wait_ge(evals_ready, 2)
            n_extra = sp.value_load(nextra_i[0:1, 0:1], min_val=0, max_val=NX)
            with sp.If(n_extra > 0):
                with sp.Fori(0, n_extra) as j:
                    load_expert(j + NE, further=True)
            for t in range(NT):
                sp.wait_ge(o_ready, t + 1)
                sp.dma_start(out[0, t * P:(t + 1) * P, :], outb[t]).then_inc(out_done, 16)
            sp.wait_ge(out_done, 16 * NT)

        @block.gpsimd
        def _(pool):
            for v, c0, n in (("norm_attn_g", 0, KD), ("kv_norm_g", KD, KL), ("diff_subln_g", KD + KL, 1)):
                with nc.allow_non_contiguous_dma("gains, one per partition"):
                    pool.dma_start(gcols[:, c0:c0 + n], a[v][0].rearrange("(k p) -> p k", p=P)).then_inc(gain_in, 16)
            pool.memset(zero_i[:, :], 0).then_inc(pool_step, 1)
            pool.dma_start(tabx[0:NB, :], a["rel_bias"]).then_inc(small_in, 16)
            pool.dma_start(oh33[:, :], a["oh33"]).then_inc(small_in, 16)
            for i, v in enumerate(("lam_q1", "lam_k1", "lam_q2", "lam_k2")):
                pool.dma_start(lamv[:, i * DI:(i + 1) * DI], a[v].broadcast_to([P, DI])).then_inc(small_in, 16)
            for r in range(3):
                pool.dma_start(bsplit[NE * r:NE * (r + 1), 0:2 * D], a["b_gate_up"][0]).then_inc(bsplit_in, 16)
                pool.dma_start(bsplit[NE * r:NE * (r + 1), 2 * D:3 * D], a["b_down"][0]).then_inc(bsplit_in, 16)
            pool.wait_ge(pool_step, 1)
            pool.dma_start(rowtok_d.rearrange("(p b) o -> p (b o)", p=P), zero_i[:, :]).then_inc(zero_out, 16)
            pool.wait_ge(const_in, 16)
            pool.tensor_copy(tok_i[:, :], con[:, C_TOK:C_TOK + NT]).then_inc(tok_ready, 1)

            pool.wait_ge(bsplit_in, 16 * 6)
            n = 1
            pool.tensor_copy(bparts[:, :], bsplit[0:96, :]).then_inc(pool_step, 1)
            for r in (1, 2):
                rows = slice(NE * r, NE * (r + 1))
                for q in range(r):
                    n += 1
                    pool.wait_ge(pool_step, n)
                    pool.tensor_tensor(bsplit[rows, :], bsplit[rows, :], bparts[rows, :], ALU.subtract).then_inc(pool_step, 1)
                    n += 1
                    pool.wait_ge(pool_step, n)
                    pool.tensor_copy(bparts[rows, :], bsplit[rows, :]).then_inc(bparts_ready if (r, q) == (2, 1) else pool_step, 1)

            pool.wait_ge(mask_row, 3)
            taken(pool, "rv0")
            taken(pool, "rv1")
            pool.dma_start(rv_d, rvec[:, :]).then_inc(rvec_out, 16)
            pool.wait_ge(rvec_out, 16)

            pool.dma_start(skew_d, rv_d.unsqueeze(1).broadcast_to([2 * NH, P, RLEN])).then_inc(skew_out, 16)
            pool.wait_ge(skew_out, 16)

            def load_strips(h0, done):
                src = bass.AP(tensor=skew_d.tensor, offset=h0 * P * RLEN + P - 1, ap=[[RLEN - 1, P], [P * RLEN, NH], [1, S]])
                pool.dma_start(strips, src).then_inc(done, 16)

            for r in range(2, NX, 2):
                n = min(2, NX - r) * D
                pool.dma_start(rest[:, r * D:r * D + n], zeros[:, 0:n]).then_inc(y_zero, 16)
            filled(pool, G_DV[-1])
            load_strips(0, strip_in)
            pool.wait_ge(score_ready, NU)
            load_strips(NH, strip2_in)
            filled(pool, LAST["bs1"])
            pool.dma_start(gffn, a["norm_ffn_g"].broadcast_to([P, D])).then_inc(gbc_in, 16)
            pool.dma_start(wr, a["w_router"][0].rearrange("(k p) e -> p k e", p=P)).then_inc(wr_in, 16)
            pool.dma_start(brt[:, :], a["b_router"].broadcast_to([P, NE])).then_inc(wr_in, 16)
            pool.dma_start(rcon[:, :], a["consts"][:, C_LEN:C_LEN + C_RLEN]).then_inc(wr_in, 16)

            for t in range(NT):
                pool.wait_ge(hn_ready, t + 1)
                pool.dma_start(hn_d[t * P:(t + 1) * P, :], hn[:, t % 2, :]).then_inc(hn_out[t % 2], 16)
            for r in range(2):
                pool.wait_ge(hn_out[r], 16 * NT // 2)
            pool.wait_ge(zero_out, 16)
            pool.wait_ge(tok_ready, 1)
            for t in range(NT):
                pool.wait_ge(slots_ready, t + 1)
                for k in range(NK):
                    pool.indirect_dma_start(rowtok_d, bass.IndirectOffsetOnAxis(ap=slot_i[:, t, k:k + 1], axis=0),
                                            tok_i[:, t:t + 1], None).then_inc(scat_out, 16)
            pool.wait_ge(scat_out, 16 * NT * NK)

            def settle():
                pool.tensor_tensor(carrier[:, 1:2], carrier[:, 0:1], carrier[:, 0:1], ALU.add).then_inc(carried, 1)

            def gather_block(i, first=False):
                if not first:
                    pool.wait_ge(xg_in, i * 16)
                pool.dma_start(ids[:, 0:1], rowtok_d[bass.ds(i * P, P), :]).then_inc(ids_in, 16)
                pool.wait_ge(ids_in, i * 16 + 16)
                if not first:
                    pool.wait_ge(carried, i)
                    pool.wait_ge(full[7], i * 2 + base_use[7])
                settle()
                pool.indirect_dma_start(xg, None, hn_d, bass.IndirectOffsetOnAxis(ap=ids[:, 0:1], axis=0)).then_inc(xg_in, 16)

            gather_block(0, first=True)
            with pool.Fori(1, NE + 1) as i:
                gather_block(i)
            pool.wait_ge(evals_ready, 2)
            n_extra = pool.value_load(nextra_i[0:1, 0:1], min_val=0, max_val=NX)
            with pool.If(n_extra > 0):
                with pool.Fori(0, n_extra) as j:
                    gather_block(j + (NE + 1))
            pool.wait_ge(xg_in, n_extra * 16 + 16 * (NE + 1))

            pool.wait_ge(carried, n_extra + NE + 1)
            pool.wait_ge(y_out, n_extra * 16 + 16 * (NE + 1))
            settle()
            for m in range(NT * NK):
                t, k = m // NK, m % NK
                if m >= NYG:
                    pool.wait_ge(yg_used, m - NYG + 1)
                pool.indirect_dma_start(yg[m % NYG], None, y_d,
                                        bass.IndirectOffsetOnAxis(ap=slot_i[:, t, k:k + 1], axis=0)).then_inc(yg_in[m % NYG], 16)
                if m == NK - 1:
                    pool.dma_start(gfin, a["norm_final_g"].rearrange("(o d) -> o d", o=1).broadcast_to([P, D])).then_inc(gbc_in, 16)

        @block.tensor
        def _(pe):
            def empty(key):
                b, n = uses[key]
                if n:
                    pe.wait_ge(free[b], n)
                return bank[b]

            def full_of(key):
                return full[uses[key][0]]

            def chunk_in(name):
                n = CH.index(name)
                pe.wait_ge(wring_in[n % NW], chunk_count(name))

            def by_token(keys, chunk, src, cols=512, c0=0, width=512):
                chunk_in(chunk)
                w = chunk_view(chunk, width)
                for t, key in enumerate(keys):
                    o = empty(key)
                    for k in range(KD):
                        ins = pe.matmul(o[:, 0:cols], src[:, k, t * P:(t + 1) * P], w[:, k, c0:c0 + cols], start=(k == 0), stop=(k == KD - 1))
                    ins.then_inc(full_of(key), 1)

            pe.wait_ge(const_in, 16)
            pe.wait_ge(x_norm, NT)
            for k in range(KD):
                o = empty(("xT", k))
                for t in range(NT):
                    ins = pe.transpose(o[:, t * P:(t + 1) * P], xbuf[:, t, k * P:(k + 1) * P], ident)
                ins.then_inc(full_of(("xT", k)), 1)

            for k in range(KD - 2, KD):
                taken(pe, ("xT", k))
            by_token(G_CKV, "ckv", xnT, cols=LAT, width=LAT)
            pe.wait_ge(small_in, 16 * 6)
            pe.wait_ge(mask_row, 1)
            pe.matmul(empty("rv0")[0:2 * NH, :], tabx[:, :], oh33[:, 0:512], start=True, stop=True).then_inc(full_of("rv0"), 1)
            pe.matmul(empty("rv1")[0:2 * NH, 0:RLEN - 512], tabx[:, :], oh33[:, 512:RLEN], start=True, stop=True).then_inc(full_of("rv1"), 1)
            for k in range(KD):
                pe.wait_ge(xeh_ready, k + 1)
                pe.wait_ge(xel_ready, k + 1)

            def early_products(p):
                name, k = EARLY[p // KD], p % KD
                keys = [early_key(name, i) for i in range(NT)]
                o = [empty(key) if k == 0 else bank[uses[key][0]] for key in keys]
                pe.wait_ge(early_l_ready, p + 1)
                wh_, wl_ = early_h(p), early_l(p)
                for i, key in enumerate(keys):
                    cols = slice(i * P, (i + 1) * P)
                    for w, x in ((wh_, xe_h), (wh_, xe_l), (wl_, xe_h)):
                        lhs, rhs = (x[:, k, cols], w[:, :]) if name[:2] == "dv" else (w[:, cols], x[:, k, :])
                        ins = pe.matmul(o[i], lhs, rhs, start=(k == 0 and w is wh_ and x is xe_h), stop=(k == KD - 1 and w is wl_))
                    if k == KD - 1:
                        ins.then_inc(full_of(key), 1)
                    elif i == NT - 1:
                        ins.then_inc(early_used, 1)

            for p in range(NQP):
                early_products(p)
            chunk_in("ikw")
            w = chunk_view("ikw", 2 * DI + NI)
            o = empty(G_IK[0])
            for k in range(KD):
                ins = pe.matmul(o[:, :], w[:, k, 0:2 * DI], xnT[:, k, :], start=(k == 0), stop=(k == KD - 1))
            ins.then_inc(full_of(G_IK[0]), 1)
            by_token(G_IW, "ikw", xnT, cols=NI, c0=2 * DI, width=2 * DI + NI)

            pe.wait_ge(c_norm, NT)
            for k in range(KL):
                o = empty(("cT", k))
                for t in range(NT):
                    ins = pe.transpose(o[:, t * P:(t + 1) * P], cbuf[:, t, k * P:(k + 1) * P], ident)
                ins.then_inc(full_of(("cT", k)), 1)

            taken(pe, G_IW[-1])
            taken(pe, G_IW[-2])
            for m, (t, h) in enumerate(INDEX):
                if m % 3 < 2:
                    early_products(NQP + 2 * (m // 3) + m % 3)
                o = empty(("ix", t, h))
                half = slice((h % 2) * DI, (h % 2 + 1) * DI)
                n = (t + 1) * P
                pe.matmul(o[:, 0:n], iqT[half, h // 2, t * P:(t + 1) * P], ikT[half, 0:n],
                          start=True, stop=True).then_inc(full_of(("ix", t, h)), 1)

            for p in range(NXP, NEP):
                early_products(p)
            chunk_in("ukv")
            ukv = wring[CH.index("ukv") % NW].rearrange("p (u k n) -> p u k n", u=2, k=KL)
            for k in range(KL):
                taken(pe, ("cT", k))
            for key in G_UK:
                o = empty(key)
                for k in range(KL):
                    ins = pe.matmul(o[:, :], ukv[:, 0, k, key[1] * P:(key[1] + 1) * P], cT[:, k, :], start=(k == 0), stop=(k == KL - 1))
                ins.then_inc(full_of(key), 1)
            for key in G_UV:
                _, j, t = key
                o = empty(key)
                for k in range(KL):
                    ins = pe.matmul(o[:, :], cT[:, k, t * P:(t + 1) * P], ukv[:, 1, k, j * 512:(j + 1) * 512], start=(k == 0), stop=(k == KL - 1))
                ins.then_inc(full_of(key), 1)

            taken(pe, G_UV[-1])
            taken(pe, G_UV[-2])
            for u in range(NU + 6):
                if u < NU:
                    h, t = UNITS[u]
                    n = (t + 1) * P
                    for c in range(2):
                        o = empty(("s", u, c))
                        half = slice(c * 64, c * 64 + 64)
                        pe.matmul(o[:, 0:n], dqT[half, h, t * P:(t + 1) * P], dkT[half, h, 0:n],
                                  start=True, stop=True).then_inc(full_of(("s", u, c)), 1)
                if 0 <= u - 2 < NU:
                    v = u - 2
                    h, t = UNITS[v]
                    pe.wait_ge(a_ready, v + 1)
                    o = empty(("pt", v))
                    for k in range(t + 1):
                        ins = pe.transpose(o[:, k * P:(k + 1) * P], srow[v % 3][0][:, k * P:(k + 1) * P], ident)
                    ins.then_inc(full_of(("pt", v)), 1)
                if 0 <= u - 3 < NU:
                    v = u - 3
                    h, t = UNITS[v]
                    taken(pe, ("pt", v))
                    o = empty(("o", v))
                    for k in range(t + 1):
                        ins = pe.matmul(o[:, 0:P], PT[v % 2][:, k * P:(k + 1) * P], dv[:, k, h * P:(h + 1) * P], start=(k == 0), stop=(k == t))
                    ins.then_inc(full_of(("o", v)), 1)
                if 0 <= u - 5 < NU and UNITS[u - 5][1] == NT - 1:
                    h = UNITS[u - 5][0]
                    pe.wait_ge(y_ready, NT * (h + 1))
                    o = empty(("yt", h))
                    for t in range(NT):
                        ins = pe.transpose(o[:, t * P:(t + 1) * P], orow[h % 2][:, t * P:(t + 1) * P], ident)
                    ins.then_inc(full_of(("yt", h)), 1)
                if sq_part(u):
                    h, q = sq_part(u)
                    chunk_in(f"sq{h // 4}")
                    w = chunk_view(f"sq{h // 4}")
                    o = empty(("sq", h)) if q == 0 else bank[7]
                    for k in range(2 * q, 2 * q + 2):
                        ins = pe.matmul(o[:, :], w[:, k, h % 4 * P:(h % 4 + 1) * P], xnT[:, k, :], start=(k == 0), stop=(k == KD - 1))
                    if q == NT - 1:
                        ins.then_inc(full_of(("sq", h)), 1)

            taken(pe, G_SQ[-1])
            taken(pe, G_SQ[-2])
            pe.wait_ge(identb_ready, 1)
            pe.wait_ge(mask_ready, NT - 1)
            for u in range(NU + 4):
                if u < NU:
                    h, t = UNITS[u]
                    n = (t + 1) * P
                    o = empty(("ss", u))
                    ins = pe.matmul(o[:, 0:n], sqT[:, h, t * P:(t + 1) * P], khT[:, h, 0:n], start=True, stop=(t == 0))
                    if t:
                        ins = pe.matmul(o[:, 0:n], identb[:, :], topmask[t][:, :], start=False, stop=True)
                    ins.then_inc(full_of(("ss", u)), 1)
                if 0 <= u - 2 < NU:
                    v = u - 2
                    h, t = UNITS[v]
                    pe.wait_ge(p_ready, v + 1)
                    o = empty(("spt", v))
                    for k in range(t + 1):
                        ins = pe.transpose(o[:, k * P:(k + 1) * P], srow[v % 3][0][:, k * P:(k + 1) * P], ident)
                    ins.then_inc(full_of(("spt", v)), 1)
                if 0 <= u - 4 < NU:
                    v = u - 4
                    h, t = UNITS[v]
                    taken(pe, ("spt", v))
                    o = empty(("so", v))
                    for k in range(t + 1):
                        ins = pe.matmul(o[:, 0:P], vh[:, k, h * P:(h + 1) * P], sparse_PT[v % 3][:, k * P:(k + 1) * P], start=(k == 0), stop=(k == t))
                    ins.then_inc(full_of(("so", v)), 1)

            for v in (NU - 2, NU - 1):
                taken(pe, ("so", v))
            taken(pe, ("yt", NH - 1))
            for m, name in enumerate(LATE):
                kind, j = name[:2], int(name[2])
                xh, xl = {"ga": (xn_h, xn_l), "gb": (xn_h, xn_l), "bd": (yd_h, yd_l), "bs": (ys_h, ys_l), "wo": (m_h, m_l)}[kind]
                o = [empty((kind, j, i)) for i in range(NT)]
                for q in range(PIECES):
                    pe.wait_ge(piece_l_ready, PIECES * m + q + 1)
                    h, l = piece_h[q], piece_l[q]
                    for k2 in range(PK):
                        k = PK * q + k2
                        if kind == "wo":
                            pe.wait_ge(mh_ready, k + 1)
                            pe.wait_ge(ml_ready, k + 1)
                        elif name in SPLIT_AT:
                            pe.wait_ge(lead_ready, KD * SPLIT_AT.index(name) + k + 1)
                        for i in range(NT):
                            cols = slice(i * P, (i + 1) * P)
                            for w, x in ((h, xh), (h, xl), (l, xh)):
                                lhs, rhs = (x[:, k, cols], w[:, k2, :]) if kind == "wo" else (w[:, k2, cols], x[:, k, :])
                                ins = pe.matmul(o[i], lhs, rhs, start=(k == 0 and w is h and x is xh), stop=(k == KD - 1 and w is l))
                            if k == KD - 1:
                                ins.then_inc(full_of((kind, j, i)), 1)
                            elif k2 == PK - 1 and i == NT - 1:
                                ins.then_inc(piece_used, 1)

            pe.wait_ge(wr_in, 48)
            for t in range(NT):
                pe.wait_ge(hn_ready, t + 1)
                for g in range(2):
                    o = empty(("hT", t, g))
                    for k in range(4):
                        c = (4 * g + k) * P
                        ins = pe.transpose(o[:, k * P:(k + 1) * P], hn[:, t % 2, c:c + P], ident)
                    ins.then_inc(full_of(("hT", t, g)), 1)
                for g in range(2):
                    taken(pe, ("hT", t, g))
                o = empty(("lg", t))
                for k in range(KD):
                    ins = pe.matmul(o[:, 0:NE], hnT[:, t % 2, k * P:(k + 1) * P], wr[:, k, :], start=(k == 0), stop=(k == KD - 1))
                ins.then_inc(full_of(("lg", t)), 1)

            pe.wait_ge(chosen_ready, NT)
            c = empty("cntT")
            for q in range(NT):
                ins = pe.matmul(c[0:NE, 0:P], chosen[:, q, :], ones, start=(q == 0), stop=(q == NT - 1))
            ins.then_inc(full_of("cntT"), 1)

            def rank(t):
                o = empty(("rank", t))
                for q in range(t + 1):
                    ins = pe.matmul(o[:, 0:NE], tri if q == t else ones, chosen[:, q, :], start=(q == 0), stop=(q == t))
                ins.then_inc(full_of(("rank", t)), 1)

            rank(0)
            rank(1)
            taken(pe, "cntT")
            pe.matmul(empty("xb")[:, 0:NE], extra[:, :], rcon[0:NE, C_SU:C_SU + NE], start=True, stop=True).then_inc(full_of("xb"), 1)
            pe.matmul(empty("xeT")[0:NE, 0:P], rcon[0:NE, C_SUI:C_SUI + NE], extra[:, :], start=True, stop=True).then_inc(full_of("xeT"), 1)
            taken(pe, "xeT")
            o = empty("xe")
            pe.matmul(o[:, 0:16], ones[0:NE, :], before[:, :], start=True, stop=True)
            pe.matmul(o[:, 16:17], ones[0:NE, :], extra[:, 0:1], start=True, stop=True).then_inc(full_of("xe"), 1)
            rank(2)
            rank(3)

            pe.wait_ge(bparts_ready, 1)
            for b in (1, 3, 5):
                pe.wait_ge(free[b], base_use[b])

            def turn_rows(i, g):
                if g == 0:
                    pe.wait_ge(xg_in, i * 16 + 16)
                pe.wait_ge(free[7], i * 2 + (base_use[7] + g))
                for k in range(4):
                    c = (4 * g + k) * P
                    ins = pe.transpose(bank[7][:, k * P:(k + 1) * P], xg[:, c:c + P], ident)
                ins.then_inc(full[7], 1)

            def turn_hidden(i, half):
                pe.wait_ge(act_ready, i * 2 + (half + 1))
                pe.wait_ge(free[6], i * 2 + (base_use[6] + half))
                for k in range(4):
                    ins = pe.transpose(bank[6][:, k * P:(k + 1) * P], act_h[half][:, k * P:(k + 1) * P], ident)
                ins.then_inc(full[6], 1)

            def chunk_products(i, c, xh, xl, k0, b, last):
                pe.wait_ge(wl_ready, i * NCH + (c + 1))
                h, l = (w[c % NSP].rearrange("p (k n) -> p k n", k=2) for w in (wh, wl))
                for k in range(2):
                    for x, w in ((xh, h), (xh, l), (xl, h)):
                        for q in range(2):
                            ins = pe.matmul(bank[b + q], x[:, k0 + k, :], w[:, k, q * 512:(q + 1) * 512],
                                            start=False, stop=(last and k == 1 and x is xl))
                ins.then_inc(e_used, 1)

            def expert_block(i):
                pe.wait_ge(ohe_ready, i + 1)
                for half in range(2):
                    pe.wait_ge(free[2 * half], i + base_use[2 * half])
                    for q in range(2):
                        c = half * D + q * 512
                        pe.matmul(bank[2 * half + q], ohe[:, :], bparts[:, c:c + 512], start=True, stop=False)
                    if half == 0:
                        pe.wait_ge(free[7], i * 2 + (base_use[7] + 2))
                    for c in range(4):
                        chunk_products(i, 4 * half + c, xgh, xgl, 2 * c, 2 * half, c == 3)
                turn_hidden(i, 0)
                turn_rows(i + 1, 0)
                pe.wait_ge(free[4], i + base_use[4])
                for q in range(2):
                    pe.matmul(bank[4 + q], ohe[:, :], bparts[:, 2 * D + q * 512:2 * D + (q + 1) * 512], start=True, stop=False)
                for half in range(2):
                    if half == 1:
                        turn_hidden(i, 1)
                        turn_rows(i + 1, 1)
                    pe.wait_ge(free[6], i * 2 + (base_use[6] + half + 1))
                    for c in range(2):
                        chunk_products(i, 8 + 2 * half + c, hTh, hTl, 4 * half + 2 * c, 4, half == 1 and c == 1)

            turn_rows(0, 0)
            turn_rows(0, 1)
            all_blocks(pe, expert_block)

        @block.scalar
        def _(act):
            act.dma_start(con[:, :], a["consts"][:, 0:C_LEN]).then_inc(const_in, 16)
            act.wait_ge(mask_row, 3)
            act.dma_start(rest[:, 0:2 * D], zeros).then_inc(y_out, 16)
            for t in range(NT):
                act.wait_ge(x_in[t], 16)
                act.activation(area(16 + 4 * t, 4), xbuf[:, t, :], ACT.Square, accum_out=stat[:, t:t + 1]).then_inc(x_sq, 1)
            act.wait_ge(gain_in, 16 * 3)
            for k in range(KD):
                act.activation(xnT[:, k, :], filled(act, ("xT", k)), ACT.Copy, scale=gcols[:, k:k + 1]).then_inc(free_of(("xT", k)), 1)
            for k in range(KD):
                taken(act, ("xT", k))
                act.activation(xe_h[:, k, :], xnT[:, k, :], ACT.Copy).then_inc(xeh_ready, 1)
            def early_lead(p):
                act.wait_ge(wring_in[CH.index(EARLY[p // KD]) % NW], chunk_count(EARLY[p // KD]))
                if p >= ERING:
                    early_done(act, p - ERING)
                raw_k = chunk_view(EARLY[p // KD])[:, p % KD, :]
                act.activation(early_h(p), raw_k, ACT.Copy).then_inc(early_h_ready, 1)

            def early_out(name):
                for i in range(NT):
                    key = early_key(name, i)
                    o = filled(act, key)
                    if name[:2] == "iq":
                        act.activation(iqT[:, key[1], :], o, ACT.Copy).then_inc(free_of(key), 1)
                    elif name[:2] == "dv":
                        act.activation(dv[:, i, key[1] * 512:(key[1] + 1) * 512], o, ACT.Copy).then_inc(free_of(key), 1)
                    else:
                        act.activation((dqT if name[:2] == "dq" else dkT)[:, key[1], :], o, ACT.Copy,
                                       scale=64 ** -0.5 if name[:2] == "dq" else 1.0).then_inc(free_of(key), 1)

            for p in range(ERING):
                early_lead(p)
            for key in G_CKV:
                act.activation(cbuf[:, key[1], :], filled(act, key)[:, 0:LAT], ACT.Copy).then_inc(free_of(key), 1)
            act.wait_ge(lam_dot, 2)
            act.activation(lam[:, 0:2], lam[:, 0:2], ACT.Exp).then_inc(lam_exp, 1)
            for t in range(NT):
                taken(act, G_CKV[t])
                act.activation(area(48 + t, 1), cbuf[:, t, :], ACT.Square, accum_out=stat[:, 8 + t:9 + t]).then_inc(c_sq, 1)
            act.wait_ge(zero_out, 16)
            for p in range(ERING, NQP):
                if p == KD + ERING:
                    early_out("iq0")
                early_lead(p)
            early_out("iq1")
            act.activation(ikT, filled(act, G_IK[0]), ACT.Copy).then_inc(free_of(G_IK[0]), 1)
            for key in G_IW:
                act.activation(iw[:, key[1], :], filled(act, key)[:, 0:NI], ACT.Copy, scale=(NI * DI) ** -0.5).then_inc(free_of(key), 1)
            for k in range(KL):
                act.activation(cT[:, k, :], filled(act, ("cT", k)), ACT.Copy, scale=gcols[:, KD + k:KD + k + 1]).then_inc(free_of(("cT", k)), 1)
            act.wait_ge(bparts_ready, 1)
            act.wait_ge(rvec_out, 16)
            for p in range(NQP, NQP + AHEAD):
                early_lead(p)
            for m, (t, h) in enumerate(INDEX):
                key = ("ix", t, h)
                n = (t + 1) * P
                if m % 3 < 2:
                    p = NQP + 2 * (m // 3) + m % 3
                    if p > NQP and p % KD == 0:
                        early_out(EARLY[p // KD - 1])
                    early_lead(p + AHEAD)
                if m >= 2:
                    act.wait_ge(relu_used, m - 1)
                act.activation(PT[m % 2][:, 0:n], filled(act, key)[:, 0:n], ACT.Relu).then_inc(free_of(key), 1)
            for p in range(NXP, NEP):
                if p % KD == 0:
                    if EARLY[p // KD - 1] == "dv0":
                        act.wait_ge(y_zero, 16 * (NX // 2))
                        act.wait_ge(y_out, 16)
                        act.wait_ge(relu_used, len(INDEX))
                    early_out(EARLY[p // KD - 1])
                if p + AHEAD < NEP:
                    early_lead(p + AHEAD)
            early_out("dv1")
            for key in G_UK:
                act.activation(khT[:, key[1], :], filled(act, key), ACT.Copy).then_inc(free_of(key), 1)
            for key in G_UV:
                act.activation(vh[:, key[2], key[1] * 512:(key[1] + 1) * 512], filled(act, key), ACT.Copy).then_inc(free_of(key), 1)

            act.wait_ge(bparts_ready, 1)
            for u in range(NU + 6):
                if sq_part(u - 1) and sq_part(u - 1)[1] == NT - 1:
                    key = ("sq", sq_part(u - 1)[0])
                    act.activation(sqT[:, key[1], :], filled(act, key), ACT.Copy, scale=P ** -0.5).then_inc(free_of(key), 1)
                if u < NU:
                    n = (UNITS[u][1] + 1) * P
                    act.wait_ge(score_ready, u + 1)
                    for c in range(2):
                        row = srow[u % 3][c][:, 0:n]
                        act.activation(row, row, ACT.Exp, bias=row_max[u % 2][:, 2 + c:3 + c],
                                       accum_out=row_sum[u % 3][:, c:c + 1]).then_inc(exp_ready, 1)
                if 0 <= u - 2 < NU:
                    v = u - 2
                    n = (UNITS[v][1] + 1) * P
                    if v >= 2:
                        filled(act, ("o", v - 2))
                    act.activation(PT[v % 2][:, 0:n], filled(act, ("pt", v))[:, 0:n], ACT.Copy).then_inc(free_of(("pt", v)), 1)
                if 0 <= u - 5 < NU and UNITS[u - 5][1] == NT - 1:
                    h = UNITS[u - 5][0]
                    act.activation(ydT[:, h, :], filled(act, ("yt", h)), ACT.Copy, scale=lam[:, 3:4]).then_inc(free_of(("yt", h)), 1)

            for u in range(NU + 3):
                if u < NU:
                    n = (UNITS[u][1] + 1) * P
                    act.wait_ge(sscore_ready, u + 1)
                    row = srow[u % 3][0][:, 0:n]
                    act.activation(row, row, ACT.Exp, bias=row_max[u % 2][:, 2:3],
                                   accum_out=row_sum[u % 3][:, 0:1]).then_inc(sexp_ready, 1)
                if 0 <= u - 2 < NU:
                    v = u - 2
                    n = (UNITS[v][1] + 1) * P
                    if v >= 3:
                        filled(act, ("so", v - 3))
                    act.activation(sparse_PT[v % 3][:, 0:n], filled(act, ("spt", v))[:, 0:n], ACT.Copy).then_inc(free_of(("spt", v)), 1)

            filled(act, ("so", NU - 1))
            filled(act, ("so", NU - 2))
            for v in (NU - 2, NU - 1):
                taken(act, ("so", v))
            taken(act, ("yt", NH - 1))
            for m, name in enumerate(LATE):
                for q in range(PIECES):
                    p = PIECES * m + q
                    if q == 0:
                        act.wait_ge(late_in[m % 2], 16 * (m // 2 + 1))
                    if m:
                        piece_done(act, m - 1, q)
                    act.activation(piece_h[q], tiles(late_ring[m % 2], KD)[:, PK * q:PK * q + PK, :], ACT.Copy).then_inc(piece_h_ready, 1)
                    if name in SPLIT_AT:
                        x, xh = {"ga0": (xnT, xn_h), "bd0": (ydT, yd_h), "bs0": (ysT, ys_h)}[name]
                        n0 = KD * SPLIT_AT.index(name)
                        for k in range(PK * q, PK * q + PK):
                            if n0 + k >= 2:
                                act.wait_ge(lead_ready, n0 + k - 1)
                            act.activation(lead_tmp[k % 2], x[:, k, :], ACT.Copy).then_inc(lead_tmp_ready, 1)
                        for k in range(PK * q, PK * q + PK):
                            act.wait_ge(rest_ready, n0 + k + 1)
                            act.activation(xh[:, k, :], lead_tmp[k % 2].bitcast(F32), ACT.Copy).then_inc(lead_ready, 1)
                prev = LATE[m - 1] if m else ""
                if prev[:1] == "g":
                    g, j = "ab".index(prev[1]), int(prev[2])
                    for i in range(NT):
                        if j and g == 0:
                            taken(act, ("bd", 0, i))
                        elif j:
                            act.wait_ge(ml_ready, i + 1)
                        key = (prev[:2], j, i)
                        act.activation(sgate[:, NT * g + i, :], filled(act, key), ACT.Sigmoid).then_inc(free_of(key), 1)
                if prev[:2] == "bs":
                    for i in range(NT):
                        n = NT * int(prev[2]) + i
                        act.wait_ge(merge_ready, n + 1)
                        act.activation(m_h[:, n, :], sgate[:, NT + i, :], ACT.Copy).then_inc(mh_ready, 1)

            def square_h(t):
                taken(act, ("wo", 0, t))
                taken(act, ("wo", 1, t))
                if t:
                    act.wait_ge(h_sq, t)
                act.activation(ptb[:, :], hbuf[:, t, :], ACT.Square, accum_out=stat[:, 16 + t:17 + t]).then_inc(h_sq, 1)

            act.wait_ge(merge_ready, KD)
            square_h(0)
            for t in range(NT):
                if t + 1 < NT:
                    square_h(t + 1)
                for g in range(2):
                    if t >= 2:
                        filled(act, ("lg", t - 2))
                    act.activation(hnT[:, t % 2, g * 512:(g + 1) * 512], filled(act, ("hT", t, g)), ACT.Copy).then_inc(free_of(("hT", t, g)), 1)
            for t in range(NT):
                act.wait_ge(top_ready, t + 1)
                act.activation(gate[:, t, :], top_v[:, t, 0:NK], ACT.Exp, bias=vneg[:, t:t + 1],
                               accum_out=gsum[:, t:t + 1]).then_inc(gate_exp, 1)

            def lead(i, c):
                act.wait_ge(raw_in[c % NRAW], i * (16 * NCH // NRAW) + 16 * (c // NRAW + 1))
                ge(act, e_used, i * NCH + (c + 1 - NSP))
                act.activation(wh[c % NSP], raw[c % NRAW], ACT.Copy).then_inc(wh_ready, 1)

            def lead_rows(i, g):
                act.wait_ge(full[7], i * 2 + (base_use[7] + g + 1))
                act.activation(xgh[:, 4 * g:4 * g + 4, :], bank[7].rearrange("p (k n) -> p k n", k=4), ACT.Copy).then_inc(xgh_ready, 1)

            def lead_hidden(i, half):
                act.wait_ge(full[6], i * 2 + (base_use[6] + half + 1))
                act.activation(hTh[:, 4 * half:4 * half + 4, :], bank[6].rearrange("p (k n) -> p k n", k=4), ACT.Copy).then_inc(hTh_ready, 1)

            def sigmoid(i, half):
                act.wait_ge(g_ready, i * 2 + (half + 1))
                act.activation(sg_h[half], gate_h[half], ACT.Sigmoid, scale=ALPHA).then_inc(sg_ready, 1)

            def store_rows(i):
                act.wait_ge(e_used, i * NCH + NCH)
                act.wait_ge(y_out, i * 16 + 16)
                act.activation(ybuf, psum[:, 4 * 512:6 * 512], ACT.Copy).then_inc(free[4], 1)
                act.wait_ge(free[4], i + (base_use[4] + 1))
                act.dma_start(y_d[bass.ds(i * P, P), :], ybuf).then_inc(y_out, 16)

            def expert_block(i):
                for c in range(4):
                    lead(i, c)
                if not isinstance(i, int):
                    store_rows(i - 1)
                for c in range(4, 8):
                    lead(i, c)
                sigmoid(i, 0)
                for c in range(8, 11):
                    lead(i, c)
                lead_hidden(i, 0)
                sigmoid(i, 1)
                lead(i, 11)
                lead_rows(i + 1, 0)
                lead_hidden(i, 1)
                lead_rows(i + 1, 1)

            lead_rows(0, 0)
            lead_rows(0, 1)
            n_extra = all_blocks(act, expert_block)
            store_rows(n_extra + (NE - 1))

            for t in range(NT):
                act.wait_ge(yg_used, NK * (t + 1))
                if t:
                    act.wait_ge(o_sq, t)
                act.activation(ptb[:, :], hbuf[:, t, :], ACT.Square, accum_out=stat[:, 24 + t:25 + t]).then_inc(o_sq, 1)

        @block.vector
        def _(dve):
            n_step = [0]

            def step(ins):
                n_step[0] += 1
                ins.then_inc(dve_step, 1)
                dve.wait_ge(dve_step, n_step[0])

            def inv_rms(src, n, width):
                m, y, t = s_ms[:, 0:n], s_rs[:, 0:n], s_nt[:, 0:n]
                step(dve.tensor_scalar(m, src, 1.0 / width, EPS, ALU.mult, ALU.add))
                step(dve.tensor_scalar(y.bitcast(I32), m.bitcast(I32), -0.5, float(0x5F3759DF), ALU.mult, ALU.add))
                for _ in range(3):
                    step(dve.tensor_tensor(t, y, y, ALU.mult))
                    step(dve.tensor_tensor(t, t, m, ALU.mult))
                    step(dve.tensor_scalar(t, t, -0.5, 1.5, ALU.mult, ALU.add))
                    step(dve.tensor_tensor(y, y, t, ALU.mult))

            s_ms, s_rs, s_nt, s_sq = (stat[:, 32 + 4 * i:36 + 4 * i] for i in range(4))
            dve.memset(tabx[NB:NB + 1, :], MASK).then_inc(mask_row, 1)
            dve.memset(carrier[:, :], 0.0).then_inc(mask_row, 1)
            dve.memset(zeros, 0.0).then_inc(mask_row, 1)
            dve.wait_ge(x_sq, NT)
            inv_rms(stat[:, 0:NT], NT, D)
            for t in range(NT):
                dve.tensor_scalar(xbuf[:, t, :], xbuf[:, t, :], s_rs[:, t:t + 1], None, ALU.mult).then_inc(x_norm, 1)
            dve.wait_ge(x_norm, NT)
            for k in range(KD):
                dve.wait_ge(xeh_ready, k + 1)
                dve.tensor_tensor(xe_l[:, k, :], xnT[:, k, :], xe_h[:, k, :].bitcast(F32), ALU.subtract).then_inc(xel_ready, 1)

            def early_rest(p):
                dve.wait_ge(early_h_ready, p + 1)
                dve.tensor_tensor(early_l(p), chunk_view(EARLY[p // KD])[:, p % KD, :],
                                  early_h(p).bitcast(F32), ALU.subtract).then_inc(early_l_ready, 1)

            for p in range(ERING):
                early_rest(p)
            dve.wait_ge(small_in, 16 * 6)
            for i in range(2):
                dve.tensor_tensor_reduce(lamj[:, :], lamv[:, 2 * i * DI:(2 * i + 1) * DI], lamv[:, (2 * i + 1) * DI:(2 * i + 2) * DI],
                                         1.0, 0.0, ALU.mult, ALU.add, lam[:, i:i + 1]).then_inc(lam_dot, 1)
                dve.wait_ge(lam_dot, i + 1)
            dve.wait_ge(const_in, 16)
            dve.tensor_copy(identb[:, :], ident).then_inc(identb_ready, 1)
            dve.tensor_copy(rvec[:, 0:512], filled(dve, "rv0")[0:2 * NH, :]).then_inc(free_of("rv0"), 1)
            dve.tensor_copy(rvec[:, 512:RLEN], filled(dve, "rv1")[0:2 * NH, 0:RLEN - 512]).then_inc(free_of("rv1"), 1)
            dve.wait_ge(gain_in, 16 * 3)
            dve.wait_ge(lam_exp, 1)
            step(dve.tensor_tensor(lam[:, 2:3], lam[:, 1:2], lam[:, 0:1], ALU.subtract))
            step(dve.tensor_scalar(lam[:, 2:3], lam[:, 2:3], -LAM_INIT, None, ALU.add))
            step(dve.tensor_scalar(lam[:, 3:4], gcols[:, KD + KL:KD + KL + 1], OUT_SCALE, None, ALU.mult))
            dve.wait_ge(c_sq, NT)
            inv_rms(stat[:, 8:8 + NT], NT, LAT)
            for t in range(NT):
                dve.tensor_scalar(cbuf[:, t, :], cbuf[:, t, :], s_rs[:, t:t + 1], None, ALU.mult).then_inc(c_norm, 1)
            dve.wait_ge(c_norm, NT)
            for p in range(ERING, NQP):
                early_rest(p)

            for k in range(KL):
                filled(dve, ("cT", k))
            taken(dve, G_IW[-1])
            taken(dve, G_IW[-2])
            dve.wait_ge(bparts_ready, 1)
            dve.wait_ge(rvec_out, 16)
            for p in range(NQP, NQP + AHEAD):
                early_rest(p)
            for m, (t, h) in enumerate(INDEX):
                n = (t + 1) * P
                if m % 3 < 2:
                    early_rest(NQP + 2 * (m // 3) + m % 3 + AHEAD)
                taken(dve, ("ix", t, h))
                if m:
                    dve.wait_ge(relu_used, m)
                r, w = PT[m % 2][:, 0:n], iw[:, t, h:h + 1]
                if h == 0:
                    ins = dve.tensor_scalar(topacc[t], r, w, None, ALU.mult)
                else:
                    ins = dve.scalar_tensor_tensor(out=topacc[t], in0=r, scalar=w, in1=topacc[t], op0=ALU.mult, op1=ALU.add)
                ins.then_inc(relu_used, 1)
            dve.wait_ge(relu_used, len(INDEX))
            p = NXP + AHEAD
            for t in range(1, NT):
                diag = topacc[t][:, t * P:(t + 1) * P]
                step(dve.tensor_tensor(diag, diag, con[:, C_CAUS:C_CAUS + P], ALU.add))
                for n in range(TOPK // 8):
                    if n % 3 == 0 and p < NEP:
                        early_rest(p)
                        p += 1
                    step(dve.max(v8[:, :], topacc[t]))
                    step(dve.match_replace(topacc[t], v8[:, :], topacc[t], TAKEN))
                dve.tensor_scalar(topmask[t][:, :], topacc[t], TAKEN * 0.9, MASK, ALU.is_gt, ALU.mult).then_inc(mask_ready, 1)

            while p < NEP:
                early_rest(p)
                p += 1

            dve.wait_ge(mask_ready, NT - 1)
            dve.wait_ge(strip_in, 16)
            for u in range(NU + 6):
                if u < NU:
                    h, t = UNITS[u]
                    n = (t + 1) * P
                    if u >= 3:
                        filled(dve, ("pt", u - 3))
                    for c in range(2):
                        dve.tensor_tensor_reduce(srow[u % 3][c][:, 0:n], filled(dve, ("s", u, c))[:, 0:n], strips[:, h, S - n:S], 1.0, 3 * MASK,
                                                 ALU.add, ALU.max, row_max[u % 2][:, c:c + 1]).then_inc(free_of(("s", u, c)), 1)
                    for c in range(2):
                        taken(dve, ("s", u, c))
                    dve.tensor_scalar(row_max[u % 2][:, 2:4], row_max[u % 2][:, 0:2], -1.0, None, ALU.mult).then_inc(score_ready, 1)
                if 1 <= u <= NU:
                    v = u - 1
                    n = (UNITS[v][1] + 1) * P
                    r, q = row_sum[v % 3], ratio[v % 4]
                    dve.wait_ge(exp_ready, 2 * v + 2)
                    step(dve.reciprocal(q[:, 0:2], r[:, :]))
                    step(dve.tensor_scalar(q[:, 2:3], q[:, 1:2], r[:, 0:1], lam[:, 2:3], ALU.mult, ALU.mult))
                    dve.scalar_tensor_tensor(out=srow[v % 3][0][:, 0:n], in0=srow[v % 3][1][:, 0:n], scalar=q[:, 2:3],
                                             in1=srow[v % 3][0][:, 0:n], op0=ALU.mult, op1=ALU.add).then_inc(a_ready, 1)
                if 0 <= u - 4 < NU:
                    v = u - 4
                    h, t = UNITS[v]
                    if t == 0 and h >= 2:
                        filled(dve, ("yt", h - 2))
                    row = orow[h % 2][:, t * P:(t + 1) * P]
                    dve.tensor_scalar(row, filled(dve, ("o", v))[:, 0:P], ratio[v % 4][:, 0:1], None, ALU.mult).then_inc(free_of(("o", v)), 1)
                    taken(dve, ("o", v))
                    step(dve.tensor_tensor_reduce(ojunk[:, :], row, row, 1.0, 0.0, ALU.mult, ALU.add, s_sq[:, t:t + 1]))
                    if t == NT - 1:
                        inv_rms(s_sq, NT, 2 * 64)
                        for q in range(NT):
                            row = orow[h % 2][:, q * P:(q + 1) * P]
                            dve.tensor_scalar(row, row, s_rs[:, q:q + 1], None, ALU.mult).then_inc(y_ready, 1)

            dve.wait_ge(strip2_in, 16)
            for u in range(NU + 5):
                if u < NU:
                    h, t = UNITS[u]
                    n = (t + 1) * P
                    if u >= 3:
                        filled(dve, ("spt", u - 3))
                    dve.tensor_tensor_reduce(srow[u % 3][0][:, 0:n], filled(dve, ("ss", u))[:, 0:n], strips[:, h, S - n:S], 1.0, 3 * MASK,
                                             ALU.add, ALU.max, row_max[u % 2][:, 0:1]).then_inc(free_of(("ss", u)), 1)
                    taken(dve, ("ss", u))
                    dve.tensor_scalar(row_max[u % 2][:, 2:3], row_max[u % 2][:, 0:1], -1.0, None, ALU.mult).then_inc(sscore_ready, 1)
                if 1 <= u <= NU:
                    v = u - 1
                    n = (UNITS[v][1] + 1) * P
                    dve.wait_ge(sexp_ready, v + 1)
                    step(dve.reciprocal(ratio[v % 4][:, 0:1], row_sum[v % 3][:, 0:1]))
                    row = srow[v % 3][0][:, 0:n]
                    dve.tensor_scalar(row, row, ratio[v % 4][:, 0:1], None, ALU.mult).then_inc(p_ready, 1)
                if 0 <= u - 5 < NU:
                    v = u - 5
                    h, t = UNITS[v]
                    dve.tensor_copy(ysT[:, h, t * P:(t + 1) * P], filled(dve, ("so", v))[:, 0:P]).then_inc(free_of(("so", v)), 1)

            def rest_merged(j):
                for i in range(NT):
                    n = NT * j + i
                    dve.wait_ge(mh_ready, n + 1)
                    dve.tensor_tensor(m_l[:, n, :], sgate[:, NT + i, :], m_h[:, n, :].bitcast(F32), ALU.subtract).then_inc(ml_ready, 1)

            for m, name in enumerate(LATE):
                for q in range(PIECES):
                    dve.wait_ge(piece_h_ready, PIECES * m + q + 1)
                    dve.tensor_tensor(piece_l[q], tiles(late_ring[m % 2], KD)[:, PK * q:PK * q + PK, :], piece_h[q].bitcast(F32),
                                      ALU.subtract).then_inc(piece_l_ready, 1)
                    if name in SPLIT_AT:
                        x, xl = {"ga0": (xnT, xn_l), "bd0": (ydT, yd_l), "bs0": (ysT, ys_l)}[name]
                        for k in range(PK * q, PK * q + PK):
                            dve.wait_ge(lead_tmp_ready, KD * SPLIT_AT.index(name) + k + 1)
                            dve.tensor_tensor(xl[:, k, :], x[:, k, :], lead_tmp[k % 2].bitcast(F32), ALU.subtract).then_inc(rest_ready, 1)
                prev = LATE[m - 1] if m else ""
                if prev[:2] == "bd":
                    j = int(prev[2])
                    for i in range(NT):
                        taken(dve, ("ga", j, i))
                        dve.tensor_tensor(mergedT[:, NT * j + i, :], filled(dve, ("bd", j, i)), sgate[:, i, :], ALU.mult).then_inc(free_of(("bd", j, i)), 1)
                    if j == 1:
                        rest_merged(0)
                if prev[:2] == "bs":
                    j = int(prev[2])
                    for i in range(NT):
                        taken(dve, ("gb", j, i))
                        if NT * j + i >= 2:
                            dve.wait_ge(merge_ready, NT * j + i - 1)
                        dve.tensor_tensor(merge_tmp[i % 2], filled(dve, ("bs", j, i)), sgate[:, NT + i, :], ALU.mult).then_inc(free_of(("bs", j, i)), 1)
                        taken(dve, ("bs", j, i))
                        taken(dve, ("bd", j, i))
                        dve.tensor_tensor(sgate[:, NT + i, :], mergedT[:, NT * j + i, :], merge_tmp[i % 2], ALU.add).then_inc(merge_ready, 1)
                    if j == 1:
                        rest_merged(1)
            dve.wait_ge(x_in2, 16)
            for j in range(2):
                for t in range(NT):
                    hcol = hbuf[:, t, j * 512:(j + 1) * 512]
                    dve.tensor_tensor(hcol, filled(dve, ("wo", j, t)), hcol, ALU.add).then_inc(free_of(("wo", j, t)), 1)

            dve.wait_ge(gbc_in, 16)
            dve.wait_ge(wr_in, 48)

            def norm_h(t):
                dve.wait_ge(h_sq, t + 1)
                inv_rms(stat[:, 16 + t:17 + t], 1, D)
                if t >= 2:
                    filled(dve, ("hT", t - 2, 1))
                    dve.wait_ge(hn_out[t % 2], 16 * (t // 2))
                dve.scalar_tensor_tensor(out=hn[:, t % 2, :], in0=hbuf[:, t, :], scalar=s_rs[:, 0:1], in1=gffn, op0=ALU.mult, op1=ALU.mult).then_inc(hn_ready, 1)
                dve.wait_ge(hn_ready, t + 1)

            def route(t):
                dve.tensor_tensor(logit[:, t, :], filled(dve, ("lg", t))[:, 0:NE], brt[:, :], ALU.add).then_inc(free_of(("lg", t)), 1)
                taken(dve, ("lg", t))
                step(dve.max(top_v[:, t, :], logit[:, t, :]))
                step(dve.max_index(top_i[:, t, :], top_v[:, t, :], logit[:, t, :]))
                dve.tensor_scalar(vneg[:, t:t + 1], top_v[:, t, 0:1], -1.0, None, ALU.mult).then_inc(top_ready, 1)
                step(dve.tensor_copy(top_f[:, t, :], top_i[:, t, :]))
                for k in range(NK):
                    step(dve.tensor_scalar(pick[:, t, k, :], rcon[:, C_E:C_E + NE], top_f[:, t, k:k + 1], None, ALU.is_equal))
                dve.tensor_reduce(chosen[:, t, :], pick[:, t].rearrange("p k e -> p e k"), X, ALU.add).then_inc(chosen_ready, 1)

            norm_h(0)
            norm_h(1)
            for t in range(NT):
                route(t)
                if t + 2 < NT:
                    norm_h(t + 2)

            cnt = filled(dve, "cntT")[0:NE, 0:P]
            step(dve.tensor_scalar(extra[:, :], cnt, P + 0.5, None, ALU.is_gt))
            step(dve.scalar_tensor_tensor(out=extra2[:, :], in0=cnt, scalar=2 * P + 0.5, in1=extra[:, :], op0=ALU.is_gt, op1=ALU.add))
            dve.scalar_tensor_tensor(out=extra[:, :], in0=cnt, scalar=3 * P + 0.5, in1=extra2[:, :], op0=ALU.is_gt, op1=ALU.add).then_inc(free_of("cntT"), 1)
            dve.scalar_tensor_tensor(out=xbase[:, :], in0=filled(dve, "xb")[:, 0:NE], scalar=float(P), in1=rcon[:, C_XB:C_XB + NE],
                                     op0=ALU.mult, op1=ALU.add).then_inc(free_of("xb"), 1)
            dve.tensor_tensor(before[:, :], filled(dve, "xeT")[0:NE, 0:16], rcon[0:NE, C_J:C_J + 16], ALU.is_le).then_inc(free_of("xeT"), 1)
            step(dve.tensor_copy(evals[:, 0:NE], rcon[:, C_E:C_E + NE]))
            o = filled(dve, "xe")
            dve.tensor_copy(nextra_i[:, 0:1], o[:, 16:17]).then_inc(evals_ready, 1)
            dve.tensor_scalar(evals[:, NE:NE + 16], o[:, 0:16], float(NE - 1), None, ALU.min).then_inc(free_of("xe"), 1)
            taken(dve, "xe")
            dve.tensor_copy(evals_i[:, :], evals[:, :]).then_inc(evals_ready, 1)
            taken(dve, "xb")
            for t in range(NT):
                o = filled(dve, ("rank", t))[:, 0:NE]
                step(dve.scalar_tensor_tensor(out=over[:, :], in0=o, scalar=P - 0.5, in1=xbase[:, :], op0=ALU.is_gt, op1=ALU.mult))
                dve.tensor_tensor(slot_e[:, :], o, rcon[:, C_EB:C_EB + NE], ALU.add).then_inc(free_of(("rank", t)), 1)
                taken(dve, ("rank", t))
                step(dve.tensor_tensor(slot_e[:, :], slot_e[:, :], over[:, :], ALU.add))
                step(dve.tensor_tensor(ptmp, pick[:, t], slot_e[:, :].unsqueeze(1).broadcast_to([P, NK, NE]), ALU.mult))
                step(dve.tensor_reduce(slot_f[:, t, :], ptmp, X, ALU.add))
                dve.tensor_copy(slot_i[:, t, :], slot_f[:, t, :]).then_inc(slots_ready, 1)
            for t in range(NT):
                dve.wait_ge(gate_exp, t + 1)
                step(dve.reciprocal(gsum[:, t:t + 1], gsum[:, t:t + 1]))
                step(dve.tensor_scalar(gate[:, t, :], gate[:, t, :], gsum[:, t:t + 1], None, ALU.mult))

            def pick_bias(i):
                dve.tensor_scalar(ohe[:, :], con[0:96, C_P32:C_P32 + 1].broadcast_to([96, P]), evals[0:96, bass.ds(i, 1)], None, ALU.is_equal).then_inc(ohe_ready, 1)

            def rest_of(i, c):
                dve.wait_ge(wh_ready, i * NCH + (c + 1))
                dve.tensor_tensor(wl[c % NSP], raw[c % NRAW], wh[c % NSP].bitcast(F32), ALU.subtract).then_inc(wl_ready, 1)

            def rest_rows(i, g):
                dve.wait_ge(xgh_ready, i * 2 + (g + 1))
                dve.tensor_tensor(xgl[:, 4 * g:4 * g + 4, :], bank[7].rearrange("p (k n) -> p k n", k=4),
                                  xgh[:, 4 * g:4 * g + 4, :].bitcast(F32), ALU.subtract).then_inc(free[7], 1)

            def rest_hidden(i, half):
                dve.wait_ge(hTh_ready, i * 2 + (half + 1))
                dve.tensor_tensor(hTl[:, 4 * half:4 * half + 4, :], bank[6].rearrange("p (k n) -> p k n", k=4),
                                  hTh[:, 4 * half:4 * half + 4, :].bitcast(F32), ALU.subtract).then_inc(free[6], 1)

            def clamp(i, half):
                dve.wait_ge(e_used, i * NCH + 4 * (half + 1))
                gu = psum[:, 1024 * half:1024 * (half + 1)].rearrange("p (n two) -> p n two", two=2)
                dve.tensor_scalar(gate_h[half], gu[:, :, 0], LIMIT, None, ALU.min).then_inc(g_ready, 1)
                dve.tensor_scalar(up_h[half], gu[:, :, 1], LIMIT, -LIMIT, ALU.min, ALU.max).then_inc(free[2 * half], 1)

            def activate(i, half):
                dve.wait_ge(sg_ready, i * 2 + (half + 1))
                dve.tensor_tensor(sg_h[half], gate_h[half], sg_h[half], ALU.mult).then_inc(glu_ready, 1)
                dve.wait_ge(glu_ready, i * 2 + (half + 1))
                dve.wait_ge(free[2 * half], i + (base_use[2 * half] + 1))
                dve.scalar_tensor_tensor(out=act_h[half], in0=up_h[half], scalar=1.0, in1=sg_h[half],
                                         op0=ALU.add, op1=ALU.mult).then_inc(act_ready, 1)

            def expert_block(i):
                for c in range(7):
                    rest_of(i, c)
                clamp(i, 0)
                rest_of(i, 7)
                activate(i, 0)
                for c in range(8, 11):
                    rest_of(i, c)
                rest_hidden(i, 0)
                clamp(i, 1)
                rest_of(i, 11)
                activate(i, 1)
                rest_rows(i + 1, 0)
                rest_hidden(i, 1)
                rest_rows(i + 1, 1)
                dve.wait_ge(e_used, i * NCH + 9)
                pick_bias(i + 1)

            pick_bias(0)
            rest_rows(0, 0)
            rest_rows(0, 1)
            all_blocks(dve, expert_block)

            for m in range(NT * NK):
                t, k = m // NK, m % NK
                if m:
                    dve.wait_ge(yg_used, m)
                dve.wait_ge(yg_in[m % NYG], 16 * (m // NYG + 1))
                dve.scalar_tensor_tensor(out=hbuf[:, t, :], in0=yg[m % NYG], scalar=gate[:, t, k:k + 1], in1=hbuf[:, t, :],
                                         op0=ALU.mult, op1=ALU.add).then_inc(yg_used, 1)
                if k == NK - 1:
                    if t == 0:
                        dve.wait_ge(gbc_in, 32)
                    dve.wait_ge(o_sq, t + 1)
                    inv_rms(stat[:, 24 + t:25 + t], 1, D)
                    dve.scalar_tensor_tensor(out=outb[t], in0=hbuf[:, t, :], scalar=s_rs[:, 0:1], in1=gfin, op0=ALU.mult, op1=ALU.mult).then_inc(o_ready, 1)
                    dve.wait_ge(o_ready, t + 1)


_INS = ["x", "norm_attn_g", "w_in", "rel_bias", "lam_q1", "lam_k1", "lam_q2", "lam_k2", "diff_subln_g", "kv_norm_g",
        "w_uk", "w_uv", "w_branch_diff", "w_branch_dsa", "w_out", "norm_ffn_g", "w_router", "b_router",
        "w_gate_up", "b_gate_up", "w_down", "b_down", "norm_final_g"]


def kernel(**inputs):
    import concourse.bacc as bacc
    from concourse.bass_utils import run_bass_kernel_spmd

    nc = bacc.Bacc("TRN2", target_bir_lowering=False, num_devices=1)
    arrays, args = {}, {}
    given = {n: np.ascontiguousarray(inputs[n]) for n in _INS}
    given["consts"] = constants()
    given["oh33"] = bucket_onehot()
    for name, v in given.items():
        arrays[f"in_{name}_dram"] = v
        args[name] = nc.dram_tensor(f"in_{name}_dram", v.shape, mybir.dt.from_np(v.dtype), kind="ExternalInput").ap()
    out = nc.dram_tensor("out_dram", (1, S, D), F32, kind="ExternalOutput").ap()
    build(nc, args, out)
    r = run_bass_kernel_spmd(nc, [arrays], core_ids=[0])
    return r.results[0]["out_dram"]
```
